# Optimizing a Trainium2 kernel written in Bass

```python
import jax, jax.numpy as jnp
from jax import lax
import numpy as np
import math

D_MODEL = 1024
BATCH = 1
SEQ = 512
DEPTH = 2

HEAD_DIM = 64
GROUP_HEADS = 4
GROUP_WIDTH = GROUP_HEADS * HEAD_DIM
N_GROUPS = 4
MIX_WIDTH = N_GROUPS * GROUP_WIDTH
BLOCK = 128
NEG_INF = -1e30

FOX_H = GROUP_HEADS
FOX_BIAS_INIT = 3.0
MLA_H = GROUP_HEADS
MLA_Q_RANK = D_MODEL // 4
MLA_KV_RANK = D_MODEL // 8
MLA_NOPE = HEAD_DIM
MLA_ROPE = HEAD_DIM // 2
MLA_V = HEAD_DIM
ROPE_THETA = 10000.0
SB_H = GROUP_HEADS
SWA_H = GROUP_HEADS
SWA_KV_H = 2
WINDOW = 128
D_FF = ((8 * D_MODEL + 767) // 768) * 256
ALPHA = (2.0 * DEPTH) ** 0.25
BETA = (8.0 * DEPTH) ** -0.25

SPLIT_SIZES = (
    FOX_H * HEAD_DIM, FOX_H * HEAD_DIM, FOX_H * HEAD_DIM, FOX_H,
    MLA_Q_RANK, MLA_KV_RANK, MLA_ROPE,
    SB_H * HEAD_DIM, SB_H * HEAD_DIM, SB_H * HEAD_DIM,
    SWA_H * HEAD_DIM, SWA_KV_H * HEAD_DIM, SWA_KV_H * HEAD_DIM,
)
IN_WIDTH = sum(SPLIT_SIZES)


def _layernorm(x, g, b, eps=1e-5):
    xf = x.astype(jnp.float32)
    mu = jnp.mean(xf, axis=-1, keepdims=True)
    var = jnp.mean(jnp.square(xf - mu), axis=-1, keepdims=True)
    return ((xf - mu) * lax.rsqrt(var + eps) * g + b).astype(x.dtype)

def _rmsnorm(x, g, eps=1e-6):
    xf = x.astype(jnp.float32)
    return (xf * lax.rsqrt(jnp.mean(jnp.square(xf), axis=-1, keepdims=True) + eps) * g).astype(x.dtype)

def _group_rmsnorm(mix, g, eps=1e-6):
    B, S, _ = mix.shape
    xf = mix.astype(jnp.float32).reshape(B, S, N_GROUPS, GROUP_WIDTH)
    xf = xf * lax.rsqrt(jnp.mean(jnp.square(xf), axis=-1, keepdims=True) + eps)
    return (xf.reshape(B, S, MIX_WIDTH) * g).astype(mix.dtype)

def _heads(t, n):
    B, S, _ = t.shape
    return t.reshape(B, S, n, -1)

def _rope_tables(S):
    pos = jnp.arange(S, dtype=jnp.float32)
    inv = ROPE_THETA ** (-jnp.arange(0, MLA_ROPE, 2, dtype=jnp.float32) / MLA_ROPE)
    ang = pos[:, None] * inv[None, :]
    return jnp.cos(ang), jnp.sin(ang)

def _rope(x, cos, sin):
    x1, x2 = jnp.split(x.astype(jnp.float32), 2, axis=-1)
    c = cos[None, :, None, :]
    s = sin[None, :, None, :]
    return jnp.concatenate([x1 * c - x2 * s, x1 * s + x2 * c], axis=-1).astype(x.dtype)

def _alibi_slopes(n):
    return jnp.exp2(-8.0 * jnp.arange(1, n + 1, dtype=jnp.float32) / n)

def _causal_softmax_blocks(q, k, v, scale, cum_log_f=None):
    B, S, H, _ = q.shape
    nb = S // BLOCK
    qb = q.reshape(B, nb, BLOCK, H, -1).swapaxes(0, 1)
    kpos = jnp.arange(S)

    def one_block(args):
        i, qi = args
        s = jnp.einsum('bqhd,bkhd->bhqk', qi, k).astype(jnp.float32) * scale
        qpos = i * BLOCK + jnp.arange(BLOCK)
        if cum_log_f is not None:
            cq = lax.dynamic_slice_in_dim(cum_log_f, i * BLOCK, BLOCK, axis=2)
            s = s + cq[..., :, None] - cum_log_f[..., None, :]
        s = jnp.where(kpos[None, :] <= qpos[:, None], s, NEG_INF)
        p = jax.nn.softmax(s, axis=-1).astype(v.dtype)
        return jnp.einsum('bhqk,bkhd->bqhd', p, v)

    out = lax.map(one_block, (jnp.arange(nb), qb))
    return out.swapaxes(0, 1).reshape(B, S, H, -1)

def _stick_breaking_blocks(q, k, v):
    B, S, H, D = q.shape
    nb = S // BLOCK
    scale = D ** -0.5
    qb = q.reshape(B, nb, BLOCK, H, D).swapaxes(0, 1)
    kpos = jnp.arange(S)

    def one_block(args):
        i, qi = args
        z = jnp.einsum('bqhd,bkhd->bhqk', qi, k).astype(jnp.float32) * scale
        qpos = i * BLOCK + jnp.arange(BLOCK)
        strict = kpos[None, :] < qpos[:, None]
        log_1mb = jnp.where(strict, jax.nn.log_sigmoid(-z), 0.0)
        between = lax.cumsum(log_1mb, axis=3, reverse=True) - log_1mb
        a = jnp.where(strict, jnp.exp(jax.nn.log_sigmoid(z) + between), 0.0)
        return jnp.einsum('bhqk,bkhd->bqhd', a.astype(v.dtype), v)

    out = lax.map(one_block, (jnp.arange(nb), qb))
    return out.swapaxes(0, 1).reshape(B, S, H, D)

def _mla(cq, ckv, kr, g_q, g_kv, w_uq, w_ukv, cos, sin):
    B, S, _ = cq.shape
    q = (_rmsnorm(cq, g_q) @ w_uq).reshape(B, S, MLA_H, MLA_NOPE + MLA_ROPE)
    kv = (_rmsnorm(ckv, g_kv) @ w_ukv).reshape(B, S, MLA_H, MLA_NOPE + MLA_V)
    k_nope, v = kv[..., :MLA_NOPE], kv[..., MLA_NOPE:]
    q = jnp.concatenate([q[..., :MLA_NOPE], _rope(q[..., MLA_NOPE:], cos, sin)], axis=-1)
    k_rope = jnp.broadcast_to(_rope(kr[:, :, None, :], cos, sin), (B, S, MLA_H, MLA_ROPE))
    k = jnp.concatenate([k_nope, k_rope.astype(k_nope.dtype)], axis=-1)
    return _causal_softmax_blocks(q.astype(k.dtype), k, v, (MLA_NOPE + MLA_ROPE) ** -0.5)

def _swa_sink_alibi(q, k, v, sinks, slopes):
    B, S, Hq, D = q.shape
    Hkv = k.shape[2]
    G = Hq // Hkv
    nb = S // BLOCK
    qb = q.reshape(B, nb, BLOCK, Hkv, G, D)
    pad = jnp.zeros((B, BLOCK, Hkv, D), k.dtype)
    kp = jnp.concatenate([pad, k], axis=1).reshape(B, nb + 1, BLOCK, Hkv, D)
    vp = jnp.concatenate([pad.astype(v.dtype), v], axis=1).reshape(B, nb + 1, BLOCK, Hkv, D)
    kb = jnp.concatenate([kp[:, :-1], kp[:, 1:]], axis=2)
    vb = jnp.concatenate([vp[:, :-1], vp[:, 1:]], axis=2)
    s = jnp.einsum('bnqhgd,bnkhd->bnhgqk', qb, kb).astype(jnp.float32) * (D ** -0.5)
    dist = jnp.arange(BLOCK)[:, None] + BLOCK - jnp.arange(2 * BLOCK)[None, :]
    band = (dist >= 0) & (dist < WINDOW)
    kpos = (jnp.arange(nb)[:, None] - 1) * BLOCK + jnp.arange(2 * BLOCK)[None, :]
    valid = band[None, :, :] & (kpos >= 0)[:, None, :]
    s = s - slopes.reshape(Hkv, G)[:, :, None, None] * dist.astype(jnp.float32)
    s = jnp.where(valid[None, :, None, None], s, NEG_INF)
    sink = jnp.broadcast_to(sinks.astype(jnp.float32).reshape(Hkv, G)[None, None, :, :, None, None],
                            s.shape[:-1] + (1,))
    p = jax.nn.softmax(jnp.concatenate([s, sink], axis=-1), axis=-1)[..., :-1]
    out = jnp.einsum('bnhgqk,bnkhd->bnqhgd', p.astype(v.dtype), vb)
    return out.reshape(B, S, Hq, D)

def first_inputs(seed: int = 0) -> dict:
    key = jax.random.key(seed)
    ks = jax.random.split(key, 17)
    L = DEPTH

    def nrm(k, shape, scale):
        return jax.random.normal(k, shape, jnp.float32) * scale

    def gain(k, shape):
        return 1.0 + 0.02 * jax.random.normal(k, shape, jnp.float32)

    return {
        'x': nrm(ks[0], (BATCH, SEQ, D_MODEL), 1.0),
        'w_in': nrm(ks[1], (L, D_MODEL, IN_WIDTH), D_MODEL ** -0.5),
        'fox_b_f': FOX_BIAS_INIT + nrm(ks[2], (L, FOX_H), 0.1),
        'mla_g_q': gain(ks[3], (L, MLA_Q_RANK)),
        'mla_g_kv': gain(ks[4], (L, MLA_KV_RANK)),
        'mla_w_uq': nrm(ks[5], (L, MLA_Q_RANK, MLA_H * (MLA_NOPE + MLA_ROPE)), MLA_Q_RANK ** -0.5),
        'mla_w_ukv': nrm(ks[6], (L, MLA_KV_RANK, MLA_H * (MLA_NOPE + MLA_V)), MLA_KV_RANK ** -0.5),
        'swa_sinks': nrm(ks[7], (L, SWA_H), 0.5),
        'mix_g': gain(ks[8], (L, MIX_WIDTH)),
        'w_o': nrm(ks[9], (L, MIX_WIDTH, D_MODEL), BETA * MIX_WIDTH ** -0.5),
        'ln1_g': gain(ks[10], (L, D_MODEL)),
        'ln1_b': nrm(ks[11], (L, D_MODEL), 0.02),
        'w_gate': nrm(ks[12], (L, D_MODEL, D_FF), D_MODEL ** -0.5),
        'w_up': nrm(ks[13], (L, D_MODEL, D_FF), D_MODEL ** -0.5),
        'w_down': nrm(ks[14], (L, D_FF, D_MODEL), BETA * D_FF ** -0.5),
        'ln2_g': gain(ks[15], (L, D_MODEL)),
        'ln2_b': nrm(ks[16], (L, D_MODEL), 0.02),
    }

def first_block(x, w_in, fox_b_f, mla_g_q, mla_g_kv, mla_w_uq, mla_w_ukv, swa_sinks, mix_g, w_o,
              ln1_g, ln1_b, w_gate, w_up, w_down, ln2_g, ln2_b):
    B, S, _ = x.shape
    cos, sin = _rope_tables(S)
    slopes = _alibi_slopes(SWA_H)
    points = [int(p) for p in np.cumsum(SPLIT_SIZES)[:-1]]
    for l in range(DEPTH):
        h = x @ w_in[l]
        (fq, fk, fv, fgate, cq, ckv, kr, sq, sk, sv, wq, wk, wv) = jnp.split(h, points, axis=-1)
        log_f = jax.nn.log_sigmoid(fgate.astype(jnp.float32) + fox_b_f[l].astype(jnp.float32))
        cum = jnp.cumsum(log_f, axis=1).transpose(0, 2, 1)
        out_a = _causal_softmax_blocks(_heads(fq, FOX_H), _heads(fk, FOX_H), _heads(fv, FOX_H),
                                       HEAD_DIM ** -0.5, cum)
        out_b = _mla(cq, ckv, kr, mla_g_q[l], mla_g_kv[l], mla_w_uq[l], mla_w_ukv[l], cos, sin)
        out_c = _stick_breaking_blocks(_heads(sq, SB_H), _heads(sk, SB_H), _heads(sv, SB_H))
        out_d = _swa_sink_alibi(_heads(wq, SWA_H), _heads(wk, SWA_KV_H), _heads(wv, SWA_KV_H),
                                swa_sinks[l], slopes)
        mix = jnp.concatenate([out_a.reshape(B, S, GROUP_WIDTH), out_b.reshape(B, S, GROUP_WIDTH),
                               out_c.reshape(B, S, GROUP_WIDTH), out_d.reshape(B, S, GROUP_WIDTH)],
                              axis=-1).astype(x.dtype)
        y = _group_rmsnorm(mix, mix_g[l]) @ w_o[l]
        x = _layernorm(ALPHA * x + y, ln1_g[l], ln1_b[l])
        f = (jax.nn.silu(x @ w_gate[l]) * (x @ w_up[l])) @ w_down[l]
        x = _layernorm(ALPHA * x + f, ln2_g[l], ln2_b[l])
    return x


MIX_WIDTH_2 = D_MODEL
DA_WIDTH = MIX_WIDTH_2 // 2
SC_WIDTH = MIX_WIDTH_2 // 4
LRU_WIDTH = MIX_WIDTH_2 - DA_WIDTH - SC_WIDTH

DA_HEAD_DIM = 64
DA_HEADS = DA_WIDTH // (2 * DA_HEAD_DIM)
Q_BLOCK = 128
NUM_BUCKETS = 32
MAX_DISTANCE = 128
SUBLN_EPS = 1e-5

SC_KERNEL = 3

LRU_BLOCKS = 4
LRU_BLOCK = LRU_WIDTH // LRU_BLOCKS
LRU_CONV = 4
LRU_C = 8.0

D_FF_2 = 2816
RMS_EPS = 1e-6
NEG_INF_2 = -1e30

IN_SPLIT_WIDTHS = (DA_WIDTH, DA_WIDTH, DA_WIDTH,
                   SC_WIDTH, SC_WIDTH, SC_WIDTH,
                   LRU_WIDTH, LRU_WIDTH)
IN_WIDTH_2 = sum(IN_SPLIT_WIDTHS)
IN_SPLIT_POINTS = tuple(int(v) for v in np.cumsum(IN_SPLIT_WIDTHS)[:-1])


def rms_norm(x, g, eps=RMS_EPS):
    xf = x.astype(jnp.float32)
    y = xf * lax.rsqrt(jnp.mean(xf * xf, axis=-1, keepdims=True) + eps)
    return (y * g.astype(jnp.float32)).astype(x.dtype)

def swiglu(x, w_gate, w_up, w_down):
    return (jax.nn.silu(x @ w_gate) * (x @ w_up)) @ w_down

def causal_dwconv(x, w):
    K = w.shape[0]
    S = x.shape[1]
    xp = jnp.pad(x, ((0, 0), (K - 1, 0), (0, 0)))
    return sum(xp[:, k:k + S] * w[k] for k in range(K))

def t5_bucket(n):
    max_exact = NUM_BUCKETS // 2
    nf = jnp.maximum(n, 1).astype(jnp.float32)
    large = max_exact + (jnp.log(nf / max_exact) / math.log(MAX_DISTANCE / max_exact)
                         * (NUM_BUCKETS - max_exact)).astype(jnp.int32)
    large = jnp.minimum(large, NUM_BUCKETS - 1)
    return jnp.where(n < max_exact, n, large)

def diff_attention(q, k, v, lq1, lk1, lq2, lk2, subln_g, rel_bias, lam_init):
    B, S, _ = q.shape
    nblk = S // Q_BLOCK
    q = q.reshape(B, S, DA_HEADS, 2, DA_HEAD_DIM) * (DA_HEAD_DIM ** -0.5)
    k = k.reshape(B, S, DA_HEADS, 2, DA_HEAD_DIM)
    v = v.reshape(B, S, DA_HEADS, 2 * DA_HEAD_DIM)
    f32 = jnp.float32
    lam = (jnp.exp(jnp.sum(lq1.astype(f32) * lk1.astype(f32)))
           - jnp.exp(jnp.sum(lq2.astype(f32) * lk2.astype(f32))) + lam_init)
    k_pos = jnp.arange(S)
    q_blocks = jnp.moveaxis(q.reshape(B, nblk, Q_BLOCK, DA_HEADS, 2, DA_HEAD_DIM), 1, 0)

    def block(args):
        qb, start = args
        q_pos = start + jnp.arange(Q_BLOCK)
        dist = q_pos[:, None] - k_pos[None, :]
        bias = rel_bias[t5_bucket(jnp.maximum(dist, 0))]
        bias = bias.reshape(Q_BLOCK, S, DA_HEADS, 2).transpose(2, 3, 0, 1).astype(f32)
        logits = jnp.einsum('bqhmd,bkhmd->bhmqk', qb, k).astype(f32) + bias
        logits = jnp.where(dist >= 0, logits, NEG_INF_2)
        p = jax.nn.softmax(logits, axis=-1)
        attn = p[:, :, 0] - lam * p[:, :, 1]
        return jnp.einsum('bhqk,bkhe->bqhe', attn.astype(v.dtype), v)

    starts = jnp.arange(nblk) * Q_BLOCK
    o = lax.map(block, (q_blocks, starts))
    o = jnp.moveaxis(o, 0, 1).reshape(B, S, DA_HEADS, 2 * DA_HEAD_DIM)
    o = rms_norm(o, subln_g, SUBLN_EPS) * (1.0 - lam_init)
    return o.reshape(B, S, DA_WIDTH)

def block_diag_linear(x, w, b):
    B, S, _ = x.shape
    xb = x.reshape(B, S, LRU_BLOCKS, LRU_BLOCK)
    y = jnp.einsum('bsni,nij->bsnj', xb, w) + b
    return y.reshape(B, S, LRU_WIDTH)

def rg_lru(x, wa, ba, wx, bx, lam):
    f32 = jnp.float32
    r = jax.nn.sigmoid(block_diag_linear(x, wa, ba)).astype(f32)
    i = jax.nn.sigmoid(block_diag_linear(x, wx, bx)).astype(f32)
    log_a = -LRU_C * r * jax.nn.softplus(-lam.astype(f32))
    a = jnp.exp(log_a)
    mult = jnp.sqrt(-jnp.expm1(2.0 * log_a))
    b = mult * (i * x.astype(f32))

    def combine(e, l):
        return (e[0] * l[0], l[0] * e[1] + l[1])

    _, h = lax.associative_scan(combine, (a, b), axis=1)
    return h.astype(x.dtype)

def second_inputs(seed: int = 0) -> dict:
    key = jax.random.key(seed)
    ks = iter(jax.random.split(key, 40))
    f32 = jnp.float32

    def nrm(shape, fan_in):
        return jax.random.normal(next(ks), shape, f32) * fan_in ** -0.5

    def gain(shape):
        return 1.0 + 0.02 * jax.random.normal(next(ks), shape, f32)

    def small(shape, s):
        return s * jax.random.normal(next(ks), shape, f32)

    u = jax.random.uniform(next(ks), (DEPTH, LRU_WIDTH), f32, minval=0.9, maxval=0.999)
    a0 = u ** (1.0 / LRU_C)
    lru_lambda = jnp.log(a0) - jnp.log1p(-a0)

    return {
        "x": jax.random.normal(next(ks), (BATCH, SEQ, D_MODEL), f32),
        "rel_bias": small((NUM_BUCKETS, 2 * DA_HEADS), 0.5),
        "ffn1_norm": gain((DEPTH, D_MODEL)),
        "ffn1_gate": nrm((DEPTH, D_MODEL, D_FF_2), D_MODEL),
        "ffn1_up": nrm((DEPTH, D_MODEL, D_FF_2), D_MODEL),
        "ffn1_down": nrm((DEPTH, D_FF_2, D_MODEL), D_FF_2),
        "mix_norm": gain((DEPTH, D_MODEL)),
        "w_in": nrm((DEPTH, D_MODEL, IN_WIDTH_2), D_MODEL),
        "w_out": nrm((DEPTH, MIX_WIDTH_2, D_MODEL), MIX_WIDTH_2),
        "lam_q1": small((DEPTH, DA_HEAD_DIM), 0.1),
        "lam_k1": small((DEPTH, DA_HEAD_DIM), 0.1),
        "lam_q2": small((DEPTH, DA_HEAD_DIM), 0.1),
        "lam_k2": small((DEPTH, DA_HEAD_DIM), 0.1),
        "subln_gain": gain((DEPTH, 2 * DA_HEAD_DIM)),
        "sc_conv_w": nrm((DEPTH, SC_KERNEL, SC_WIDTH), SC_KERNEL),
        "lru_conv_w": nrm((DEPTH, LRU_CONV, LRU_WIDTH), LRU_CONV),
        "lru_conv_b": small((DEPTH, LRU_WIDTH), 0.01),
        "lru_wa": nrm((DEPTH, LRU_BLOCKS, LRU_BLOCK, LRU_BLOCK), LRU_BLOCK),
        "lru_ba": small((DEPTH, LRU_BLOCKS, LRU_BLOCK), 0.01),
        "lru_wx": nrm((DEPTH, LRU_BLOCKS, LRU_BLOCK, LRU_BLOCK), LRU_BLOCK),
        "lru_bx": small((DEPTH, LRU_BLOCKS, LRU_BLOCK), 0.01),
        "lru_lambda": lru_lambda,
        "ffn2_norm": gain((DEPTH, D_MODEL)),
        "ffn2_gate": nrm((DEPTH, D_MODEL, D_FF_2), D_MODEL),
        "ffn2_up": nrm((DEPTH, D_MODEL, D_FF_2), D_MODEL),
        "ffn2_down": nrm((DEPTH, D_FF_2, D_MODEL), D_FF_2),
        "final_norm": gain((D_MODEL,)),
    }

def second_block(x, rel_bias, ffn1_norm, ffn1_gate, ffn1_up, ffn1_down, mix_norm, w_in, w_out,
              lam_q1, lam_k1, lam_q2, lam_k2, subln_gain, sc_conv_w, lru_conv_w, lru_conv_b,
              lru_wa, lru_ba, lru_wx, lru_bx, lru_lambda, ffn2_norm, ffn2_gate, ffn2_up,
              ffn2_down, final_norm):
    for l in range(DEPTH):
        h = x + 0.5 * swiglu(rms_norm(x, ffn1_norm[l]), ffn1_gate[l], ffn1_up[l], ffn1_down[l])

        u = rms_norm(h, mix_norm[l])
        z = u @ w_in[l]
        q, k, v, sc_b, sc_c, sc_x, lru_x, lru_g = jnp.split(z, IN_SPLIT_POINTS, axis=-1)

        lam_init = 0.8 - 0.6 * math.exp(-0.3 * l)
        y_da = diff_attention(q, k, v, lam_q1[l], lam_k1[l], lam_q2[l], lam_k2[l],
                              subln_gain[l], rel_bias, lam_init)
        y_sc = sc_b * causal_dwconv(sc_c * sc_x, sc_conv_w[l])
        xr = causal_dwconv(lru_x, lru_conv_w[l]) + lru_conv_b[l]
        y_lru = jax.nn.gelu(lru_g) * rg_lru(xr, lru_wa[l], lru_ba[l], lru_wx[l], lru_bx[l],
                                            lru_lambda[l])

        h = h + jnp.concatenate([y_da, y_sc, y_lru], axis=-1) @ w_out[l]

        x = h + 0.5 * swiglu(rms_norm(h, ffn2_norm[l]), ffn2_gate[l], ffn2_up[l], ffn2_down[l])
    return rms_norm(x, final_norm)


def setup_inputs(seed=0):
    out = dict(first_inputs(seed))
    for name, value in second_inputs(seed + 1).items():
        if name != "x":
            out[name + "_2"] = value
    return out


def reference(
    x, w_in, fox_b_f, mla_g_q, mla_g_kv, mla_w_uq, mla_w_ukv, swa_sinks, mix_g, w_o, ln1_g,
    ln1_b, w_gate, w_up, w_down, ln2_g, ln2_b, rel_bias_2, ffn1_norm_2, ffn1_gate_2, ffn1_up_2,
    ffn1_down_2, mix_norm_2, w_in_2, w_out_2, lam_q1_2, lam_k1_2, lam_q2_2, lam_k2_2,
    subln_gain_2, sc_conv_w_2, lru_conv_w_2, lru_conv_b_2, lru_wa_2, lru_ba_2, lru_wx_2,
    lru_bx_2, lru_lambda_2, ffn2_norm_2, ffn2_gate_2, ffn2_up_2, ffn2_down_2, final_norm_2,
):
    x = first_block(
        x, w_in, fox_b_f, mla_g_q, mla_g_kv, mla_w_uq, mla_w_ukv, swa_sinks, mix_g, w_o, ln1_g,
        ln1_b, w_gate, w_up, w_down, ln2_g, ln2_b,
    )
    return second_block(
        x, rel_bias_2, ffn1_norm_2, ffn1_gate_2, ffn1_up_2, ffn1_down_2, mix_norm_2, w_in_2,
        w_out_2, lam_q1_2, lam_k1_2, lam_q2_2, lam_k2_2, subln_gain_2, sc_conv_w_2,
        lru_conv_w_2, lru_conv_b_2, lru_wa_2, lru_ba_2, lru_wx_2, lru_bx_2, lru_lambda_2,
        ffn2_norm_2, ffn2_gate_2, ffn2_up_2, ffn2_down_2, final_norm_2,
    )


_drawn_inputs = setup_inputs


def setup_inputs(seed=0):
    import zlib

    import numpy as np

    out = dict(_drawn_inputs(seed))
    spreads = {}
    factors = {'fox_b_f': 26.392,
     'mla_g_q': 8.0,
     'mla_g_kv': 4.183,
     'swa_sinks': 3.68,
     'mix_g': 2.832,
     'ffn1_norm_2': 4.28,
     'lam_k1_2': 5.857,
     'lam_k2_2': 8.0,
     'subln_gain_2': 20.45,
     'lru_conv_b_2': 13.626,
     'lru_ba_2': 170.939,
     'lru_bx_2': 64.0,
     'ffn2_norm_2': 6.345,
     'final_norm_2': 21.102,
     'mix_norm_2': 3.077,
     'lru_wa_2': 3.109}
    for name, (base, spread) in spreads.items():
        noise = np.random.default_rng([zlib.crc32(name.encode()), seed]).standard_normal(out[name].shape)
        drawn = base * np.exp(spread * noise) if base else spread * noise
        out[name] = __import__('jax').numpy.asarray(drawn.astype(out[name].dtype))
    for name, factor in factors.items():
        out[name] = (out[name] * factor).astype(out[name].dtype)
    return out
```

```python
from contextlib import ExitStack, contextmanager
import math

import numpy as np
import concourse.bass as bass
from concourse import mybir

F32 = mybir.dt.float32
F32R = mybir.dt.float32r
ALU = mybir.AluOpType
ACT = mybir.ActivationFunctionType
AX = mybir.AxisListType

P = 128
D = 1024
S = 512
DEPTH = 2
HD = 64
DC = D // P
TT = S // P
FF = 2816
FC = FF // P
NEG = -1e30
ALPHA = (2.0 * DEPTH) ** 0.25
ROPE = 32
BUCKETS = 32
SLOTS = 4
UNIT = 8 * P
FFN_UNITS = 3 * FC
B1_PROJ = 22
B1_UNITS = B1_PROJ + DC + FFN_UNITS
B2_PROJ = 24
B2_UNITS = 2 * FFN_UNITS + B2_PROJ + DC
UNITS = DEPTH * (B1_UNITS + B2_UNITS)

C1 = dict(mix_g=0, ln1_g=8, ln1_b=16, ln2_g=24, ln2_b=32, g_q=40, g_kv=42, b_f=43, sink=44)
N1 = 48
C2 = dict(ffn1=0, mix=8, ffn2=16, sc_w=24, lru_w=30, lru_b=38, ba=40, bx=42, lam=44, subln=46,
          final=47, lq1=55, lk1=56, lq2=57, lk2=58)
N2 = 59
UV_TILES = ((0, 1), (2,), (3,))
T5W = 3 * P


class Counts:

    def __init__(self, known):
        self.known = known or {}
        self.found = {}
        self.loops = []

    @contextmanager
    def loop(self, engine, name, rounds):
        with engine.Fori(0, rounds) as i:
            self.loops.append((name, rounds, i))
            for s in self.signals:
                s.enter()
            yield i
            for s in self.signals:
                s.leave(name, rounds)
            self.loops.pop()


class Signal:

    def __init__(self, counts, sem, name, credit=0):
        self.counts, self.sem, self.name, self.credit = counts, sem, name, credit
        self.total, self.base, self.open, self.events = credit, [], [[]], {}

    def enter(self):
        self.base.append(self.total)
        self.open.append([])

    def leave(self, name, rounds):
        start = self.base.pop()
        each = self.total - start
        mine = self.open.pop()
        for key in mine:
            self.events[key][1][name] = (each, rounds)
        self.open[-1] += mine
        self.total = start + each * rounds
        self.counts.found[self.name] = self.events

    def done(self, key, n=1):
        assert key not in self.events, (self.name, key)
        self.total += n
        self.events[key] = [self.total, {}]
        self.open[-1].append(key)
        self.counts.found[self.name] = self.events
        return self.sem, n

    def number(self, key):
        known = self.counts.known
        if not known:
            return 1
        value, loops = known[self.name][key]
        here = {name: i for name, _, i in self.counts.loops}
        for name, (each, rounds) in loops.items():
            value = value + (here[name] * each if name in here else (rounds - 1) * each)
        return value

    def after(self, key):
        return self.sem, self.number(key)

    def before(self, key):
        return self.sem, self.number(key) - self.credit

    def slot(self, key, depth):
        if not self.counts.known:
            return 0
        value, loops = self.counts.known[self.name][key]
        assert all(each % depth == 0 for each, _ in loops.values()), (self.name, key, loops)
        return (value - self.credit - 1) % depth


def build(nc, t, known):
    counts = Counts(known)
    loop = counts.loop
    with ExitStack() as ctx:
        def sb(name, shape, dt=F32):
            return ctx.enter_context(nc.sbuf_tensor(name, shape, dt))

        def overlay(*entries):
            with ExitStack() as scope:
                return [scope.enter_context(nc.sbuf_tensor(*entry)) for entry in entries]

        counts.signals = []

        def signal(name, credit=0):
            s = Signal(counts, ctx.enter_context(nc.semaphore(name)), name, credit)
            counts.signals.append(s)
            return s

        resid = sb("resid", [P, DC, S])
        raw = sb("raw", [P, SLOTS, UNIT])
        w_hi = sb("w_hi", [P, SLOTS, UNIT], F32R)
        w_lo = sb("w_lo", [P, SLOTS, UNIT], F32R)
        ident = sb("ident", [P, P])
        mask = sb("mask", [P, P])
        mask_t = sb("mask_t", [P, P])
        neg_tri = sb("neg_tri", [P, P])
        ones = sb("ones", [P, P])
        neg_ones = sb("neg_ones", [P, P])
        zero = sb("zero", [P, 1])
        par1 = sb("par1", [P, N1])
        par2 = sb("par2", [P, N2 + 2])
        small = sb("small", [P, 128])
        cum = sb("cum", [4, S])
        diag = sb("diag", [P, 4 * TT, P])
        work = sb("work", [P, 4, S])
        xn_hi, xn_lo = overlay(("xn_hi", [P, DC, S], F32R), ("xn_lo", [P, DC, S], F32R))
        probs_t, probs, aug_q, aug_k = overlay(
            ("probs_t", [P, 2, TT, S], F32), ("probs", [P, 3, S], F32),
            ("aug_q", [P, 4, S], F32), ("aug_k", [P, S], F32))
        probs2_t, probs2 = overlay(("probs2_t", [P, 2, TT, S], F32), ("probs2", [P, 6, S], F32))
        sb("place_of_xn", [P, 2 * DC * S])
        h_hi, h_lo = overlay(("h_hi", [P, FC, S], F32R), ("h_lo", [P, FC, S], F32R))
        (qmix, fox_k, fox_v, sb_k, sb_v, swa_k, swa_v, cq, mla_q, mla_k, mla_v, rope, alibi,
         lat_hi, lat_lo) = overlay(
            ("qmix", [P, DC, S], F32), ("fox_k", [P, 2, S], F32), ("fox_v", [P, TT, 256], F32),
            ("sb_k", [P, 2, S], F32), ("sb_v", [P, TT, 256], F32), ("swa_k", [P, S], F32),
            ("swa_v", [P, TT, P], F32), ("cq", [P, 3, S], F32),
            ("mla_q", [P, 4, S], F32), ("mla_k", [P, 4, S], F32), ("mla_v", [P, TT, 256], F32),
            ("rope", [P, 4, S], F32), ("alibi", [P, 4, 256], F32),
            ("lat_hi", [P, 3, S], F32R), ("lat_lo", [P, 3, S], F32R))
        (mix2, da_k, da_v, sc_c, sc_x, sc_b, lru_x, lru_g, xr, gate_r, gate_i, lru_a, lru_w, t5) = overlay(
            ("mix2", [P, DC, S], F32), ("da_k", [P, 4, S], F32), ("da_v", [P, TT, S], F32),
            ("sc_c", [P, 2, S], F32), ("sc_x", [P, 2, S], F32), ("sc_b", [P, 2, S], F32),
            ("lru_x", [P, 2, S], F32), ("lru_g", [P, 2, S], F32), ("xr", [P, 2, S], F32),
            ("gate_r", [P, 2, S], F32), ("gate_i", [P, 2, S], F32), ("lru_a", [P, 2, S], F32),
            ("lru_w", [P, 4, P], F32), ("t5", [P, 8, 256], F32))
        bucket_of, rel, rel_far, rel_rows, t5_row = overlay(
            ("bucket_of", [P, T5W], F32), ("rel", [P, 8], F32), ("rel_far", [P, 8], F32),
            ("rel_rows", [P, 8, P], F32), ("t5_row", [P, 8, T5W], F32))
        sb("place_of_h", [P, 2 * FC * S])

        bank_a = [ctx.enter_context(nc.psum_tensor(f"bank_a{i}", [P, S], F32)) for i in range(2)]
        bank_v = [ctx.enter_context(nc.psum_tensor(f"bank_v{i}", [P, S], F32)) for i in range(2)]
        bank_s = [ctx.enter_context(nc.psum_tensor(f"bank_s{i}", [P, S], F32)) for i in range(4)]
        stat_bank = bank_s[3]
        t5_dram = t["t5_rows"]

        raw_in = [signal(f"raw_in{u}") for u in range(SLOTS)]
        const_in = signal("const_in")
        par_in = signal("par_in")
        t5_out = signal("t5_out")
        out_done = signal("out_done")
        fills = signal("fills")
        hi_split = signal("hi_split")
        w_split = signal("w_split", SLOTS)
        w_used = signal("w_used", SLOTS)
        sums = signal("sums")
        scores_ready = signal("scores_ready")
        ffn_entered = signal("ffn_entered")
        turned = signal("turned")
        a_read = signal("a_read", 2)
        s_read = signal("s_read", 4)
        x_hi = signal("x_hi")
        squared = signal("squared")
        rooted = signal("rooted")
        affine = signal("affine")
        act_step = signal("act_step")
        v_read = signal("v_read", 2)
        x_lo = signal("x_lo")
        value = signal("value")
        centered = signal("centered")
        scaled = signal("scaled")
        diag_ready = signal("diag_ready")
        row_max = signal("row_max")
        softplus_ready = signal("softplus_ready")
        probs_ready = signal("probs_ready")
        dve_step = signal("dve_step")

        block = ctx.enter_context(nc.Block())

        @block.sync
        def _(sp):
            with loop(sp, "stream", UNITS // SLOTS) as i:
                for u in range(SLOTS):
                    sp.wait_ge(*w_split.before(("unit", u)))
                    sp.dma_start(raw[:, u, :], t["w_stream"][i, u]
                                 ).then_inc(*raw_in[u].done("unit", 16))
            sp.wait_ge(*scaled.after(("final", DC - 1)))
            sp.dma_start(t["out"], resid[:, :, :]).then_inc(*out_done.done("out", 16))
            sp.wait_ge(*out_done.after("out"))

        @block.gpsimd
        def _(pool):
            pool.sem_inc(w_split.sem, SLOTS)
            pool.memset(zero[:, :], 0.0).then_inc(*fills.done("zero"))
            pool.memset(ones[:, :], 1.0).then_inc(*fills.done("ones"))
            pool.memset(neg_ones[:, :], -1.0).then_inc(*fills.done("neg_ones"))
            pool.wait_ge(*fills.after("neg_ones"))
            with loop(pool, "stream", UNITS // SLOTS):
                for u in range(SLOTS):
                    pool.wait_ge(*raw_in[u].after("unit"))
                    pool.wait_ge(w_used.sem, w_split.before(("unit", u))[1])
                    pool.tensor_tensor(w_hi[:, u, :], raw[:, u, :], zero[:, 0:1].to_broadcast([P, UNIT]),
                                       ALU.add).then_inc(*hi_split.done(("unit", u)))
                    pool.wait_ge(*hi_split.after(("unit", u)))
                    pool.tensor_tensor(w_lo[:, u, :], raw[:, u, :], w_hi[:, u, :].bitcast(F32),
                                       ALU.subtract).then_inc(*w_split.done(("unit", u)))

        @block.tensor
        def _(pe):
            def a_bank(key):
                pe.wait_ge(*a_read.before(key))
                return bank_a[a_read.slot(key, 2)]

            def v_bank(key):
                pe.wait_ge(*v_read.before(key))
                return bank_v[v_read.slot(key, 2)]

            def s_bank(key):
                pe.wait_ge(*s_read.before(key))
                return bank_s[s_read.slot(key, 4)]

            def unit(key):
                pe.wait_ge(w_split.sem, w_used.number(key))
                return w_used.slot(key, SLOTS)

            def mm3(out, lhs_hi, lhs_lo, rhs_hi, rhs_lo, first, last):
                pe.matmul(out, lhs_hi, rhs_hi, start=first, stop=False)
                pe.matmul(out, lhs_hi, rhs_lo, start=False, stop=False)
                return pe.matmul(out, lhs_lo, rhs_hi, start=False, stop=last)

            def w_tile(u, k, n=P):
                return w_hi[:, u, k * n:(k + 1) * n], w_lo[:, u, k * n:(k + 1) * n]

            def project(key, bank, wait=None, hi=xn_hi, lo=xn_lo):
                u = unit(key)
                b = bank(key)
                for c in range(DC):
                    if wait:
                        pe.wait_ge(*x_lo.after((wait, c)))
                    mm = mm3(b[:, :], *w_tile(u, c), hi[:, c, :], lo[:, c, :], c == 0, c == DC - 1)
                mm.then_inc(*w_used.done(key))

            def project_rows(tag, n_units, cols):
                per = DC // n_units
                banks = [a_bank((tag, 0)), v_bank((tag, 1)), a_bank((tag, 2)), v_bank((tag, 3))]
                for n in range(n_units):
                    u = unit((tag, "unit", n))
                    for tile in range(TT):
                        cut = slice(tile * P, (tile + 1) * P)
                        for k in range(per):
                            c = n * per + k
                            mm = mm3(banks[tile][:, 0:cols], xn_hi[:, c, cut], xn_lo[:, c, cut],
                                     *w_tile(u, k, cols), c == 0, c == DC - 1)
                        if n == n_units - 1 and tile < TT - 1:
                            mm.then_inc(*sums.done((tag, tile)))
                    mm.then_inc(*w_used.done((tag, "unit", n)))

            def token_sums(key, tiles, n, first, last):
                for tile in range(TT):
                    mm = pe.matmul(stat_bank[:, n + tile:n + tile + 1], tiles(slice(tile * P, (tile + 1) * P)),
                                   ones[:, 0:1], start=first and tile == 0, stop=True,
                                   skip_group_check=True)
                mm.then_inc(*sums.done(key))

            def spread(tag, groups=1):
                for g in range(groups):
                    pe.wait_ge(*diag_ready.after((tag, g)))
                    for tile in range(TT):
                        mm = pe.matmul(bank_s[g][:, tile * P:(tile + 1) * P], ones[:, :],
                                       diag[:, g * TT + tile, :], start=True, stop=True)
                    mm.then_inc(*sums.done((tag, "spread", g)))

            def rms(tag, groups, per):
                n = groups * per
                for c in range(n):
                    pe.wait_ge(*squared.after((tag, c)))
                    token_sums((tag, "sum", c), lambda cut: work[:, c % 2, cut], c // per * TT,
                               c == 0, c == n - 1)
                spread(tag, groups)

            def mean_chunk(tag, c):
                token_sums((tag, "mean", c), lambda cut: resid[:, c, cut], 0, c == 0, c == DC - 1)

            def variance(tag):
                spread(tag + "_mean")
                for c in range(DC):
                    pe.wait_ge(*squared.after((tag, c)))
                    token_sums((tag, "sum", c), lambda cut: work[:, c % 2, cut], 0, c == 0, c == DC - 1)
                spread(tag)

            def down(tag, after_chunk=None):
                for c in range(DC):
                    key = (tag, "down", c)
                    b = v_bank(key)
                    for f in range(FC):
                        i = c * FC + f
                        if i % 8 == 0:
                            u = unit((tag, "wd", i // 8))
                        if c == 0:
                            pe.wait_ge(*x_lo.after((tag, "h", f % 2)))
                        mm = mm3(b[:, :], *w_tile(u, i % 8), h_hi[:, f, :], h_lo[:, f, :], f == 0, f == FC - 1)
                        if i % 8 == 7:
                            mm.then_inc(*w_used.done((tag, "wd", i // 8)))
                        elif f == FC - 1:
                            mm.then_inc(*sums.done(key))
                    if after_chunk and c:
                        pe.wait_ge(*v_read.after((tag, "down", c - 1)))
                        after_chunk(c - 1)
                if after_chunk:
                    pe.wait_ge(*v_read.after((tag, "down", DC - 1)))
                    after_chunk(DC - 1)

            def ffn(tag, split, after_chunk=None):
                for c in range(DC):
                    pe.wait_ge(*x_lo.after((split, c)))
                pe.sem_inc(*ffn_entered.done(tag))
                with loop(pe, tag, FC // 2):
                    for k in range(2):
                        project((tag, "gate", k), a_bank)
                        project((tag, "up", k), v_bank)
                down(tag, after_chunk)

            def turn(key, source, n):
                pe.wait_ge(*probs_ready.after(key))
                b = a_bank(key)
                for j in range(n):
                    mm = pe.transpose(b[:, j * P:(j + 1) * P], source[:, j * P:(j + 1) * P], ident[:, :])
                mm.then_inc(*turned.done(key))

            def attend(items, scores, turn_item, finish):
                for n in range(len(items) + 3):
                    if n < len(items):
                        scores(items[n])
                    if 2 <= n < len(items) + 2:
                        turn_item(n - 2)
                    if n >= 3 and items[n - 3][1] == TT - 1:
                        finish(items[n - 3][0])

            heads = [(h, i) for h in range(4) for i in range(TT)]

            def values(tag, h, v, pt, rows, banded=False):
                pe.wait_ge(*a_read.after((tag, h, TT - 1)))
                b = v_bank((tag, "out", h))
                for j in range(TT):
                    end = min((j + 2) * P, S) if banded else S
                    mm = pe.matmul(b[rows, j * P:end], v(j, h), pt[:, h % 2, j, j * P:end],
                                   start=(j == 0), stop=True, skip_group_check=True)
                mm.then_inc(*sums.done((tag, "out", h)))

            def half(n):
                return slice(n * HD, (n + 1) * HD)

            def fox():
                def scores(item):
                    h, i = item
                    key = ("fox", h, i)
                    n, cut, r, c = (i + 1) * P, slice(i * P, (i + 1) * P), half(h % 2), h // 2
                    b = s_bank(key)
                    pe.matmul(b[:, 0:n], qmix[r, c, cut], fox_k[r, c, 0:n], start=True, stop=True)
                    pe.matmul(b[:, 0:n], aug_q[:, h, cut], aug_k[:, 0:n], start=False, stop=True, skip_group_check=True)
                    pe.matmul(b[:, i * P:n], ident[:, :], mask[:, :], start=False, stop=True,
                              skip_group_check=True).then_inc(*scores_ready.done(key))

                pe.wait_ge(*dve_step.after("aug"))
                attend(heads, scores, lambda n: turn(("fox", *heads[n]), probs[:, n % 3, :], heads[n][1] + 1),
                       lambda h: values("fox", h, lambda j, h: fox_v[:, j, half(h)], probs_t, half(h % 2)))

            def mla():
                def scores(item):
                    h, i = item
                    key = ("mla", h, i)
                    n, cut = (i + 1) * P, slice(i * P, (i + 1) * P)
                    b = s_bank(key)
                    pe.matmul(b[:, 0:n], mla_q[0:96, h, cut], mla_k[0:96, h, 0:n], start=True, stop=True)
                    pe.matmul(b[:, i * P:n], ident[:, :], mask[:, :], start=False, stop=True,
                              skip_group_check=True).then_inc(*scores_ready.done(key))

                attend(heads, scores, lambda n: turn(("mla", *heads[n]), probs[:, n % 3, :], heads[n][1] + 1),
                       lambda h: values("mla", h, lambda j, h: mla_v[:, j, half(h)], probs_t, half(h % 2)))

            def swa():
                def scores(item):
                    h, i = item
                    key = ("swa", h, i)
                    lo, n, cut, r = max(i - 1, 0) * P, (i + 1) * P, slice(i * P, (i + 1) * P), half(h // 2)
                    b = s_bank(key)
                    pe.matmul(b[:, 0:n - lo], qmix[r, 6 + h % 2, cut], swa_k[r, lo:n], start=True, stop=True)
                    pe.matmul(b[:, 0:n - lo], ident[:, :], alibi[:, h, 256 - (n - lo):256],
                              start=False, stop=True, skip_group_check=True).then_inc(*scores_ready.done(key))

                attend(heads, scores, lambda n: turn(("swa", *heads[n]), probs[:, n % 3, :], min(heads[n][1], 1) + 1),
                       lambda h: values("swa", h, lambda j, h: swa_v[:, j, half(h // 2)], probs_t,
                                        half(h // 2), banded=True))

            def stick():
                order = [(h, j) for h in range(4) for j in reversed(range(TT))]

                def z(n):
                    h, j = order[n]
                    key, r = ("stick", h, j), half(h % 2)
                    b = s_bank(key)
                    pe.matmul(b[:, 0:S - j * P], sb_k[r, h // 2, j * P:(j + 1) * P],
                              qmix[r, 4 + h // 2, j * P:S], start=True, stop=True)
                    pe.matmul(b[:, 0:P], ident[:, :], mask_t[:, :], start=False, stop=True,
                              skip_group_check=True).then_inc(*scores_ready.done(key))

                def minus_sums(n):
                    h, j = order[n]
                    key = ("stick", h, j)
                    b = bank_s[s_read.slot(key, 4)]
                    pe.wait_ge(*softplus_ready.after(key))
                    mm = pe.matmul(b[:, 0:S - j * P], neg_tri[:, :], probs_t[:, 1, j, j * P:S],
                                   start=False, stop=True, skip_group_check=True)
                    for k in range(j + 1, TT):
                        mm = pe.matmul(b[:, (k - j) * P:S - j * P], neg_ones[:, :], probs_t[:, 1, k, k * P:S],
                                       start=False, stop=True, skip_group_check=True)
                    mm.then_inc(*sums.done(key))

                def out(h):
                    pe.wait_ge(*s_read.after(("stick", h, 0)))
                    b = v_bank(("stick", "out", h))
                    for j in range(TT):
                        mm = pe.matmul(b[half(h % 2), j * P:S], sb_v[:, j, half(h)], probs_t[:, 0, j, j * P:S],
                                       start=(j == 0), stop=True, skip_group_check=True)
                    mm.then_inc(*sums.done(("stick", "out", h)))

                for n in range(len(order) + 2):
                    if n < len(order):
                        z(n)
                    if 1 <= n <= len(order):
                        minus_sums(n - 1)
                    if n >= 2 and order[n - 2][1] == 0:
                        out(order[n - 2][0])

            def diff():
                def scores(item):
                    h, i = item
                    n, cut = (i + 1) * P, slice(i * P, (i + 1) * P)
                    lo = max(i - 1, 0) * P
                    for m in range(2):
                        key = ("diff", h, i, m)
                        b = s_bank(key)
                        pe.matmul(b[:, 0:n], mix2[half(m), h, cut], da_k[half(m), h, 0:n], start=True, stop=True)
                        pe.matmul(b[:, lo:n], ident[:, :], t5[:, 2 * h + m, 256 - (n - lo):256],
                                  start=False, stop=True, skip_group_check=True
                                  ).then_inc(*scores_ready.done(key))

                attend(heads, scores,
                       lambda n: turn(("diff", *heads[n]), probs2[:, n % 3 * 2, :], heads[n][1] + 1),
                       lambda h: values("diff", h, lambda j, h: da_v[:, j, h * P:(h + 1) * P], probs2_t, slice(0, P)))

            pe.sem_inc(w_used.sem, SLOTS)
            pe.wait_ge(*fills.after("neg_ones"))
            pe.wait_ge(*const_in.after("all"))
            pe.wait_ge(*dve_step.after("rel_rows"))
            for m in range(8):
                b = a_bank(("t5", m))
                pe.matmul(b[:, 0:T5W], rel_rows[0:BUCKETS + 1, m, :], bucket_of[0:BUCKETS + 1, :],
                          start=True, stop=True).then_inc(*sums.done(("t5", m)))

            with loop(pe, "layer1", DEPTH):
                project("kr", v_bank, "in1")
                for n in range(2):
                    project(("fq", n), a_bank)
                for n in range(2):
                    project(("fk", n), v_bank)
                project_rows("fv", 2, 256)
                for n in range(3):
                    project(("c", n), a_bank)
                for n in range(2):
                    project(("sq", n), a_bank)
                for n in range(2):
                    project(("sk", n), v_bank)
                project_rows("sv", 2, 256)
                for n in range(2):
                    project(("wq", n), a_bank)
                project("wk", v_bank)
                u = unit("wv")
                b = v_bank("wv")
                for tile in range(TT):
                    cut = slice(tile * P, (tile + 1) * P)
                    for c in range(DC):
                        mm = mm3(b[:, cut], xn_hi[:, c, cut], xn_lo[:, c, cut], *w_tile(u, c), c == 0, c == DC - 1)
                mm.then_inc(*w_used.done("wv"))
                for tag, chunks in (("lat_q", (0, 1)), ("lat_kv", (2,))):
                    for n, c in enumerate(chunks):
                        pe.wait_ge(*squared.after((tag, n)))
                        token_sums((tag, "sum", n), lambda cut: work[:, n % 2, cut], 0, n == 0, n == len(chunks) - 1)
                    spread(tag)
                u = unit("uq")
                for c in range(2):
                    pe.wait_ge(*x_lo.after(("lat", c)))
                for n in range(5):
                    b = v_bank(("uq", n))
                    rows = slice(0, 96 if n < 4 else P)
                    for c in range(2):
                        cols = slice(c * S + n * 96, c * S + n * 96 + rows.stop)
                        mm = mm3(b[rows, :], w_hi[:, u, cols], w_lo[:, u, cols], lat_hi[:, c, :], lat_lo[:, c, :],
                                 c == 0, c == 1)
                    mm.then_inc(*(sums.done(("uq", n)) if n < 4 else w_used.done("uq")))
                u = unit("ukv")
                pe.wait_ge(*x_lo.after(("lat", 2)))
                for h in range(4):
                    b = a_bank(("uk", h))
                    cols = slice(h * HD, h * HD + P)
                    mm3(b[:, :], w_hi[:, u, cols], w_lo[:, u, cols], lat_hi[:, 2, :], lat_lo[:, 2, :],
                        True, True).then_inc(*sums.done(("uk", h)))
                for n, tiles in enumerate(UV_TILES):
                    b = a_bank(("uv", n))
                    for k, tile in enumerate(tiles):
                        cut = slice(tile * P, (tile + 1) * P)
                        mm = mm3(b[:, k * 256:(k + 1) * 256], lat_hi[:, 2, cut], lat_lo[:, 2, cut],
                                 w_hi[:, u, 256:512], w_lo[:, u, 256:512], True, True)
                    mm.then_inc(*(sums.done(("uv", n)) if n < 2 else w_used.done("ukv")))
                fox()
                mla()
                stick()
                swa()
                rms("mixnorm", 4, 2)
                for c in range(DC):
                    project(("wo", c), v_bank, "mixnorm" if c == 0 else None)
                    if c:
                        pe.wait_ge(*v_read.after(("wo", c - 1)))
                        mean_chunk("ln1", c - 1)
                pe.wait_ge(*v_read.after(("wo", DC - 1)))
                mean_chunk("ln1", DC - 1)
                variance("ln1")
                ffn("ffn", "ln1", lambda c: mean_chunk("ln2", c))
                variance("ln2")

            with loop(pe, "layer2", DEPTH):
                rms("rms1", 1, DC)
                ffn("ffn1", "rms1")
                rms("rms2", 1, DC)
                for n in range(4):
                    project(("q2", n), a_bank, "rms2" if n == 0 else None)
                for n in range(4):
                    project(("k2", n), v_bank)
                project_rows("v2", 4, S)
                for n in range(2):
                    project(("scc", n), a_bank)
                for n in range(2):
                    project(("scx", n), v_bank)
                for n in range(2):
                    project(("scb", n), a_bank)
                for n in range(2):
                    project(("lx", n), v_bank)
                for n in range(2):
                    project(("lg", n), a_bank)
                for n in range(2):
                    unit(("pad", n))
                    pe.matmul(stat_bank[:, 2:4], ones[:, :], ones[:, 0:2], start=True, stop=True
                              ).then_inc(*w_used.done(("pad", n)))
                pe.wait_ge(*dve_step.after("lam_products"))
                pe.matmul(stat_bank[:, 0:2], ones[0:HD, :], small[0:HD, 64:66], start=True, stop=True
                          ).then_inc(*sums.done("lam_sums"))
                pe.wait_ge(*par_in.after("tables2"))
                for c in range(2):
                    pe.wait_ge(*dve_step.after(("xr", c)))
                    for m, name in enumerate("ri"):
                        b = a_bank(("gate", name, c))
                        pe.matmul(b[:, :], lru_w[:, 2 * m + c, :], xr[:, c, :], start=True, stop=True
                                  ).then_inc(*sums.done(("gate", name, c)))
                diff()
                rms("subln", 4, 1)
                for c in range(DC):
                    project(("wout", c), v_bank, "subln" if c == 0 else None)
                rms("rms3", 1, DC)
                ffn("ffn2", "rms3")
            rms("final", 1, DC)

        @block.scalar
        def _(act):
            def a_bank(key):
                return bank_a[a_read.slot(key, 2)]

            def split_hi(tag, c, source, dest=xn_hi):
                act.activation(dest[:, c, :], source, ACT.Copy).then_inc(*x_hi.done((tag, c)))

            def square(tag, c, source):
                if c >= 2:
                    act.wait_ge(*sums.after((tag, "sum", c - 2)))
                act.activation(work[:, c % 2, :], source, ACT.Square).then_inc(*squared.done((tag, c)))

            def root(tag, groups):
                act.wait_ge(*dve_step.after((tag, "var")))
                act.activation(small[:, 16:16 + groups * TT], small[:, 0:groups * TT], ACT.Sqrt
                               ).then_inc(*rooted.done(tag))

            def copy_bank(key, ready, out, rows=slice(0, P), n=S, func=ACT.Copy, **kw):
                act.wait_ge(*ready.after(key))
                act.activation(out, a_bank(key)[rows, 0:n], func, **kw).then_inc(*a_read.done(key))

            def rms(tag, groups, per, source, ready, split=True):
                n = groups * per
                for c in range(n):
                    ready(c)
                    square(tag, c, source(c))
                root(tag, groups)
                if split:
                    for c in range(n):
                        last = c % per == per - 1
                        act.wait_ge(*(scaled if last else value).after((tag, c)))
                        split_hi(tag, c, work[:, c % 4, :])

            def norm_ln(tag, columns, split):
                for c in range(DC):
                    act.wait_ge(*centered.after((tag, c)))
                    square(tag, c, resid[:, c, :])
                root(tag, 1)
                g, b = (C1[x] for x in columns)
                for c in range(DC + 1):
                    if c < DC:
                        act.wait_ge(*scaled.after((tag, c)))
                        act.activation(resid[:, c, :], resid[:, c, :], ACT.Identity, scale=par1[:, g + c:g + c + 1],
                                       bias=par1[:, b + c:b + c + 1]).then_inc(*affine.done((tag, c)))
                    if c and split:
                        act.wait_ge(*affine.after((tag, c - 1)))
                        split_hi(tag, c - 1, resid[:, c - 1, :])
                act.wait_ge(*affine.after((tag, DC - 1)))

            def ffn(tag):
                with loop(act, tag, FC // 2) as i:
                    for k in range(2):
                        key = (tag, "gate", k)
                        act.wait_ge(*w_used.after(key))
                        act.activation(work[:, k, :], a_bank(key)[:, :], ACT.Silu).then_inc(*a_read.done(key))
                        act.wait_ge(*v_read.after((tag, "up", k)))
                        act.activation(h_hi[:, bass.ds(i * 2 + k, 1), :], work[:, 2 + k:3 + k, :], ACT.Copy
                                       ).then_inc(*x_hi.done((tag, "h", k)))

            def exp_item(key, slot, n, item):
                act.wait_ge(*row_max.after(key))
                b = bank_s[s_read.slot(key, 4)]
                act.activation(slot[:, 0:n], b[:, 0:n], ACT.Exp, bias=small[:, 32 + item:33 + item],
                               accum_out=small[:, 64 + item:65 + item]).then_inc(*s_read.done(key))

            def keep_turned(tag, n, pt, blocks):
                h, i = heads[n]
                key = (tag, h, i)
                if i == 0 and h >= 2:
                    act.wait_ge(*sums.after((tag, "out", h - 2)))
                act.wait_ge(*turned.after(key))
                lo = i + 1 - blocks
                act.activation(pt[:, h % 2, lo:i + 1, i * P:(i + 1) * P],
                               a_bank(key)[:, 0:blocks * P].rearrange("p (j q) -> p j q", q=P), ACT.Copy
                               ).then_inc(*a_read.done(key))

            heads = [(h, i) for h in range(4) for i in range(TT)]

            def softmax(tag, width, blocks, extra=None):
                for n in range(len(heads) + 2):
                    if n < len(heads):
                        exp_item((tag, *heads[n]), probs[:, n % 3, :], width(heads[n][1]), n)
                        if extra:
                            extra(n)
                    if n >= 2:
                        keep_turned(tag, n - 2, probs_t, blocks(heads[n - 2][1]))

            act.sem_inc(a_read.sem, 2)
            act.sem_inc(s_read.sem, 4)
            for name, dest in (("ident", ident[:, :]), ("mask", mask[:, :]), ("mask_t", mask_t[:, :]),
                               ("neg_tri", neg_tri[:, :]), ("bucket_of", bucket_of[0:BUCKETS + 1, :]),
                               ("rel", rel[0:BUCKETS, :]), ("rel_far", rel_far[0:BUCKETS, :])):
                act.dma_start(dest, t[name]).then_inc(*const_in.done(name, 16))
            act.dma_start(resid[:, :, :], t["x"]).then_inc(*const_in.done("all", 16))
            for m in range(8):
                copy_bank(("t5", m), sums, t5_row[:, m, :], n=T5W)
            act.wait_ge(*a_read.after(("t5", 7)))
            act.dma_start(t5_dram.rearrange("m q w -> q m w"), t5_row[:, :, :]).then_inc(*t5_out.done("rows", 16))
            act.wait_ge(*const_in.after("all"))
            act.wait_ge(*t5_out.after("rows"))

            with loop(act, "layer1", DEPTH) as l:
                for c in range(DC):
                    split_hi("in1", c, resid[:, c, :])
                act.wait_ge(*x_hi.after(("in1", DC - 1)))
                act.dma_start(par1[:, :], t["par1"][l]).then_inc(*par_in.done("par1", 16))
                act.dma_start(rope[:, :, :], t["rope"]).then_inc(*par_in.done("rope", 16))
                act.dma_start(alibi[:, :, :], t["alibi"]).then_inc(*par_in.done("tables1", 16))
                for n in range(2):
                    copy_bank(("fq", n), w_used, qmix[:, n, :], scale=HD ** -0.5)
                act.wait_ge(*dve_step.after("fz"))
                f = work[0:4, 0:4, :]
                act.activation(f[:, 1, :], f[:, 0, :], ACT.Abs).then_inc(*act_step.done("f_abs"))
                act.wait_ge(*act_step.after("f_abs"))
                act.activation(f[:, 1, :], f[:, 1, :], ACT.Exp, scale=-1.0).then_inc(*act_step.done("f_exp"))
                act.wait_ge(*act_step.after("f_exp"))
                act.activation(f[:, 1, :], f[:, 1, :], ACT.Ln, bias=ones[0:4, 0:1]).then_inc(*act_step.done("f_ln"))
                rows_bank = lambda tag, tile, out, n: copy_bank((tag, tile), sums, out, n=n)
                for tile in (0, 2):
                    rows_bank("fv", tile, fox_v[:, tile, :], 256)
                for n in range(3):
                    copy_bank(("c", n), w_used, cq[:, n, :])
                for n in range(2):
                    copy_bank(("sq", n), w_used, qmix[:, 4 + n, :], scale=HD ** -0.5)
                for tile in (0, 2):
                    rows_bank("sv", tile, sb_v[:, tile, :], 256)
                for n in range(2):
                    copy_bank(("wq", n), w_used, qmix[:, 6 + n, :], scale=HD ** -0.5)
                act.wait_ge(*dve_step.after("cum"))
                act.wait_ge(*a_read.after(("c", 2)))
                for n in range(2):
                    square("lat_q", n, cq[:, n, :])
                root("lat_q", 1)
                for n in range(2):
                    act.wait_ge(*value.after(("lat", n)))
                    split_hi("lat", n, work[:, 2 + n, :], lat_hi)
                square("lat_kv", 0, cq[:, 2, :])
                root("lat_kv", 1)
                act.wait_ge(*value.after(("lat", 2)))
                split_hi("lat", 2, work[:, 2, :], lat_hi)
                for h in range(4):
                    copy_bank(("uk", h), sums, mla_k[0:HD, h, :], rows=slice(0, HD))
                for n, tiles in enumerate(UV_TILES):
                    k = len(tiles)
                    act.wait_ge(*(sums.after(("uv", n)) if n < 2 else w_used.after("ukv")))
                    act.activation(mla_v[:, tiles[0]:tiles[0] + k, :],
                                   a_bank(("uv", n))[:, 0:k * 256].rearrange("p (t c) -> p t c", t=k),
                                   ACT.Copy).then_inc(*a_read.done(("uv", n)))
                causal = lambda i: (i + 1) * P
                softmax("fox", causal, lambda i: i + 1)
                act.wait_ge(*sums.after(("fox", "out", 3)))
                softmax("mla", causal, lambda i: i + 1)
                act.wait_ge(*sums.after(("mla", "out", 3)))
                order = [(h, j) for h in range(4) for j in reversed(range(TT))]
                for n in range(len(order) + 1):
                    if n < len(order):
                        h, j = order[n]
                        key = ("stick", h, j)
                        w = S - j * P
                        b, tmp = bank_s[s_read.slot(key, 4)], probs[:, n % 3, 0:w]
                        act.wait_ge(*scores_ready.after(key))
                        act.activation(tmp, b[:, 0:w], ACT.Abs).then_inc(*act_step.done((*key, "abs")))
                        act.wait_ge(*act_step.after((*key, "abs")))
                        act.activation(tmp, tmp, ACT.Exp, scale=-1.0).then_inc(*act_step.done((*key, "exp")))
                        act.wait_ge(*act_step.after((*key, "exp")))
                        act.activation(tmp, tmp, ACT.Ln, bias=ones[:, 0:1]).then_inc(*act_step.done((*key, "ln")))
                    if n:
                        h, j = order[n - 1]
                        key = ("stick", h, j)
                        w = S - j * P
                        act.wait_ge(*sums.after(key))
                        if j == TT - 1 and h:
                            act.wait_ge(*sums.after(("stick", "out", h - 1)))
                        act.activation(probs_t[:, 0, j, j * P:S], bank_s[s_read.slot(key, 4)][:, 0:w], ACT.Exp
                                       ).then_inc(*s_read.done(key))
                act.wait_ge(*sums.after(("stick", "out", 3)))

                def sink(n):
                    h = heads[n][0]
                    act.activation(small[:, 80 + n:81 + n], par1[:, C1["sink"] + h:C1["sink"] + h + 1], ACT.Exp,
                                   bias=small[:, 32 + n:33 + n]).then_inc(*act_step.done(("sink", n)))

                softmax("swa", lambda i: min(i + 1, 2) * P, lambda i: min(i, 1) + 1, sink)
                rms("mixnorm", 4, 2, lambda c: qmix[:, c, :],
                    lambda c: act.wait_ge(*v_read.after(("swa", "out", 3))))
                norm_ln("ln1", ("ln1_g", "ln1_b"), True)
                ffn("ffn")
                norm_ln("ln2", ("ln2_g", "ln2_b"), False)

            with loop(act, "layer2", DEPTH) as l:
                act.dma_start(par2[:, :], t["par2"][l]).then_inc(*par_in.done("par2", 16))
                rms("rms1", 1, DC, lambda c: resid[:, c, :], lambda c: None)
                ffn("ffn1")
                rms("rms2", 1, DC, lambda c: resid[:, c, :], lambda c: act.wait_ge(*v_read.after(("ffn1", "down", c))))
                act.dma_start(lru_w[:, :, :], t["lru_w"][l]).then_inc(*par_in.done("lru_w", 16))
                act.dma_start(t5[:, :, :], t["t5_skewed"]).then_inc(*par_in.done("tables2", 16))
                for n in range(4):
                    copy_bank(("q2", n), w_used, mix2[:, n, :], scale=HD ** -0.5)
                for tile in (0, 2):
                    copy_bank(("v2", tile), sums, da_v[:, tile, :])
                for n in range(2):
                    copy_bank(("scc", n), w_used, sc_c[:, n, :])
                for n in range(2):
                    copy_bank(("scb", n), w_used, sc_b[:, n, :])
                for n in range(2):
                    copy_bank(("lg", n), w_used, lru_g[:, n, :], func=ACT.Gelu_apprx_tanh)
                lam = par2[:, C2["lam"]:C2["lam"] + 2]
                act.activation(small[:, 96:98], lam, ACT.Abs).then_inc(*act_step.done("lam_abs"))
                act.wait_ge(*act_step.after("lam_abs"))
                act.activation(small[:, 98:100], small[:, 96:98], ACT.Exp, scale=-1.0).then_inc(*act_step.done("lam_exp"))
                act.wait_ge(*sums.after("lam_sums"))
                act.activation(small[:, 66:68], stat_bank[:, 0:2], ACT.Exp).then_inc(*act_step.done("lam_sums"))
                act.wait_ge(*dve_step.after("s8"))
                for c in range(2):
                    for name, dest, column in (("r", gate_r, "ba"), ("i", gate_i, "bx")):
                        copy_bank(("gate", name, c), sums, dest[:, c, :], func=ACT.Sigmoid,
                                  bias=par2[:, C2[column] + c:C2[column] + c + 1])
                act.wait_ge(*a_read.after(("gate", "i", 1)))
                for c in range(2):
                    act.activation(lru_a[:, c, :], gate_r[:, c, :], ACT.Exp, scale=small[:, 104 + c:105 + c]
                                   ).then_inc(*act_step.done(("lru_a", c)))
                for c in range(2):
                    act.activation(gate_r[:, c, :], gate_r[:, c, :], ACT.Tanh, scale=small[:, 102 + c:103 + c]
                                   ).then_inc(*act_step.done(("tanh", c)))
                for c in range(2):
                    act.wait_ge(*dve_step.after(("mult2", c)))
                    act.activation(gate_r[:, c, :], gate_r[:, c, :], ACT.Sqrt).then_inc(*act_step.done(("mult", c)))
                for n in range(len(heads) + 2):
                    if n < len(heads):
                        h, i = heads[n]
                        for m in range(2):
                            exp_item(("diff", h, i, m), probs2[:, n % 3 * 2 + m, :], (i + 1) * P, 2 * (n % 8) + m)
                    if n >= 2:
                        keep_turned("diff", n - 2, probs2_t, heads[n - 2][1] + 1)
                rms("subln", 4, 1, lambda c: mix2[:, c, :], lambda c: act.wait_ge(*v_read.after(("diff", "out", c))))
                for c in range(4, DC):
                    act.wait_ge(*dve_step.after(("mix2", c)))
                    split_hi("subln", c, mix2[:, c, :])
                rms("rms3", 1, DC, lambda c: resid[:, c, :], lambda c: act.wait_ge(*v_read.after(("wout", c))))
                ffn("ffn2")
                act.wait_ge(*v_read.after(("ffn2", "down", DC - 1)))
            rms("final", 1, DC, lambda c: resid[:, c, :], lambda c: None, split=False)

        @block.vector
        def _(dve):
            def v_bank(key):
                return bank_v[v_read.slot(key, 2)]

            def step(ins, key):
                ins.then_inc(*dve_step.done(key))
                dve.wait_ge(*dve_step.after(key))

            def split_lo(tag, c, source, hi=xn_hi, lo=xn_lo):
                dve.wait_ge(*x_hi.after((tag, c)))
                dve.tensor_tensor(lo[:, c, :], source, hi[:, c, :].bitcast(F32), ALU.subtract
                                  ).then_inc(*x_lo.done((tag, c)))

            def diagonals(tag, groups, column):
                for g in range(groups):
                    for tile in range(TT):
                        j = g * TT + tile
                        ins = dve.tensor_scalar(diag[:, j, :], ident[:, :], small[:, column + j:column + j + 1],
                                                None, ALU.mult)
                    ins.then_inc(*diag_ready.done((tag, g)))

            def inverse_root(tag, groups, last, n, eps):
                dve.wait_ge(*sums.after((tag, "sum", last)))
                dve.tensor_scalar(small[:, 0:groups * TT], stat_bank[:, 0:groups * TT], 1.0 / n, eps,
                                  ALU.mult, ALU.add).then_inc(*dve_step.done((tag, "var")))
                dve.wait_ge(*rooted.after(tag))
                step(dve.reciprocal(small[:, 0:groups * TT], small[:, 16:16 + groups * TT]), (tag, "rstd"))
                diagonals(tag, groups, 0)

            def rms(tag, groups, per, source, par, column, n, eps, split=True, dest=None):
                inverse_root(tag, groups, groups * per - 1, n, eps)
                total = groups * per
                for c in range(total + 1):
                    if c < total:
                        g, last = c // per, c % per == per - 1
                        if c % per == 0:
                            dve.wait_ge(*sums.after((tag, "spread", g)))
                        if c >= 4 and split:
                            dve.wait_ge(*x_lo.after((tag, c - 4)))
                        out = dest(c) if dest else work[:, c % 4, :]
                        dve.scalar_tensor_tensor(out=out, in0=source(c), scalar=par(c), in1=bank_s[g][:, :],
                                                 op0=ALU.mult, op1=ALU.mult
                                                 ).then_inc(*(scaled if last or dest else value).done((tag, c)))
                    if c and split:
                        split_lo(tag, c - 1, work[:, (c - 1) % 4, :])

            def col(par, table, name, c=0):
                return par[:, table[name] + c:table[name] + c + 1]

            def norm_ln(tag, split):
                dve.wait_ge(*sums.after((tag, "mean", DC - 1)))
                step(dve.tensor_scalar(small[:, 0:TT], stat_bank[:, 0:TT], 1.0 / D, None, ALU.mult), (tag, "mean"))
                diagonals(tag + "_mean", 1, 0)
                dve.wait_ge(*sums.after((tag + "_mean", "spread", 0)))
                for c in range(DC):
                    dve.tensor_tensor(resid[:, c, :], resid[:, c, :], bank_s[0][:, :], ALU.subtract
                                      ).then_inc(*centered.done((tag, c)))
                inverse_root(tag, 1, DC - 1, D, 1e-5)
                dve.wait_ge(*sums.after((tag, "spread", 0)))
                for c in range(DC):
                    dve.tensor_tensor(resid[:, c, :], resid[:, c, :], bank_s[0][:, :], ALU.mult
                                      ).then_inc(*scaled.done((tag, c)))
                for c in range(DC if split else 0):
                    split_lo(tag, c, resid[:, c, :])

            def ffn(tag, first, second, swap):
                with loop(dve, tag, FC // 2) as i:
                    for k in range(2):
                        dve.wait_ge(*a_read.after((tag, "gate", k)))
                        dve.wait_ge(*w_used.after((tag, "up", k)))
                        dve.tensor_tensor(work[:, 2 + k, :], work[:, k, :], v_bank((tag, "up", k))[:, :], ALU.mult
                                          ).then_inc(*v_read.done((tag, "up", k)))
                        dve.wait_ge(*x_hi.after((tag, "h", k)))
                        at = bass.ds(i * 2 + k, 1)
                        dve.tensor_tensor(h_lo[:, at, :], work[:, 2 + k:3 + k, :], h_hi[:, at, :].bitcast(F32),
                                          ALU.subtract).then_inc(*x_lo.done((tag, "h", k)))
                for c in range(DC):
                    key = (tag, "down", c)
                    end = c * FC + FC - 1
                    dve.wait_ge(*(w_used.after((tag, "wd", end // 8)) if end % 8 == 7 else sums.after(key)))
                    b = v_bank(key)
                    if swap:
                        ins = dve.scalar_tensor_tensor(out=resid[:, c, :], in0=b[:, :], scalar=second,
                                                       in1=resid[:, c, :], op0=ALU.mult, op1=ALU.add)
                    else:
                        ins = dve.scalar_tensor_tensor(out=resid[:, c, :], in0=resid[:, c, :], scalar=first,
                                                       in1=b[:, :], op0=ALU.mult, op1=ALU.add)
                    ins.then_inc(*v_read.done(key))

            def keep(key, ready, out, rows=slice(0, P), n=S):
                dve.wait_ge(*ready.after(key))
                dve.tensor_copy(out, v_bank(key)[rows, 0:n]).then_inc(*v_read.done(key))

            heads = [(h, i) for h in range(4) for i in range(TT)]

            def half(n):
                return slice(n * HD, (n + 1) * HD)

            def softmax(tag, width, out, sink=False):
                for n in range(len(heads) + 4):
                    if n < len(heads):
                        h, i = heads[n]
                        key = (tag, h, i)
                        b = bank_s[s_read.slot(key, 4)]
                        dve.wait_ge(*scores_ready.after(key))
                        if sink:
                            step(dve.tensor_reduce(small[:, 48 + n:49 + n], b[:, 0:width(i)], AX.X, ALU.max), (*key, "max"))
                            dve.tensor_scalar(small[:, 32 + n:33 + n], small[:, 48 + n:49 + n],
                                              col(par1, C1, "sink", h), -1.0, ALU.max, ALU.mult
                                              ).then_inc(*row_max.done(key))
                        else:
                            dve.tensor_reduce(small[:, 32 + n:33 + n], b[:, 0:width(i)], AX.X, ALU.max, negate=True
                                              ).then_inc(*row_max.done(key))
                    if 1 <= n <= len(heads):
                        m = n - 1
                        h, i = heads[m]
                        key = (tag, h, i)
                        total = small[:, 64 + m:65 + m]
                        if sink:
                            dve.wait_ge(*act_step.after(("sink", m)))
                            step(dve.tensor_tensor(total, total, small[:, 80 + m:81 + m], ALU.add), (*key, "total"))
                        else:
                            dve.wait_ge(*s_read.after(key))
                        step(dve.reciprocal(small[:, 96 + m:97 + m], total), (*key, "inverse"))
                        dve.tensor_scalar(probs[:, m % 3, 0:width(i)], probs[:, m % 3, 0:width(i)],
                                          small[:, 96 + m:97 + m], None, ALU.mult).then_inc(*probs_ready.done(key))
                    if n >= 4 and heads[n - 4][1] == TT - 1:
                        h = heads[n - 4][0]
                        rows, dest = out(h)
                        keep((tag, "out", h), sums, dest, rows)

            dve.sem_inc(v_read.sem, 2)
            dve.wait_ge(*fills.after("neg_ones"))
            dve.wait_ge(*const_in.after("all"))
            dve.memset(rel_rows[BUCKETS:BUCKETS + 1, :, :], NEG)
            dve.tensor_tensor(rel[0:BUCKETS, :], rel[0:BUCKETS, :], rel_far[0:BUCKETS, :], ALU.subtract
                              ).then_inc(*dve_step.done("rel"))
            dve.wait_ge(*dve_step.after("rel"))
            dve.tensor_copy(rel_rows[0:BUCKETS, :, :], rel[0:BUCKETS, :].unsqueeze(2).to_broadcast([BUCKETS, 8, P])
                            ).then_inc(*dve_step.done("rel_rows"))

            with loop(dve, "layer1", DEPTH):
                for c in range(DC):
                    split_lo("in1", c, resid[:, c, :])
                dve.wait_ge(*par_in.after("tables1"))
                dve.wait_ge(*w_used.after("kr"))
                b = v_bank("kr")
                dve.tensor_scalar(work[0:4, 0, :], b[0:4, :], par1[0:4, C1["b_f"]:C1["b_f"] + 1], None, ALU.add
                                  ).then_inc(*dve_step.done("fz"))
                dve.tensor_tensor(work[64:96, 2, :], b[64:96, :], rope[64:96, 2, :], ALU.mult
                                  ).then_inc(*dve_step.done("kr_cos"))
                dve.tensor_tensor(work[64:96, 3, :], b[32:64, :], rope[32:64, 3, :], ALU.mult
                                  ).then_inc(*v_read.done("kr"))
                dve.wait_ge(*v_read.after("kr"))
                for h in range(4):
                    dve.tensor_tensor(mla_k[64:96, h, :], work[64:96, 2, :], work[64:96, 3, :], ALU.add
                                      ).then_inc(*dve_step.done(("kr", h)))
                for n in range(2):
                    keep(("fk", n), w_used, fox_k[:, n, :])
                dve.wait_ge(*act_step.after("f_ln"))
                step(dve.scalar_tensor_tensor(out=work[0:4, 2, :], in0=work[0:4, 0, :], scalar=0.0,
                                              in1=work[0:4, 1, :], op0=ALU.min, op1=ALU.subtract), "log_f")
                step(dve.memset(work[0:4, 0, :], 1.0), "log_ones")
                step(dve.tensor_tensor_scan(work[0:4, 3, :], work[0:4, 0, :], work[0:4, 2, :], 0.0,
                                            ALU.mult, ALU.add), "cum0")
                dve.tensor_copy(cum[0:4, :], work[0:4, 3, :]).then_inc(*dve_step.done("cum"))
                for tile in (1, 3):
                    dve.wait_ge(*(sums.after(("fv", 1)) if tile == 1 else w_used.after(("fv", "unit", 1))))
                    dve.tensor_copy(fox_v[:, tile, :], v_bank(("fv", tile))[:, 0:256]).then_inc(*v_read.done(("fv", tile)))
                for n in range(2):
                    keep(("sk", n), w_used, sb_k[:, n, :])
                for tile in (1, 3):
                    dve.wait_ge(*(sums.after(("sv", 1)) if tile == 1 else w_used.after(("sv", "unit", 1))))
                    dve.tensor_copy(sb_v[:, tile, :], v_bank(("sv", tile))[:, 0:256]).then_inc(*v_read.done(("sv", tile)))
                keep("wk", w_used, swa_k[:, :])
                dve.wait_ge(*w_used.after("wv"))
                dve.tensor_copy(swa_v[:, :, :], v_bank("wv")[:, :].rearrange("p (t c) -> p t c", t=TT)
                                ).then_inc(*v_read.done("wv"))
                step(dve.memset(aug_q[:, :, :], 0.0), "aug_q0")
                step(dve.memset(aug_k[:, :], 0.0), "aug_k0")
                step(dve.memset(aug_k[0:4, :], 1.0), "aug_k1")
                dve.tensor_scalar(aug_k[32:36, :], cum[0:4, :], -1.0, None, ALU.mult)
                for h in range(4):
                    dve.tensor_scalar(aug_q[0:4, h, :], cum[0:4, :], ident[0:4, h:h + 1], None, ALU.mult)
                    ins = dve.tensor_scalar(aug_q[32:36, h, :], aug_k[0:4, :], ident[0:4, h:h + 1], None, ALU.mult)
                ins.then_inc(*dve_step.done("aug"))
                inverse_root("lat_q", 1, 1, 256, 1e-6)
                dve.wait_ge(*sums.after(("lat_q", "spread", 0)))
                for n in range(2):
                    dve.scalar_tensor_tensor(out=work[:, 2 + n, :], in0=cq[:, n, :], scalar=col(par1, C1, "g_q", n),
                                             in1=bank_s[0][:, :], op0=ALU.mult, op1=ALU.mult
                                             ).then_inc(*value.done(("lat", n)))
                for n in range(2):
                    split_lo("lat", n, work[:, 2 + n, :], lat_hi, lat_lo)
                inverse_root("lat_kv", 1, 0, P, 1e-6)
                dve.wait_ge(*sums.after(("lat_kv", "spread", 0)))
                dve.scalar_tensor_tensor(out=work[:, 2, :], in0=cq[:, 2, :], scalar=col(par1, C1, "g_kv"),
                                         in1=bank_s[0][:, :], op0=ALU.mult, op1=ALU.mult
                                         ).then_inc(*value.done(("lat", 2)))
                split_lo("lat", 2, work[:, 2, :], lat_hi, lat_lo)
                for h in range(4):
                    key = ("uq", h)
                    dve.wait_ge(*sums.after(key))
                    b = v_bank(key)
                    dve.tensor_scalar(mla_q[0:HD, h, :], b[0:HD, :], 96.0 ** -0.5, None, ALU.mult
                                      ).then_inc(*dve_step.done(("q_plain", h)))
                    dve.tensor_tensor(mla_q[64:96, h, :], b[64:96, :], rope[64:96, 0, :], ALU.mult
                                      ).then_inc(*v_read.done(key))
                dve.wait_ge(*w_used.after("uq"))
                b = v_bank(("uq", 4))
                for h in range(4):
                    r = slice(h * ROPE, (h + 1) * ROPE)
                    ins = dve.tensor_tensor(work[64:96, h, :], b[r, :], rope[r, 1, :], ALU.mult)
                ins.then_inc(*v_read.done(("uq", 4)))
                dve.wait_ge(*v_read.after(("uq", 4)))
                for h in range(4):
                    dve.tensor_tensor(mla_q[64:96, h, :], mla_q[64:96, h, :], work[64:96, h, :], ALU.add
                                      ).then_inc(*dve_step.done(("mla_q", h)))

                causal = lambda i: (i + 1) * P
                softmax("fox", causal, lambda h: (half(h % 2), qmix[half(h % 2), h // 2, :]))
                softmax("mla", causal, lambda h: (half(h % 2), qmix[half(h % 2), 2 + h // 2, :]))
                order = [(h, j) for h in range(4) for j in reversed(range(TT))]
                for n in range(len(order) + 2):
                    if n < len(order):
                        h, j = order[n]
                        key = ("stick", h, j)
                        w = S - j * P
                        dve.wait_ge(*act_step.after((*key, "ln")))
                        if j == TT - 1 and h:
                            dve.wait_ge(*sums.after(("stick", h - 1, 0)))
                        dve.scalar_tensor_tensor(out=probs_t[:, 1, j, j * P:S], in0=bank_s[s_read.slot(key, 4)][:, 0:w],
                                                 scalar=0.0, in1=probs[:, n % 3, 0:w], op0=ALU.max, op1=ALU.add
                                                 ).then_inc(*softplus_ready.done(key))
                    if n >= 2 and order[n - 2][1] == 0:
                        h = order[n - 2][0]
                        keep(("stick", "out", h), sums, qmix[half(h % 2), 4 + h // 2, :], half(h % 2))
                softmax("swa", lambda i: min(i + 1, 2) * P, lambda h: (half(h // 2), qmix[half(h // 2), 6 + h % 2, :]),
                        sink=True)
                rms("mixnorm", 4, 2, lambda c: qmix[:, c, :], lambda c: col(par1, C1, "mix_g", c), None, 256, 1e-6)
                for c in range(DC):
                    dve.wait_ge(*w_used.after(("wo", c)))
                    dve.scalar_tensor_tensor(out=resid[:, c, :], in0=resid[:, c, :], scalar=ALPHA,
                                             in1=v_bank(("wo", c))[:, :], op0=ALU.mult, op1=ALU.add
                                             ).then_inc(*v_read.done(("wo", c)))
                norm_ln("ln1", True)
                ffn("ffn", ALPHA, 1.0, False)
                norm_ln("ln2", False)

            with loop(dve, "layer2", DEPTH):
                g = lambda name: (lambda c: col(par2, C2, name, c))
                chunk = lambda c: resid[:, c, :]
                dve.wait_ge(*par_in.after("par2"))
                rms("rms1", 1, DC, chunk, g("ffn1"), None, D, 1e-6)
                ffn("ffn1", 1.0, 0.5, True)
                rms("rms2", 1, DC, chunk, g("mix"), None, D, 1e-6)
                for n in range(4):
                    keep(("k2", n), w_used, da_k[:, n, :])
                for tile in (1, 3):
                    dve.wait_ge(*(sums.after(("v2", 1)) if tile == 1 else w_used.after(("v2", "unit", 3))))
                    dve.tensor_copy(da_v[:, tile, :], v_bank(("v2", tile))[:, :]).then_inc(*v_read.done(("v2", tile)))
                for n in range(2):
                    key = ("scx", n)
                    dve.wait_ge(*a_read.after(("scc", n)))
                    dve.wait_ge(*w_used.after(key))
                    dve.tensor_tensor(sc_x[:, n, :], sc_c[:, n, :], v_bank(key)[:, :], ALU.mult
                                      ).then_inc(*v_read.done(key))
                dve.wait_ge(*v_read.after(("scx", 1)))
                for c in range(2):
                    w = lambda k: par2[:, C2["sc_w"] + 2 * k + c:C2["sc_w"] + 2 * k + c + 1]
                    step(dve.tensor_scalar(sc_c[:, c, :], sc_x[:, c, :], w(2), None, ALU.mult), ("conv", c, 0))
                    for d in (1, 2):
                        step(dve.scalar_tensor_tensor(out=sc_c[:, c, d:S], in0=sc_x[:, c, 0:S - d], scalar=w(2 - d),
                                                      in1=sc_c[:, c, d:S], op0=ALU.mult, op1=ALU.add), ("conv", c, d))
                    dve.wait_ge(*a_read.after(("scb", c)))
                    dve.tensor_tensor(mix2[:, 4 + c, :], sc_c[:, c, :], sc_b[:, c, :], ALU.mult
                                      ).then_inc(*dve_step.done(("mix2", 4 + c)))
                for n in range(2):
                    keep(("lx", n), w_used, lru_x[:, n, :])
                dve.wait_ge(*v_read.after(("lx", 1)))
                for c in range(2):
                    w = lambda k: par2[:, C2["lru_w"] + 2 * k + c:C2["lru_w"] + 2 * k + c + 1]
                    step(dve.tensor_scalar(xr[:, c, :], lru_x[:, c, :], w(3), col(par2, C2, "lru_b", c),
                                           ALU.mult, ALU.add), ("lconv", c, 0))
                    for d in (1, 2, 3):
                        ins = dve.scalar_tensor_tensor(out=xr[:, c, d:S], in0=lru_x[:, c, 0:S - d], scalar=w(3 - d),
                                                       in1=xr[:, c, d:S], op0=ALU.mult, op1=ALU.add)
                        step(ins, ("lconv", c, d) if d < 3 else ("xr", c))
                for m, (q, k) in enumerate((("lq1", "lk1"), ("lq2", "lk2"))):
                    ins = dve.tensor_tensor(small[0:HD, 64 + m:65 + m], par2[0:HD, C2[q]:C2[q] + 1],
                                            par2[0:HD, C2[k]:C2[k] + 1], ALU.mult)
                ins.then_inc(*dve_step.done("lam_products"))
                dve.wait_ge(*act_step.after("lam_exp"))
                e, s, s2, p = (small[:, x:x + 2] for x in (98, 100, 106, 108))
                step(dve.tensor_scalar(s, e, 2.0, None, ALU.add), "sp0")
                step(dve.reciprocal(s, s), "sp1")
                step(dve.tensor_tensor(s, s, e, ALU.mult), "sp2")
                step(dve.tensor_tensor(s2, s, s, ALU.mult), "sp3")
                step(dve.tensor_scalar(p, s2, 1.0 / 13, None, ALU.mult), "sp4")
                for k in (11, 9, 7, 5, 3):
                    step(dve.scalar_tensor_tensor(out=p, in0=p, scalar=1.0 / k, in1=s2, op0=ALU.add, op1=ALU.mult), ("sp", k))
                step(dve.scalar_tensor_tensor(out=p, in0=p, scalar=1.0, in1=s, op0=ALU.add, op1=ALU.mult), "sp5")
                step(dve.tensor_scalar(s, par2[:, C2["lam"]:C2["lam"] + 2], -1.0, 0.0, ALU.mult, ALU.max), "sp6")
                step(dve.scalar_tensor_tensor(out=s, in0=p, scalar=2.0, in1=s, op0=ALU.mult, op1=ALU.add), "sp7")
                dve.tensor_scalar(small[:, 102:104], s, 8.0, None, ALU.mult)
                step(dve.tensor_scalar(small[:, 104:106], s, -8.0, None, ALU.mult), "s8")
                dve.wait_ge(*act_step.after("lam_sums"))
                step(dve.tensor_tensor(small[:, 68:69], small[:, 67:68], small[:, 66:67], ALU.subtract), "lam0")
                dve.tensor_scalar(small[:, 126:127], small[:, 68:69], par2[:, N2:N2 + 1], None, ALU.subtract
                                  ).then_inc(*dve_step.done("neg_lam"))
                step(dve.tensor_scalar(small[:, 127:128], col(par2, C2, "subln"), par2[:, N2 + 1:N2 + 2], None, ALU.mult),
                     "subln")
                for c in range(2):
                    dve.wait_ge(*act_step.after(("tanh", c)))
                    step(dve.tensor_scalar(lru_x[:, c, :], gate_r[:, c, :], 1.0, None, ALU.add), ("t1", c))
                    step(dve.reciprocal(lru_x[:, c, :], lru_x[:, c, :]), ("t2", c))
                    step(dve.scalar_tensor_tensor(out=gate_r[:, c, :], in0=gate_r[:, c, :], scalar=2.0,
                                                  in1=lru_x[:, c, :], op0=ALU.mult, op1=ALU.mult), ("mult2", c))
                for c in range(2):
                    step(dve.tensor_tensor(xr[:, c, :], xr[:, c, :], gate_i[:, c, :], ALU.mult), ("ix", c))
                    dve.wait_ge(*act_step.after(("mult", c)))
                    step(dve.tensor_tensor(xr[:, c, :], xr[:, c, :], gate_r[:, c, :], ALU.mult), ("b", c))
                    step(dve.tensor_tensor_scan(lru_x[:, c, :], lru_a[:, c, :], xr[:, c, :], 0.0, ALU.mult, ALU.add),
                         ("h", c))
                    dve.tensor_tensor(mix2[:, 6 + c, :], lru_x[:, c, :], lru_g[:, c, :], ALU.mult
                                      ).then_inc(*dve_step.done(("mix2", 6 + c)))
                for n in range(len(heads) + 4):
                    if n < len(heads):
                        h, i = heads[n]
                        for m in range(2):
                            key, k = ("diff", h, i, m), 32 + 2 * (n % 8) + m
                            dve.wait_ge(*scores_ready.after(key))
                            dve.tensor_reduce(small[:, k:k + 1], bank_s[s_read.slot(key, 4)][:, 0:(i + 1) * P],
                                              AX.X, ALU.max, negate=True).then_inc(*row_max.done(key))
                    if 1 <= n <= len(heads):
                        h, i = heads[n - 1]
                        w, k, slot = (i + 1) * P, 2 * ((n - 1) % 8), (n - 1) % 3 * 2
                        dve.wait_ge(*s_read.after(("diff", h, i, 1)))
                        step(dve.reciprocal(small[:, 96 + k:98 + k], small[:, 64 + k:66 + k]), ("inv", h, i))
                        step(dve.tensor_scalar(small[:, 97 + k:98 + k], small[:, 97 + k:98 + k], small[:, 126:127],
                                               None, ALU.mult), ("weight", h, i))
                        step(dve.tensor_scalar(probs2[:, slot, 0:w], probs2[:, slot, 0:w], small[:, 96 + k:97 + k],
                                               None, ALU.mult), ("p0", h, i))
                        dve.scalar_tensor_tensor(out=probs2[:, slot, 0:w], in0=probs2[:, slot + 1, 0:w],
                                                 scalar=small[:, 97 + k:98 + k], in1=probs2[:, slot, 0:w],
                                                 op0=ALU.mult, op1=ALU.add).then_inc(*probs_ready.done(("diff", h, i)))
                    if n >= 4 and heads[n - 4][1] == TT - 1:
                        h = heads[n - 4][0]
                        keep(("diff", "out", h), sums, mix2[:, h, :])
                rms("subln", 4, 1, lambda c: mix2[:, c, :], lambda c: small[:, 127:128], None, P, 1e-5)
                for c in range(4, DC):
                    split_lo("subln", c, mix2[:, c, :])
                for c in range(DC):
                    dve.wait_ge(*w_used.after(("wout", c)))
                    dve.tensor_tensor(resid[:, c, :], resid[:, c, :], v_bank(("wout", c))[:, :], ALU.add
                                      ).then_inc(*v_read.done(("wout", c)))
                rms("rms3", 1, DC, chunk, g("ffn2"), None, D, 1e-6)
                ffn("ffn2", 1.0, 0.5, True)
            rms("final", 1, DC, chunk, g("final"), None, D, 1e-6, split=False, dest=chunk)
    return counts.found


def _cols_unit(w):
    return w.reshape(DC, P, P).transpose(1, 0, 2).reshape(P, UNIT)


def _proj_units(w):
    return [_cols_unit(w[:, c:c + P]) for c in range(0, w.shape[1], P)]


def _row_units(w):
    per = UNIT // w.shape[1]
    return [w[n * per * P:(n + 1) * per * P].reshape(per, P, -1).transpose(1, 0, 2).reshape(P, UNIT)
            for n in range(DC // per)]


def _ffn_units(gate, up, down):
    out = []
    for g, u in zip(_proj_units(gate), _proj_units(up)):
        out += [g, u]
    tiles = down.reshape(FC, P, DC, P).transpose(1, 2, 0, 3).reshape(P, FC, UNIT)
    return out + [tiles[:, n] for n in range(FC)]


def _columns(v):
    return v.reshape(-1, P).T


def _units(a):
    half_of = (np.arange(ROPE) + ROPE // 2) % ROPE
    pairs = [0, 2, 1, 3]
    out = []
    for l in range(DEPTH):
        w = a["w_in"][l]
        cut = dict(zip("fq fk fv fg cq ckv kr sq sk sv wq wk wv".split(), np.split(
            w, np.cumsum([256, 256, 256, 4, 256, 128, 32, 256, 256, 256, 256, 128]), axis=1)))
        first = np.zeros((D, P), np.float32)
        first[:, 0:4] = cut["fg"]
        first[:, 32:64] = cut["kr"][:, half_of]
        first[:, 64:96] = cut["kr"]
        wq = cut["wq"].reshape(D, 4, HD)[:, pairs].reshape(D, 256)
        out.append(_cols_unit(first))
        for name in ("fq", "fk"):
            out += _proj_units(cut[name])
        out += _row_units(cut["fv"]) + _proj_units(np.concatenate([cut["cq"], cut["ckv"]], 1))
        out += _proj_units(cut["sq"]) + _proj_units(cut["sk"]) + _row_units(cut["sv"])
        out += _proj_units(wq) + _proj_units(cut["wk"]) + _row_units(cut["wv"])
        uq = a["mla_w_uq"][l]
        turned = uq.reshape(256, 4, 96)[:, :, 64:][:, :, half_of].reshape(256, P)
        out.append(np.concatenate([uq, turned], 1).reshape(2, P, S).transpose(1, 0, 2).reshape(P, UNIT))
        ukv = np.zeros((P, UNIT), np.float32)
        ukv[:, 0:512] = a["mla_w_ukv"][l].reshape(P, 4, 2, HD).transpose(0, 2, 1, 3).reshape(P, 512)
        out.append(ukv)
        wo = a["w_o"][l].copy()
        wo[768:] = wo[768:].reshape(4, HD, D)[pairs].reshape(256, D)
        out += _proj_units(wo) + _ffn_units(a["w_gate"][l], a["w_up"][l], a["w_down"][l])
    for l in range(DEPTH):
        q, k, v, b, c, x, lx, lg = np.split(a["w_in_2"][l], [512, 1024, 1536, 1792, 2048, 2304, 2560], axis=1)
        out += _ffn_units(a["ffn1_gate_2"][l], a["ffn1_up_2"][l], a["ffn1_down_2"][l])
        out += _proj_units(q) + _proj_units(k) + _row_units(v)
        for w in (c, x, b, lx, lg):
            out += _proj_units(w)
        out += [np.zeros((P, UNIT), np.float32)] * 2
        out += _proj_units(a["w_out_2"][l])
        out += _ffn_units(a["ffn2_gate_2"][l], a["ffn2_up_2"][l], a["ffn2_down_2"][l])
    assert len(out) == UNITS
    return np.stack(out).reshape(UNITS // SLOTS, SLOTS, P, UNIT)


def _parameters(a):
    pairs = [0, 2, 1, 3]
    par1 = np.zeros((DEPTH, P, N1), np.float32)
    par2 = np.zeros((DEPTH, P, N2 + 2), np.float32)
    lru_w = np.zeros((DEPTH, P, 4, P), np.float32)
    for l in range(DEPTH):
        def put(par, at, v):
            v = _columns(v)
            par[l, :, at:at + v.shape[1]] = v

        mix_g = a["mix_g"][l].copy()
        mix_g[768:] = mix_g[768:].reshape(4, HD)[pairs].reshape(256)
        put(par1, C1["mix_g"], mix_g)
        for name in ("ln1_g", "ln1_b", "ln2_g", "ln2_b"):
            put(par1, C1[name], a[name][l])
        put(par1, C1["g_q"], a["mla_g_q"][l])
        put(par1, C1["g_kv"], a["mla_g_kv"][l])
        par1[l, 0:4, C1["b_f"]] = a["fox_b_f"][l]
        par1[l, :, C1["sink"]:C1["sink"] + 4] = a["swa_sinks"][l]
        for name, source in (("ffn1", "ffn1_norm_2"), ("mix", "mix_norm_2"), ("ffn2", "ffn2_norm_2"),
                             ("lru_b", "lru_conv_b_2"), ("lam", "lru_lambda_2"), ("subln", "subln_gain_2")):
            put(par2, C2[name], a[source][l])
        put(par2, C2["ba"], a["lru_ba_2"][l].reshape(-1))
        put(par2, C2["bx"], a["lru_bx_2"][l].reshape(-1))
        put(par2, C2["sc_w"], a["sc_conv_w_2"][l].reshape(-1))
        put(par2, C2["lru_w"], a["lru_conv_w_2"][l].reshape(-1))
        put(par2, C2["final"], a["final_norm_2"])
        for name in ("q1", "k1", "q2", "k2"):
            par2[l, 0:HD, C2["l" + name]] = a[f"lam_{name}_2"][l]
        lam_init = 0.8 - 0.6 * math.exp(-0.3 * l)
        par2[l, :, N2] = lam_init
        par2[l, :, N2 + 1] = 1.0 - lam_init
        for m, name in enumerate(("lru_wa_2", "lru_wx_2")):
            for n in range(4):
                r = slice(n % 2 * HD, (n % 2 + 1) * HD)
                lru_w[l, r, 2 * m + n // 2, r] = a[name][l, n]
    return par1, par2, lru_w


def _tables():
    at = np.arange(P)
    f32 = np.float32
    causal = np.where(at[None, :] <= at[:, None], 0.0, NEG).astype(f32)
    strict_t = np.where(at[:, None] < at[None, :], 0.0, NEG).astype(f32)
    neg_tri = np.where(at[:, None] >= at[None, :], -1.0, 0.0).astype(f32)
    inv = (f32(10000.0) ** (-np.arange(0, ROPE, 2, dtype=f32) / f32(ROPE))).astype(f32)
    angle = np.arange(S, dtype=f32)[:, None] * inv[None, :]
    cos, sin = np.cos(angle).astype(f32).T, np.sin(angle).astype(f32).T
    cos, sin = np.tile(cos, (8, 1)), np.tile(np.concatenate([-sin, sin]), (4, 1))
    scale = f32(96.0 ** -0.5)
    rope = np.stack([cos * scale, sin * scale, cos, sin], axis=1).astype(f32)
    dist = at[:, None] + P - np.arange(2 * P)[None, :]
    slopes = np.exp2(-8.0 * np.arange(1, 5, dtype=f32) / 4)
    alibi = np.stack([np.where((dist >= 0) & (dist < P), -s * dist, NEG) for s in slopes], axis=1).astype(f32)
    d = 2 * P - 1 - np.arange(T5W)
    n = np.maximum(d, 1).astype(f32)
    large = 16 + (np.log(n / f32(16)) / f32(math.log(8.0)) * f32(16)).astype(np.int32)
    bucket = np.where(d < 16, np.maximum(d, 0), np.minimum(large, BUCKETS - 1))
    bucket_of = np.zeros((BUCKETS + 1, T5W), f32)
    bucket_of[bucket[d >= 0], np.nonzero(d >= 0)[0]] = 1.0
    bucket_of[BUCKETS, d < 0] = 1.0
    return dict(ident=np.eye(P, dtype=f32), mask=causal, mask_t=strict_t, neg_tri=neg_tri,
                bucket_of=bucket_of, rope=np.ascontiguousarray(rope), alibi=np.ascontiguousarray(alibi))


def arrays(inputs):
    a = {k: np.asarray(v) for k, v in inputs.items()}
    par1, par2, lru_w = _parameters(a)
    return dict(_tables(), w_stream=_units(a), par1=par1, par2=par2, lru_w=lru_w,
                x=np.ascontiguousarray(a["x"][0].T.reshape(DC, P, S).transpose(1, 0, 2)),
                rel=a["rel_bias_2"], rel_far=np.tile(a["rel_bias_2"][BUCKETS - 1:], (BUCKETS, 1)))


def program(nc, ins):
    t = {name: nc.dram_tensor(f"in_{name}", a.shape, F32, kind="ExternalInput").ap() for name, a in ins.items()}
    t["out"] = nc.dram_tensor("out_0", (P, DC, S), F32, kind="ExternalOutput").ap()
    rows = nc.dram_tensor("t5_rows", (8, P, T5W), F32, kind="Internal")
    t["t5_rows"] = rows.ap()
    t["t5_skewed"] = bass.AP(rows, P - 1, [[T5W - 1, P], [P * T5W, 8], [1, 2 * P]])
    return t


def kernel(**inputs):
    from concourse import bacc
    from concourse.bass_utils import run_bass_kernel_spmd

    ins = arrays(inputs)

    def fresh():
        return bacc.Bacc("TRN2", target_bir_lowering=False, num_devices=1)

    draft = fresh()
    counted = build(draft, program(draft, ins), None)
    nc = fresh()
    build(nc, program(nc, ins), counted)
    r = run_bass_kernel_spmd(nc, [{f"in_{name}": a for name, a in ins.items()}], core_ids=[0])
    y = r.results[0]["out_0"]
    return y.transpose(2, 1, 0).reshape(1, S, D)
```

```python
from contextlib import ExitStack, contextmanager
import math

import numpy as np
import concourse.bass as bass
from concourse import mybir

F32 = mybir.dt.float32
F32R = mybir.dt.float32r
ALU = mybir.AluOpType
ACT = mybir.ActivationFunctionType
AX = mybir.AxisListType

P = 128
D = 1024
S = 512
DEPTH = 2
HD = 64
DC = D // P
TT = S // P
FF = 2816
FC = FF // P
NEG = -1e30
ALPHA = (2.0 * DEPTH) ** 0.25
ROPE = 32
BUCKETS = 32
SLOTS = 4
UNIT = 8 * P
FFN_UNITS = 3 * FC
B1_PROJ = 22
B1_UNITS = B1_PROJ + DC + FFN_UNITS
B2_PROJ = 24
B2_UNITS = 2 * FFN_UNITS + B2_PROJ + DC
UNITS = DEPTH * (B1_UNITS + B2_UNITS)

C1 = dict(mix_g=0, ln1_g=8, ln1_b=16, ln2_g=24, ln2_b=32, g_q=40, g_kv=42, b_f=43, sink=44)
N1 = 48
C2 = dict(ffn1=0, mix=8, ffn2=16, sc_w=24, lru_w=30, lru_b=38, ba=40, bx=42, lam=44, subln=46,
          final=47, lq1=55, lk1=56, lq2=57, lk2=58)
N2 = 59
UV_TILES = ((0, 1), (2,), (3,))
T5W = 3 * P


class Counts:

    def __init__(self, known):
        self.known = known or {}
        self.found = {}
        self.loops = []

    @contextmanager
    def loop(self, engine, name, rounds):
        with engine.Fori(0, rounds) as i:
            self.loops.append((name, rounds, i))
            for s in self.signals:
                s.enter()
            yield i
            for s in self.signals:
                s.leave(name, rounds)
            self.loops.pop()


class Signal:

    def __init__(self, counts, sem, name, credit=0):
        self.counts, self.sem, self.name, self.credit = counts, sem, name, credit
        self.total, self.base, self.open, self.events = credit, [], [[]], {}

    def enter(self):
        self.base.append(self.total)
        self.open.append([])

    def leave(self, name, rounds):
        start = self.base.pop()
        each = self.total - start
        mine = self.open.pop()
        for key in mine:
            self.events[key][1][name] = (each, rounds)
        self.open[-1] += mine
        self.total = start + each * rounds
        self.counts.found[self.name] = self.events

    def done(self, key, n=1):
        assert key not in self.events, (self.name, key)
        self.total += n
        self.events[key] = [self.total, {}]
        self.open[-1].append(key)
        self.counts.found[self.name] = self.events
        return self.sem, n

    def number(self, key):
        known = self.counts.known
        if not known:
            return 1
        value, loops = known[self.name][key]
        here = {name: i for name, _, i in self.counts.loops}
        for name, (each, rounds) in loops.items():
            value = value + (here[name] * each if name in here else (rounds - 1) * each)
        return value

    def after(self, key):
        return self.sem, self.number(key)

    def before(self, key):
        return self.sem, self.number(key) - self.credit

    def carried(self, first, again):
        known = self.counts.known
        if not known:
            return self.sem, 1
        (start, _), (later, loops) = known[self.name][first], known[self.name][again]
        name, _, i = self.counts.loops[-1]
        each = loops[name][0]
        assert later == start + each, (self.name, first, again)
        return self.sem, start + i * each

    def slot(self, key, depth):
        if not self.counts.known:
            return 0
        value, loops = self.counts.known[self.name][key]
        assert all(each % depth == 0 for each, _ in loops.values()), (self.name, key, loops)
        return (value - self.credit - 1) % depth


def build(nc, t, known):
    counts = Counts(known)
    loop = counts.loop
    with ExitStack() as ctx:
        def sb(name, shape, dt=F32):
            return ctx.enter_context(nc.sbuf_tensor(name, shape, dt))

        def overlay(*entries):
            with ExitStack() as scope:
                return [scope.enter_context(nc.sbuf_tensor(*entry)) for entry in entries]

        counts.signals = []

        def signal(name, credit=0):
            s = Signal(counts, ctx.enter_context(nc.semaphore(name)), name, credit)
            counts.signals.append(s)
            return s

        resid = sb("resid", [P, DC, S])
        raw = sb("raw", [P, SLOTS, UNIT])
        w_hi = sb("w_hi", [P, SLOTS, UNIT], F32R)
        w_lo = sb("w_lo", [P, SLOTS, UNIT], F32R)
        ident = sb("ident", [P, P])
        ident_r = sb("ident_r", [P, P], F32R)
        mask_r = sb("mask_r", [P, P], F32R)
        strict_r = sb("strict_r", [P, P], F32R)
        ones = sb("ones", [P, P])
        zero = sb("zero", [P, 1])
        par1 = sb("par1", [P, N1])
        par2 = sb("par2", [P, N2 + 2])
        small = sb("small", [P, 128])
        cum = sb("cum", [4, S])
        scale_by = sb("scale_by", [P, S])
        diag = sb("diag", [P, 4 * TT, P])
        work = sb("work", [P, 4, S])
        xn_hi, xn_lo = overlay(("xn_hi", [P, DC, S], F32R), ("xn_lo", [P, DC, S], F32R))
        probs_t, probs, aug_q, aug_k = overlay(
            ("probs_t", [P, 2, TT, S], F32), ("probs", [P, 3, S], F32),
            ("aug_q", [P, 4, S], F32R), ("aug_k", [P, S], F32R))
        probs2_t, probs2 = overlay(("probs2_t", [P, 2, TT, S], F32), ("probs2", [P, 6, S], F32))
        sb("place_of_xn", [P, 2 * DC * S])
        h_hi, h_lo = overlay(("h_hi", [P, FC, S], F32R), ("h_lo", [P, FC, S], F32R))
        (qmix, fox_k, fox_v, sb_k, sb_v, swa_k, swa_v, cq, mla_q, mla_k, mla_v, rope, alibi,
         lat_hi, lat_lo) = overlay(
            ("qmix", [P, DC, S], F32), ("fox_k", [P, 2, S], F32), ("fox_v", [P, TT, 256], F32),
            ("sb_k", [P, 2, S], F32), ("sb_v", [P, TT, 256], F32), ("swa_k", [P, S], F32),
            ("swa_v", [P, TT, P], F32), ("cq", [P, 3, S], F32),
            ("mla_q", [P, 4, S], F32), ("mla_k", [P, 4, S], F32), ("mla_v", [P, TT, 256], F32),
            ("rope", [P, 4, S], F32), ("alibi", [P, 4, 256], F32R),
            ("lat_hi", [P, 3, S], F32R), ("lat_lo", [P, 3, S], F32R))
        (mix2, da_k, da_v, sc_c, sc_x, sc_b, lru_x, lru_g, xr, gate_r, gate_i, lru_a, lru_w, t5) = overlay(
            ("mix2", [P, DC, S], F32), ("da_k", [P, 4, S], F32), ("da_v", [P, TT, S], F32),
            ("sc_c", [P, 2, S], F32), ("sc_x", [P, 2, S], F32), ("sc_b", [P, 2, S], F32),
            ("lru_x", [P, 2, S], F32), ("lru_g", [P, 2, S], F32), ("xr", [P, 2, S], F32),
            ("gate_r", [P, 2, S], F32), ("gate_i", [P, 2, S], F32), ("lru_a", [P, 2, S], F32),
            ("lru_w", [P, 4, P], F32), ("t5", [P, 8, 256], F32))
        _, mix_hi, mix_lo = overlay(("mix2_again", [P, DC, S], F32), ("mix_hi", [P, DC, S], F32R),
                                    ("mix_lo", [P, DC, S], F32R))
        bucket_of, rel, rel_far, rel_rows, t5_row = overlay(
            ("bucket_of", [P, T5W], F32), ("rel", [P, 8], F32), ("rel_far", [P, 8], F32),
            ("rel_rows", [P, 8, P], F32), ("t5_row", [P, 8, T5W], F32))
        sb("place_of_h", [P, 2 * FC * S])


        bank_a = [ctx.enter_context(nc.psum_tensor(f"bank_a{i}", [P, S], F32)) for i in range(2)]
        bank_v = [ctx.enter_context(nc.psum_tensor(f"bank_v{i}", [P, S], F32)) for i in range(2)]
        bank_s = [ctx.enter_context(nc.psum_tensor(f"bank_s{i}", [P, S], F32)) for i in range(4)]
        stat_bank = bank_s[3]
        t5_dram = t["t5_rows"]

        def as_r(ap):
            return ap.bitcast(F32R)


        raw_in = [signal(f"raw_in{u}") for u in range(SLOTS)]
        const_in = signal("const_in")
        rel_in = signal("rel_in")
        x_in = [signal(f"x_in{c}") for c in range(DC)]
        par_in = signal("par_in")
        t5_out = signal("t5_out")
        out_done = signal("out_done")
        fills = signal("fills")
        hi_split = signal("hi_split")
        w_split = signal("w_split", SLOTS)
        w_used = signal("w_used", SLOTS)
        sums = signal("sums")
        scores_ready = signal("scores_ready")
        turned = signal("turned")
        a_read = signal("a_read", 2)
        s_read = signal("s_read", 4)
        x_hi = signal("x_hi")
        squared = signal("squared")
        rooted = signal("rooted")
        affine = signal("affine")
        gated = signal("gated")
        act_step = signal("act_step")
        v_read = signal("v_read", 2)
        x_lo = signal("x_lo")
        value = signal("value")
        centered = signal("centered")
        scaled = signal("scaled")
        diag_ready = signal("diag_ready")
        row_max = signal("row_max")
        probs_ready = signal("probs_ready")
        product = signal("product")
        dve_step = signal("dve_step")

        block = ctx.enter_context(nc.Block())

        @block.sync
        def _(sp):
            for c in range(0, DC, 2):
                sp.dma_start(resid[:, c, :], t["x"][:, c, :]).then_inc(*x_in[c].done("x", 16))
            with loop(sp, "stream", UNITS // SLOTS) as i:
                for u in range(SLOTS):
                    sp.wait_ge(*w_split.before(("unit", u)))
                    sp.dma_start(raw[:, u, :], t["w_stream"][i, u]
                                 ).then_inc(*raw_in[u].done("unit", 16))
            for c in range(0, DC, 2):
                sp.wait_ge(*scaled.after(("final", c + 1)))
                sp.dma_start(t["out"][:, c:c + 2, :], resid[:, c:c + 2, :]).then_inc(*out_done.done(("out", c), 16))
            sp.wait_ge(*out_done.after(("out", DC - 2)))

        @block.gpsimd
        def _(pool):
            pool.sem_inc(w_split.sem, SLOTS)
            pool.memset(zero[:, :], 0.0).then_inc(*fills.done("zero"))
            pool.memset(ones[:, :], 1.0).then_inc(*fills.done("ones"))
            pool.wait_ge(*fills.after("ones"))
            with loop(pool, "stream", UNITS // SLOTS):
                for u in range(SLOTS):
                    pool.wait_ge(*raw_in[u].after("unit"))
                    pool.wait_ge(w_used.sem, w_split.before(("unit", u))[1])
                    pool.tensor_tensor(w_hi[:, u, :], raw[:, u, :], zero[:, 0:1].to_broadcast([P, UNIT]),
                                       ALU.add).then_inc(*hi_split.done(("unit", u)))
                    pool.wait_ge(*hi_split.after(("unit", u)))
                    pool.tensor_tensor(w_lo[:, u, :], raw[:, u, :], w_hi[:, u, :].bitcast(F32),
                                       ALU.subtract).then_inc(*w_split.done(("unit", u)))

        @block.tensor
        def _(pe):
            def a_bank(key):
                pe.wait_ge(*a_read.before(key))
                return bank_a[a_read.slot(key, 2)]

            def v_bank(key):
                pe.wait_ge(*v_read.before(key))
                return bank_v[v_read.slot(key, 2)]

            def s_bank(key):
                pe.wait_ge(*s_read.before(key))
                return bank_s[s_read.slot(key, 4)]

            def unit(key):
                pe.wait_ge(w_split.sem, w_used.number(key))
                return w_used.slot(key, SLOTS)

            def mm3(out, lhs_hi, lhs_lo, rhs_hi, rhs_lo, first, last):
                pe.matmul(out, lhs_hi, rhs_hi, start=first, stop=False)
                pe.matmul(out, lhs_hi, rhs_lo, start=False, stop=False)
                return pe.matmul(out, lhs_lo, rhs_hi, start=False, stop=last)

            def w_tile(u, k, n=P):
                return w_hi[:, u, k * n:(k + 1) * n], w_lo[:, u, k * n:(k + 1) * n]

            def project(key, bank, wait=None, hi=xn_hi, lo=xn_lo):
                u = unit(key)
                b = bank(key)
                for c in range(DC):
                    if wait:
                        pe.wait_ge(*wait(c))
                    mm = mm3(b[:, :], *w_tile(u, c), hi[:, c, :], lo[:, c, :], c == 0, c == DC - 1)
                mm.then_inc(*w_used.done(key))

            def is_split(tag):
                return lambda c: x_lo.after((tag, c))

            def project_rows(tag, n_units, cols):
                per = DC // n_units
                banks = [a_bank((tag, 0)), v_bank((tag, 1)), a_bank((tag, 2)), v_bank((tag, 3))]
                for n in range(n_units):
                    u = unit((tag, "unit", n))
                    for tile in range(TT):
                        cut = slice(tile * P, (tile + 1) * P)
                        for k in range(per):
                            c = n * per + k
                            mm = mm3(banks[tile][:, 0:cols], xn_hi[:, c, cut], xn_lo[:, c, cut],
                                     *w_tile(u, k, cols), c == 0, c == DC - 1)
                        if n == n_units - 1 and tile < TT - 1:
                            mm.then_inc(*sums.done((tag, tile)))
                    mm.then_inc(*w_used.done((tag, "unit", n)))

            def token_sums(key, tiles, n, first, last):
                for tile in range(TT):
                    mm = pe.matmul(stat_bank[:, n + tile:n + tile + 1], tiles(slice(tile * P, (tile + 1) * P)),
                                   ones[:, 0:1], start=first and tile == 0, stop=True,
                                   skip_group_check=True)
                mm.then_inc(*sums.done(key))

            def spread(tag, groups=1):
                for g in range(groups):
                    pe.wait_ge(*diag_ready.after((tag, g)))
                    for tile in range(TT):
                        mm = pe.matmul(bank_s[g][:, tile * P:(tile + 1) * P], ones[:, :],
                                       diag[:, g * TT + tile, :], start=True, stop=True)
                    mm.then_inc(*sums.done((tag, "spread", g)))

            def square_sums(tag, c, per, n, wait=None):
                pe.wait_ge(*(wait or squared.after((tag, c))))
                token_sums((tag, "sum", c), lambda cut: work[:, c % 4, cut], c // per * TT, c == 0, c == n - 1)

            def rms(tag, groups, per):
                n = groups * per
                for c in range(n):
                    square_sums(tag, c, per, n)
                spread(tag, groups)

            def mean_chunk(tag, c):
                pe.matmul(bank_s[0][:, :], ones[:, :], resid[:, c, :], start=c == 0, stop=True,
                          skip_group_check=True).then_inc(*sums.done((tag, "mean", c)))

            def variance(tag):
                for c in range(DC):
                    square_sums(tag, c, DC, DC)
                spread(tag)

            def down(tag, after_chunk=None):
                for c in range(DC):
                    key = (tag, "down", c)
                    b = v_bank(key)
                    for f in range(FC):
                        i = c * FC + f
                        if i % 8 == 0:
                            u = unit((tag, "wd", i // 8))
                        if c == 0:
                            pe.wait_ge(*x_lo.after((tag, "h", f % 2)))
                        mm = mm3(b[:, :], *w_tile(u, i % 8), h_hi[:, f, :], h_lo[:, f, :], f == 0, f == FC - 1)
                        if i % 8 == 7:
                            mm.then_inc(*w_used.done((tag, "wd", i // 8)))
                        elif f == FC - 1:
                            mm.then_inc(*sums.done(key))
                    if after_chunk and c:
                        pe.wait_ge(*v_read.after((tag, "down", c - 1)))
                        after_chunk(c - 1)
                if after_chunk:
                    pe.wait_ge(*v_read.after((tag, "down", DC - 1)))
                    after_chunk(DC - 1)

            def ffn(tag, split, after_chunk=None, stats=None):
                for k in range(2):
                    project((tag, "gate0", k), a_bank, None if k else split)
                    if stats and k == 0:
                        square_sums(stats[0], DC - 1, DC, DC, stats[1])
                    project((tag, "up0", k), v_bank)
                    if stats and k == 0:
                        spread(stats[0])
                with loop(pe, tag, FC // 2 - 1):
                    for k in range(2):
                        project((tag, "gate", k), a_bank)
                        project((tag, "up", k), v_bank)
                down(tag, after_chunk)

            def turn(key, source, n):
                pe.wait_ge(*probs_ready.after(key))
                b = a_bank(key)
                for j in range(n):
                    mm = pe.transpose(b[:, j * P:(j + 1) * P], source[:, j * P:(j + 1) * P], ident[:, :])
                mm.then_inc(*turned.done(key))

            def attend(items, scores, turn_item, finish):
                for n in range(len(items) + 3):
                    if n < len(items):
                        scores(items[n])
                    if 2 <= n < len(items) + 2:
                        turn_item(n - 2)
                    if n >= 3 and items[n - 3][1] == TT - 1:
                        finish(items[n - 3][0])

            heads = [(h, i) for h in range(4) for i in range(TT)]

            def values(tag, h, v, pt, rows, banded=False):
                pe.wait_ge(*a_read.after((tag, h, TT - 1)))
                b = v_bank((tag, "out", h))
                for j in range(TT):
                    end = min((j + 2) * P, S) if banded else S
                    mm = pe.matmul(b[rows, j * P:end], v(j, h), pt[:, h % 2, j, j * P:end],
                                   start=(j == 0), stop=True, skip_group_check=True)
                mm.then_inc(*sums.done((tag, "out", h)))

            def half(n):
                return slice(n * HD, (n + 1) * HD)

            def fox():
                def scores(item):
                    h, i = item
                    key = ("fox", h, i)
                    n, cut, r, c = (i + 1) * P, slice(i * P, (i + 1) * P), half(h % 2), h // 2
                    b = s_bank(key)
                    pe.matmul(b[:, 0:n], qmix[r, c, cut], fox_k[r, c, 0:n], start=True, stop=True)
                    pe.matmul(b[:, 0:n], aug_q[:, h, cut], aug_k[:, 0:n], start=False, stop=True, skip_group_check=True)
                    pe.matmul(b[:, i * P:n], ident_r[:, :], mask_r[:, :], start=False, stop=True,
                              skip_group_check=True).then_inc(*scores_ready.done(key))

                pe.wait_ge(*act_step.after("aug"))
                pe.wait_ge(*dve_step.after("aug"))
                attend(heads, scores, lambda n: turn(("fox", *heads[n]), probs[:, n % 3, :], heads[n][1] + 1),
                       lambda h: values("fox", h, lambda j, h: fox_v[:, j, half(h)], probs_t, half(h % 2)))

            def mla():
                def scores(item):
                    h, i = item
                    key = ("mla", h, i)
                    n, cut = (i + 1) * P, slice(i * P, (i + 1) * P)
                    b = s_bank(key)
                    pe.matmul(b[:, 0:n], mla_q[0:96, h, cut], mla_k[0:96, h, 0:n], start=True, stop=True)
                    pe.matmul(b[:, i * P:n], ident_r[:, :], mask_r[:, :], start=False, stop=True,
                              skip_group_check=True).then_inc(*scores_ready.done(key))

                attend(heads, scores, lambda n: turn(("mla", *heads[n]), probs[:, n % 3, :], heads[n][1] + 1),
                       lambda h: values("mla", h, lambda j, h: mla_v[:, j, half(h)], probs_t, half(h % 2)))

            def swa():
                def scores(item):
                    h, i = item
                    key = ("swa", h, i)
                    lo, n, cut, r = max(i - 1, 0) * P, (i + 1) * P, slice(i * P, (i + 1) * P), half(h // 2)
                    b = s_bank(key)
                    pe.matmul(b[:, n - lo:n - lo + 1], ones[0:1, :], par1[0:1, C1["sink"] + h:C1["sink"] + h + 1],
                              start=True, stop=True)
                    pe.matmul(b[:, 0:n - lo], qmix[r, 6 + h % 2, cut], swa_k[r, lo:n], start=True, stop=True)
                    pe.matmul(b[:, 0:n - lo], ident_r[:, :], alibi[:, h, 256 - (n - lo):256],
                              start=False, stop=True, skip_group_check=True).then_inc(*scores_ready.done(key))

                attend(heads, scores, lambda n: turn(("swa", *heads[n]), probs[:, n % 3, :], min(heads[n][1], 1) + 1),
                       lambda h: values("swa", h, lambda j, h: swa_v[:, j, half(h // 2)], probs_t,
                                        half(h // 2), banded=True))

            def stick():
                def scores(item):
                    h, i = item
                    key = ("stick", h, i)
                    n, r = (i + 1) * P, half(h % 2)
                    b = s_bank(key)
                    pe.matmul(b[:, 0:n], qmix[r, 4 + h // 2, i * P:n], sb_k[r, h // 2, 0:n], start=True, stop=True)
                    pe.matmul(b[:, i * P:n], ident_r[:, :], strict_r[:, :], start=False, stop=True,
                              skip_group_check=True).then_inc(*scores_ready.done(key))

                attend(heads, scores, lambda n: turn(("stick", *heads[n]), probs[:, n % 3, :], heads[n][1] + 1),
                       lambda h: values("stick", h, lambda j, h: sb_v[:, j, half(h)], probs_t, half(h % 2)))

            def diff():
                def scores(item):
                    h, i = item
                    n, cut = (i + 1) * P, slice(i * P, (i + 1) * P)
                    lo = max(i - 1, 0) * P
                    for m in range(2):
                        key = ("diff", h, i, m)
                        b = s_bank(key)
                        pe.matmul(b[:, 0:n], mix2[half(m), h, cut], da_k[half(m), h, 0:n], start=True, stop=True)
                        pe.matmul(b[:, lo:n], ident[:, :], t5[:, 2 * h + m, 256 - (n - lo):256],
                                  start=False, stop=True, skip_group_check=True
                                  ).then_inc(*scores_ready.done(key))

                attend(heads, scores,
                       lambda n: turn(("diff", *heads[n]), probs2[:, n % 3 * 2, :], heads[n][1] + 1),
                       lambda h: values("diff", h, lambda j, h: da_v[:, j, h * P:(h + 1) * P], probs2_t, slice(0, P)))

            pe.sem_inc(w_used.sem, SLOTS)
            pe.wait_ge(*fills.after("ones"))
            pe.wait_ge(*rel_in.after("bucket_of"))
            pe.wait_ge(*dve_step.after("rel_rows"))
            for m in range(8):
                b = a_bank(("t5", m))
                pe.matmul(b[:, 0:T5W], rel_rows[0:BUCKETS + 1, m, :], bucket_of[0:BUCKETS + 1, :],
                          start=True, stop=True).then_inc(*sums.done(("t5", m)))

            with loop(pe, "layer1", DEPTH):
                project("kr", v_bank, lambda c: x_lo.carried(("in1", c), ("ln2", c)))
                for n in range(3):
                    project(("c", n), a_bank)
                for n in range(2):
                    project(("fq", n), a_bank)
                for n, at in enumerate((0, 0, TT)):
                    pe.wait_ge(*squared.after(("lat", n)))
                    token_sums(("lat", "sum", n), lambda cut: mla_q[:, n, cut], at, n == 0, n == 2)
                for n in range(2):
                    project(("fk", n), v_bank)
                spread("lat", 2)
                project_rows("fv", 2, 256)
                for n in range(2):
                    project(("sq", n), a_bank)
                for n in range(2):
                    project(("sk", n), v_bank)
                project_rows("sv", 2, 256)
                for n in range(2):
                    project(("wq", n), a_bank)
                project("wk", v_bank)
                u = unit("wv")
                b = v_bank("wv")
                for tile in range(TT):
                    cut = slice(tile * P, (tile + 1) * P)
                    for c in range(DC):
                        mm = mm3(b[:, cut], xn_hi[:, c, cut], xn_lo[:, c, cut], *w_tile(u, c), c == 0, c == DC - 1)
                mm.then_inc(*w_used.done("wv"))
                u = unit("uq")
                for c in range(2):
                    pe.wait_ge(*x_lo.after(("lat", c)))
                for n in range(5):
                    b = v_bank(("uq", n))
                    rows = slice(0, 96 if n < 4 else P)
                    for c in range(2):
                        cols = slice(c * S + n * 96, c * S + n * 96 + rows.stop)
                        mm = mm3(b[rows, :], w_hi[:, u, cols], w_lo[:, u, cols], lat_hi[:, c, :], lat_lo[:, c, :],
                                 c == 0, c == 1)
                    mm.then_inc(*(sums.done(("uq", n)) if n < 4 else w_used.done("uq")))
                u = unit("ukv")
                pe.wait_ge(*x_lo.after(("lat", 2)))
                for h in range(4):
                    b = a_bank(("uk", h))
                    cols = slice(h * HD, h * HD + P)
                    mm3(b[:, :], w_hi[:, u, cols], w_lo[:, u, cols], lat_hi[:, 2, :], lat_lo[:, 2, :],
                        True, True).then_inc(*sums.done(("uk", h)))
                for n, tiles in enumerate(UV_TILES):
                    b = a_bank(("uv", n))
                    for k, tile in enumerate(tiles):
                        cut = slice(tile * P, (tile + 1) * P)
                        mm = mm3(b[:, k * 256:(k + 1) * 256], lat_hi[:, 2, cut], lat_lo[:, 2, cut],
                                 w_hi[:, u, 256:512], w_lo[:, u, 256:512], True, True)
                    mm.then_inc(*(sums.done(("uv", n)) if n < 2 else w_used.done("ukv")))
                fox()
                mla()
                stick()
                swa()
                rms("mixnorm", 4, 2)
                for c in range(DC):
                    project(("wo", c), v_bank, is_split("mixnorm") if c == 0 else None)
                    if c:
                        pe.wait_ge(*v_read.after(("wo", c - 1)))
                        mean_chunk("ln1", c - 1)
                pe.wait_ge(*v_read.after(("wo", DC - 1)))
                mean_chunk("ln1", DC - 1)
                variance("ln1")
                ffn("ffn", is_split("ln1"), lambda c: mean_chunk("ln2", c))
                variance("ln2")

            def all_but_last(tag):
                return lambda c: square_sums(tag, c, DC, DC) if c < DC - 1 else None

            for c in range(DC - 1):
                square_sums("first", c, DC, DC)
            with loop(pe, "layer2", DEPTH):
                ffn("ffn1", lambda c: x_lo.carried(("first", c), ("next", c)), all_but_last("rms2"),
                    ("rms1", squared.carried(("first", DC - 1), ("next", DC - 1))))
                project(("lg", 0), a_bank, is_split("rms2"))
                square_sums("rms2", DC - 1, DC, DC)
                project(("lg", 1), a_bank)
                spread("rms2")
                for n in range(2):
                    project(("lx", n), v_bank)
                for n in range(2):
                    project(("scc", n), a_bank)
                for n in range(2):
                    project(("scx", n), v_bank)
                for n in range(2):
                    project(("scb", n), a_bank)
                pe.wait_ge(*dve_step.after("lam_products"))
                pe.matmul(stat_bank[:, 0:2], ones[0:HD, :], small[0:HD, 64:66], start=True, stop=True
                          ).then_inc(*sums.done("lam_sums"))
                for n in range(4):
                    project(("q2", n), a_bank)
                pe.wait_ge(*par_in.after("tables2"))
                for c in range(2):
                    pe.wait_ge(*dve_step.after(("xr", c)))
                    for m, name in enumerate("ri"):
                        b = a_bank(("gate", name, c))
                        pe.matmul(b[:, :], lru_w[:, 2 * m + c, :], xr[:, c, :], start=True, stop=True
                                  ).then_inc(*sums.done(("gate", name, c)))
                for n in range(4):
                    project(("k2", n), v_bank)
                project_rows("v2", 4, S)
                for n in range(2):
                    unit(("pad", n))
                    pe.matmul(stat_bank[:, 2:4], ones[:, :], ones[:, 0:2], start=True, stop=True
                              ).then_inc(*w_used.done(("pad", n)))
                pe.wait_ge(*dve_step.after(("q2", 3)))
                diff()
                rms("subln", 4, 1)
                for c in range(DC):
                    project(("wout", c), v_bank, is_split("subln") if c == 0 else None, mix_hi, mix_lo)
                    if c:
                        square_sums("rms3", c - 1, DC, DC)
                ffn("ffn2", is_split("rms3"), all_but_last("next"),
                    ("rms3", squared.after(("rms3", DC - 1))))
            square_sums("final", DC - 1, DC, DC, squared.after(("next", DC - 1)))
            spread("final")

        @block.scalar
        def _(act):
            def a_bank(key):
                return bank_a[a_read.slot(key, 2)]

            def split_hi(tag, c, source, dest=xn_hi):
                act.activation(dest[:, c, :], source, ACT.Copy).then_inc(*x_hi.done((tag, c)))

            def square(tag, c, source):
                if c >= 4:
                    act.wait_ge(*sums.after((tag, "sum", c - 4)))
                act.activation(work[:, c % 4, :], source, ACT.Square).then_inc(*squared.done((tag, c)))

            def root(tag, groups):
                act.wait_ge(*dve_step.after((tag, "var")))
                act.activation(small[:, 16:16 + groups * TT], small[:, 0:groups * TT], ACT.Sqrt
                               ).then_inc(*rooted.done(tag))

            def copy_bank(key, ready, out, rows=slice(0, P), n=S, func=ACT.Copy, **kw):
                act.wait_ge(*ready.after(key))
                act.activation(out, a_bank(key)[rows, 0:n], func, **kw).then_inc(*a_read.done(key))

            def rms(tag, groups, per, source, ready, dest=xn_hi):
                for c in range(groups * per):
                    ready(c)
                    square(tag, c, source(c))
                root(tag, groups)
                for c in range(groups * per):
                    last = c % per == per - 1
                    act.wait_ge(*(scaled if last else value).after((tag, c)))
                    split_hi(tag, c, work[:, c % 4, :], dest)

            def gained(tag, column, ready):
                for c in range(DC):
                    ready(c)
                    act.activation(xn_hi[:, c, :], resid[:, c, :], ACT.Copy, scale=par2[:, column + c:column + c + 1]
                                   ).then_inc(*x_hi.done((tag, c)))
                    square(tag, c, resid[:, c, :])

            def norm_ln(tag, columns, split):
                for c in range(DC):
                    act.wait_ge(*centered.after((tag, c)))
                    square(tag, c, resid[:, c, :])
                root(tag, 1)
                g, b = (C1[x] for x in columns)
                for c in range(DC + 1):
                    if c < DC:
                        act.wait_ge(*scaled.after((tag, c)))
                        act.activation(resid[:, c, :], resid[:, c, :], ACT.Identity, scale=par1[:, g + c:g + c + 1],
                                       bias=par1[:, b + c:b + c + 1]).then_inc(*affine.done((tag, c)))
                    if c and split:
                        act.wait_ge(*affine.after((tag, c - 1)))
                        split_hi(tag, c - 1, resid[:, c - 1, :])
                act.wait_ge(*affine.after((tag, DC - 1)))

            def ffn(tag):
                def hidden(k, at, gate, up, h):
                    act.wait_ge(*w_used.after((tag, gate, k)))
                    act.activation(work[:, k, :], a_bank((tag, gate, k))[:, :], ACT.Silu
                                   ).then_inc(*a_read.done((tag, gate, k)))
                    act.wait_ge(*v_read.after((tag, up, k)))
                    act.activation(h_hi[:, at, :], work[:, 2 + k:3 + k, :], ACT.Copy
                                   ).then_inc(*x_hi.done((tag, h, k)))

                for k in range(2):
                    hidden(k, slice(k, k + 1), "gate0", "up0", "h0")
                with loop(act, tag, FC // 2 - 1) as i:
                    for k in range(2):
                        hidden(k, bass.ds(i * 2 + (2 + k), 1), "gate", "up", "h")

            def ffn_scaled(tag, stats):
                root(stats, 1)

                def hidden(k, at, gate, up, h):
                    key = (tag, gate, k)
                    act.wait_ge(*w_used.after(key))
                    act.activation(work[:, k, :], a_bank(key)[:, :], ACT.Copy).then_inc(*a_read.done(key))
                    act.wait_ge(*value.after(key))
                    act.activation(work[:, k, :], work[:, k, :], ACT.Silu).then_inc(*gated.done(key))
                    act.wait_ge(*product.after((tag, h, k)))
                    act.activation(h_hi[:, at, :], work[:, 2 + k:3 + k, :], ACT.Copy).then_inc(*x_hi.done((tag, h, k)))

                for k in range(2):
                    hidden(k, slice(k, k + 1), "gate0", "up0", "h0")
                with loop(act, tag, FC // 2 - 1) as i:
                    for k in range(2):
                        hidden(k, bass.ds(i * 2 + (2 + k), 1), "gate", "up", "h")

            def exp_item(key, slot, n, item):
                act.wait_ge(*row_max.after(key))
                b = bank_s[s_read.slot(key, 4)]
                act.activation(slot[:, 0:n], b[:, 0:n], ACT.Exp, bias=small[:, 32 + item:33 + item],
                               accum_out=small[:, 64 + item:65 + item]).then_inc(*s_read.done(key))

            def keep_turned(tag, n, pt, blocks):
                h, i = heads[n]
                key = (tag, h, i)
                if i == 0 and h >= 2:
                    act.wait_ge(*sums.after((tag, "out", h - 2)))
                act.wait_ge(*turned.after(key))
                lo = i + 1 - blocks
                act.activation(pt[:, h % 2, lo:i + 1, i * P:(i + 1) * P],
                               a_bank(key)[:, 0:blocks * P].rearrange("p (j q) -> p j q", q=P), ACT.Copy
                               ).then_inc(*a_read.done(key))

            heads = [(h, i) for h in range(4) for i in range(TT)]

            def softmax(tag, width, blocks):
                for n in range(len(heads) + 2):
                    if n < len(heads):
                        exp_item((tag, *heads[n]), probs[:, n % 3, :], width(heads[n][1]), n)
                    if n >= 2:
                        keep_turned(tag, n - 2, probs_t, blocks(heads[n - 2][1]))

            act.sem_inc(a_read.sem, 2)
            act.sem_inc(s_read.sem, 4)
            for name, dest in (("rel", rel[0:BUCKETS, :]), ("rel_far", rel_far[0:BUCKETS, :]),
                               ("bucket_of", bucket_of[0:BUCKETS + 1, :])):
                act.dma_start(dest, t[name]).then_inc(*rel_in.done(name, 16))
            for c in range(1, DC, 2):
                act.dma_start(resid[:, c, :], t["x"][:, c, :]).then_inc(*x_in[c].done("x", 16))
            for name, dest in (("ident", ident[:, :]), ("mask", work[:, 0, 0:P]), ("strict", work[:, 0, P:2 * P])):
                act.dma_start(dest, t[name]).then_inc(*const_in.done(name, 16))
            for m in range(8):
                copy_bank(("t5", m), sums, t5_row[:, m, :], n=T5W)
            act.wait_ge(*const_in.after("strict"))
            act.activation(ident_r[:, :], ident[:, :], ACT.Copy).then_inc(*act_step.done("ident_r"))
            act.activation(mask_r[:, :], work[:, 0, 0:P], ACT.Copy).then_inc(*act_step.done("mask_r"))
            act.activation(strict_r[:, :], work[:, 0, P:2 * P], ACT.Copy).then_inc(*act_step.done("strict_r"))
            act.wait_ge(*a_read.after(("t5", 7)))
            act.dma_start(t5_dram.rearrange("m q w -> q m w"), t5_row[:, :, :]).then_inc(*t5_out.done("rows", 16))

            for c in range(DC):
                act.wait_ge(*x_in[c].after("x"))
                split_hi("in1", c, resid[:, c, :])
            with loop(act, "layer1", DEPTH) as l:
                act.wait_ge(*t5_out.after("rows"))
                act.dma_start(par1[:, :], t["par1"][l]).then_inc(*par_in.done("par1", 16))
                act.dma_start(rope[:, :, :], t["rope"]).then_inc(*par_in.done("rope", 16))
                act.dma_start(mla_v[:, :, :], t["alibi"]).then_inc(*par_in.done("tables1", 16))
                for n in range(3):
                    copy_bank(("c", n), w_used, cq[:, n, :])
                    act.wait_ge(*a_read.after(("c", n)))
                    act.activation(mla_q[:, n, :], cq[:, n, :], ACT.Square).then_inc(*squared.done(("lat", n)))
                for n in range(2):
                    copy_bank(("fq", n), w_used, qmix[:, n, :], scale=HD ** -0.5)
                act.wait_ge(*par_in.after("tables1"))
                act.activation(alibi[:, :, :], mla_v[:, :, :], ACT.Copy).then_inc(*act_step.done("alibi_r"))
                root("lat", 2)
                act.wait_ge(*dve_step.after("fz"))
                f = work[0:4, 0:4, :]
                act.activation(f[:, 1, :], f[:, 0, :], ACT.Abs).then_inc(*act_step.done("f_abs"))
                act.wait_ge(*act_step.after("f_abs"))
                act.activation(f[:, 1, :], f[:, 1, :], ACT.Exp, scale=-1.0).then_inc(*act_step.done("f_exp"))
                act.wait_ge(*act_step.after("f_exp"))
                act.activation(f[:, 1, :], f[:, 1, :], ACT.Ln, bias=ones[0:4, 0:1]).then_inc(*act_step.done("f_ln"))
                rows_bank = lambda tag, tile, out, n: copy_bank((tag, tile), sums, out, n=n)
                for tile in (0, 2):
                    rows_bank("fv", tile, fox_v[:, tile, :], 256)
                for n in range(3):
                    act.wait_ge(*value.after(("lat", n)))
                    split_hi("lat", n, cq[:, n, :], lat_hi)
                for n in range(2):
                    copy_bank(("sq", n), w_used, qmix[:, 4 + n, :], scale=HD ** -0.5)
                for tile in (0, 2):
                    rows_bank("sv", tile, sb_v[:, tile, :], 256)
                for n in range(2):
                    copy_bank(("wq", n), w_used, qmix[:, 6 + n, :], scale=HD ** -0.5)
                act.wait_ge(*dve_step.after("cum_lo"))
                for h in range(4):
                    for r, part in ((0, 2), (64, 3)):
                        ins = act.activation(aug_q[r:r + 4, h, :], work[0:4, part, :], ACT.Copy, scale=ident[0:4, h:h + 1])
                ins.then_inc(*act_step.done("aug"))
                for h in range(4):
                    copy_bank(("uk", h), sums, mla_k[0:HD, h, :], rows=slice(0, HD))
                for n, tiles in enumerate(UV_TILES):
                    k = len(tiles)
                    act.wait_ge(*(sums.after(("uv", n)) if n < 2 else w_used.after("ukv")))
                    act.activation(mla_v[:, tiles[0]:tiles[0] + k, :],
                                   a_bank(("uv", n))[:, 0:k * 256].rearrange("p (t c) -> p t c", t=k),
                                   ACT.Copy).then_inc(*a_read.done(("uv", n)))
                causal = lambda i: (i + 1) * P
                softmax("fox", causal, lambda i: i + 1)
                act.wait_ge(*sums.after(("fox", "out", 3)))
                softmax("mla", causal, lambda i: i + 1)
                act.wait_ge(*sums.after(("mla", "out", 3)))
                for n in range(len(heads) + 2):
                    if n < len(heads):
                        key, w = ("stick", *heads[n]), (heads[n][1] + 1) * P
                        b = bank_s[s_read.slot(key, 4)]
                        act.wait_ge(*scores_ready.after(key))
                        act.activation(probs[:, n % 3, 0:w], b[:, 0:w], ACT.Sigmoid).then_inc(*act_step.done((*key, "beta")))
                        if n >= 2:
                            act.wait_ge(*dve_step.after(("stick", *heads[n - 2], "products")))
                        act.activation(work[:, n % 2, 0:w], b[:, 0:w], ACT.Sigmoid, scale=-1.0).then_inc(*s_read.done(key))
                    if n >= 2:
                        keep_turned("stick", n - 2, probs_t, heads[n - 2][1] + 1)
                act.wait_ge(*sums.after(("stick", "out", 3)))

                softmax("swa", lambda i: min(i + 1, 2) * P + 1, lambda i: min(i, 1) + 1)
                rms("mixnorm", 4, 2, lambda c: qmix[:, c, :],
                    lambda c: act.wait_ge(*v_read.after(("swa", "out", 3))))
                norm_ln("ln1", ("ln1_g", "ln1_b"), True)
                ffn("ffn")
                norm_ln("ln2", ("ln2_g", "ln2_b"), True)

            act.dma_start(par2[:, :], t["par2"][0]).then_inc(*par_in.done("par2", 16))
            act.wait_ge(*par_in.after("par2"))
            act.wait_ge(*x_lo.after(("ln2", DC - 1)))
            gained("first", C2["ffn1"], lambda c: None)
            with loop(act, "layer2", DEPTH) as l:
                ffn_scaled("ffn1", "rms1")
                gained("rms2", C2["mix"], lambda c: act.wait_ge(*v_read.after(("ffn1", "down", c))))
                root("rms2", 1)
                act.dma_start(lru_w[:, :, :], t["lru_w"][l]).then_inc(*par_in.done("lru_w", 16))
                act.dma_start(t5[:, :, :], t["t5_skewed"]).then_inc(*par_in.done("tables2", 16))
                for n in range(2):
                    copy_bank(("lg", n), w_used, lru_g[:, n, :])
                for n in range(2):
                    copy_bank(("scc", n), w_used, sc_c[:, n, :])
                for n in range(2):
                    act.wait_ge(*value.after(("lg", n)))
                    act.activation(lru_g[:, n, :], lru_g[:, n, :], ACT.Gelu_apprx_tanh).then_inc(*act_step.done(("gelu", n)))
                for n in range(2):
                    copy_bank(("scb", n), w_used, sc_b[:, n, :])
                lam = par2[:, C2["lam"]:C2["lam"] + 2]
                act.activation(small[:, 96:98], lam, ACT.Abs).then_inc(*act_step.done("lam_abs"))
                act.wait_ge(*act_step.after("lam_abs"))
                act.activation(small[:, 98:100], small[:, 96:98], ACT.Exp, scale=-1.0).then_inc(*act_step.done("lam_exp"))
                act.wait_ge(*sums.after("lam_sums"))
                act.activation(small[:, 66:68], stat_bank[:, 0:2], ACT.Exp).then_inc(*act_step.done("lam_sums"))
                for n in range(4):
                    copy_bank(("q2", n), w_used, mix2[:, n, :])
                for c in range(2):
                    for name, dest, column in (("r", gate_r, "ba"), ("i", gate_i, "bx")):
                        copy_bank(("gate", name, c), sums, dest[:, c, :], func=ACT.Sigmoid,
                                  bias=par2[:, C2[column] + c:C2[column] + c + 1])
                act.wait_ge(*a_read.after(("gate", "i", 1)))
                act.wait_ge(*dve_step.after("s8"))
                for c in range(2):
                    act.activation(lru_a[:, c, :], gate_r[:, c, :], ACT.Exp, scale=small[:, 104 + c:105 + c]
                                   ).then_inc(*act_step.done(("lru_a", c)))
                    act.activation(gate_r[:, c, :], gate_r[:, c, :], ACT.Tanh, scale=small[:, 102 + c:103 + c]
                                   ).then_inc(*act_step.done(("tanh", c)))
                for c in range(2):
                    act.wait_ge(*dve_step.after(("mult2", c)))
                    act.activation(gate_r[:, c, :], gate_r[:, c, :], ACT.Sqrt).then_inc(*act_step.done(("mult", c)))
                for tile in (0, 2):
                    copy_bank(("v2", tile), sums, da_v[:, tile, :], scale=small[:, tile:tile + 1])
                for n in range(len(heads) + 2):
                    if n < len(heads):
                        h, i = heads[n]
                        for m in range(2):
                            exp_item(("diff", h, i, m), probs2[:, n % 3 * 2 + m, :], (i + 1) * P, 2 * (n % 8) + m)
                    if n >= 2:
                        keep_turned("diff", n - 2, probs2_t, heads[n - 2][1] + 1)
                rms("subln", 4, 1, lambda c: mix2[:, c, :], lambda c: act.wait_ge(*v_read.after(("diff", "out", c))),
                    mix_hi)
                for c in range(4, DC):
                    act.wait_ge(*dve_step.after(("mix2", c)))
                    split_hi("subln", c, mix2[:, c, :], mix_hi)
                gained("rms3", C2["ffn2"], lambda c: act.wait_ge(*v_read.after(("wout", c))))
                act.wait_ge(*x_lo.after(("rms3", DC - 1)))
                act.dma_start(par2[:, :], t["par2"][l + 1]).then_inc(*par_in.done("par2_next", 16))
                ffn_scaled("ffn2", "rms3")
                act.wait_ge(*par_in.after("par2_next"))
                gained("next", C2["ffn1"], lambda c: act.wait_ge(*v_read.after(("ffn2", "down", c))))
            root("final", 1)

        @block.vector
        def _(dve):
            def v_bank(key):
                return bank_v[v_read.slot(key, 2)]

            def step(ins, key):
                ins.then_inc(*dve_step.done(key))
                dve.wait_ge(*dve_step.after(key))

            def split_lo(tag, c, source, hi=xn_hi, lo=xn_lo):
                dve.wait_ge(*x_hi.after((tag, c)))
                dve.tensor_tensor(lo[:, c, :], source, hi[:, c, :].bitcast(F32), ALU.subtract
                                  ).then_inc(*x_lo.done((tag, c)))

            def diagonals(tag, groups, column):
                for g in range(groups):
                    for tile in range(TT):
                        j = g * TT + tile
                        ins = dve.tensor_scalar(diag[:, j, :], ident[:, :], small[:, column + j:column + j + 1],
                                                None, ALU.mult)
                    ins.then_inc(*diag_ready.done((tag, g)))

            def inverse_root(tag, groups, last, n, eps):
                dve.wait_ge(*sums.after((tag, "sum", last)))
                dve.tensor_scalar(small[:, 0:groups * TT], stat_bank[:, 0:groups * TT], 1.0 / n, eps,
                                  ALU.mult, ALU.add).then_inc(*dve_step.done((tag, "var")))
                inverse(tag, groups)

            def inverse(tag, groups):
                dve.wait_ge(*rooted.after(tag))
                step(dve.reciprocal(small[:, 0:groups * TT], small[:, 16:16 + groups * TT]), (tag, "rstd"))
                diagonals(tag, groups, 0)

            def rms(tag, groups, per, source, par, n, eps, hi=xn_hi, lo=xn_lo):
                inverse_root(tag, groups, groups * per - 1, n, eps)
                total = groups * per
                for c in range(total + 1):
                    if c < total:
                        g, last = c // per, c % per == per - 1
                        if c % per == 0:
                            dve.wait_ge(*sums.after((tag, "spread", g)))
                        if c >= 4:
                            dve.wait_ge(*x_lo.after((tag, c - 4)))
                        dve.scalar_tensor_tensor(out=work[:, c % 4, :], in0=source(c), scalar=par(c), in1=bank_s[g][:, :],
                                                 op0=ALU.mult, op1=ALU.mult
                                                 ).then_inc(*(scaled if last else value).done((tag, c)))
                    if c:
                        split_lo(tag, c - 1, work[:, (c - 1) % 4, :], hi, lo)

            def factor(tag):
                inverse_root(tag, 1, DC - 1, D, 1e-6)
                dve.wait_ge(*sums.after((tag, "spread", 0)))
                step(dve.tensor_copy(scale_by[:, :], bank_s[0][:, :]), (tag, "factor"))

            def gained_lo(tag, column, c):
                dve.wait_ge(*x_hi.after((tag, c)))
                dve.scalar_tensor_tensor(out=xn_lo[:, c, :], in0=resid[:, c, :], scalar=par2[:, column + c:column + c + 1],
                                         in1=xn_hi[:, c, :].bitcast(F32), op0=ALU.mult, op1=ALU.subtract
                                         ).then_inc(*x_lo.done((tag, c)))

            def times_factor(out, signalled, ready, source=None):
                dve.wait_ge(*ready)
                dve.tensor_tensor(out, out if source is None else source, scale_by[:, :], ALU.mult).then_inc(*signalled)

            def col(par, table, name, c=0):
                return par[:, table[name] + c:table[name] + c + 1]

            def norm_ln(tag, split):
                dve.wait_ge(*sums.after((tag, "mean", DC - 1)))
                for c in range(DC):
                    dve.scalar_tensor_tensor(out=resid[:, c, :], in0=bank_s[0][:, :], scalar=-1.0 / D, in1=resid[:, c, :],
                                             op0=ALU.mult, op1=ALU.add).then_inc(*centered.done((tag, c)))
                inverse_root(tag, 1, DC - 1, D, 1e-5)
                dve.wait_ge(*sums.after((tag, "spread", 0)))
                for c in range(DC + 2):
                    if c < DC:
                        dve.tensor_tensor(resid[:, c, :], resid[:, c, :], bank_s[0][:, :], ALU.mult
                                          ).then_inc(*scaled.done((tag, c)))
                    if c >= 2 and split:
                        split_lo(tag, c - 2, resid[:, c - 2, :])

            def ffn(tag):
                def hidden(k, at, gate, up, h):
                    dve.wait_ge(*a_read.after((tag, gate, k)))
                    dve.wait_ge(*w_used.after((tag, up, k)))
                    dve.tensor_tensor(work[:, 2 + k, :], work[:, k, :], v_bank((tag, up, k))[:, :], ALU.mult
                                      ).then_inc(*v_read.done((tag, up, k)))
                    hidden_lo(tag, k, at, h)

                for k in range(2):
                    hidden(k, slice(k, k + 1), "gate0", "up0", "h0")
                with loop(dve, tag, FC // 2 - 1) as i:
                    for k in range(2):
                        hidden(k, bass.ds(i * 2 + (2 + k), 1), "gate", "up", "h")

            def hidden_lo(tag, k, at, h):
                dve.wait_ge(*x_hi.after((tag, h, k)))
                dve.tensor_tensor(h_lo[:, at, :], work[:, 2 + k:3 + k, :], h_hi[:, at, :].bitcast(F32),
                                  ALU.subtract).then_inc(*x_lo.done((tag, h, k)))

            def ffn_scaled(tag, stats):
                factor(stats)

                def hidden(k, at, gate, up, h):
                    times_factor(work[:, k, :], value.done((tag, gate, k)), a_read.after((tag, gate, k)))
                    times_factor(work[:, 2 + k, :], v_read.done((tag, up, k)), w_used.after((tag, up, k)),
                                 v_bank((tag, up, k))[:, :])
                    dve.wait_ge(*v_read.after((tag, up, k)))
                    dve.wait_ge(*gated.after((tag, gate, k)))
                    dve.tensor_tensor(work[:, 2 + k, :], work[:, k, :], work[:, 2 + k, :], ALU.mult
                                      ).then_inc(*product.done((tag, h, k)))
                    hidden_lo(tag, k, at, h)

                for k in range(2):
                    hidden(k, slice(k, k + 1), "gate0", "up0", "h0")
                with loop(dve, tag, FC // 2 - 1) as i:
                    for k in range(2):
                        hidden(k, bass.ds(i * 2 + (2 + k), 1), "gate", "up", "h")

            def down(tag, first, second, swap, after_chunk=None):
                for c in range(DC):
                    key = (tag, "down", c)
                    end = c * FC + FC - 1
                    dve.wait_ge(*(w_used.after((tag, "wd", end // 8)) if end % 8 == 7 else sums.after(key)))
                    b = v_bank(key)
                    if swap:
                        ins = dve.scalar_tensor_tensor(out=resid[:, c, :], in0=b[:, :], scalar=second,
                                                       in1=resid[:, c, :], op0=ALU.mult, op1=ALU.add)
                    else:
                        ins = dve.scalar_tensor_tensor(out=resid[:, c, :], in0=resid[:, c, :], scalar=first,
                                                       in1=b[:, :], op0=ALU.mult, op1=ALU.add)
                    ins.then_inc(*v_read.done(key))
                    if after_chunk:
                        after_chunk(c)

            def keep(key, ready, out, rows=slice(0, P), n=S):
                dve.wait_ge(*ready.after(key))
                dve.tensor_copy(out, v_bank(key)[rows, 0:n]).then_inc(*v_read.done(key))

            heads = [(h, i) for h in range(4) for i in range(TT)]

            def half(n):
                return slice(n * HD, (n + 1) * HD)

            def softmax(tag, width, out):
                for n in range(len(heads) + 4):
                    if n < len(heads):
                        h, i = heads[n]
                        key = (tag, h, i)
                        b = bank_s[s_read.slot(key, 4)]
                        dve.wait_ge(*scores_ready.after(key))
                        dve.tensor_reduce(small[:, 32 + n:33 + n], b[:, 0:width(i)], AX.X, ALU.max, negate=True
                                          ).then_inc(*row_max.done(key))
                    if 1 <= n <= len(heads):
                        m = n - 1
                        h, i = heads[m]
                        key = (tag, h, i)
                        total = small[:, 64 + m:65 + m]
                        dve.wait_ge(*s_read.after(key))
                        step(dve.reciprocal(small[:, 96 + m:97 + m], total), (*key, "inverse"))
                        dve.tensor_scalar(probs[:, m % 3, 0:width(i)], probs[:, m % 3, 0:width(i)],
                                          small[:, 96 + m:97 + m], None, ALU.mult).then_inc(*probs_ready.done(key))
                    if n >= 4 and heads[n - 4][1] == TT - 1:
                        h = heads[n - 4][0]
                        rows, dest = out(h)
                        keep((tag, "out", h), sums, dest, rows)

            dve.sem_inc(v_read.sem, 2)
            dve.wait_ge(*fills.after("ones"))
            dve.wait_ge(*rel_in.after("bucket_of"))
            dve.memset(rel_rows[BUCKETS:BUCKETS + 1, :, :], NEG)
            dve.tensor_tensor(rel[0:BUCKETS, :], rel[0:BUCKETS, :], rel_far[0:BUCKETS, :], ALU.subtract
                              ).then_inc(*dve_step.done("rel"))
            dve.wait_ge(*dve_step.after("rel"))
            dve.tensor_copy(rel_rows[0:BUCKETS, :, :], rel[0:BUCKETS, :].unsqueeze(2).to_broadcast([BUCKETS, 8, P])
                            ).then_inc(*dve_step.done("rel_rows"))

            for c in range(DC):
                dve.wait_ge(*x_in[c].after("x"))
                split_lo("in1", c, resid[:, c, :])
            dve.wait_ge(*act_step.after("strict_r"))

            with loop(dve, "layer1", DEPTH):
                dve.wait_ge(*par_in.after("tables1"))
                dve.wait_ge(*w_used.after("kr"))
                b = v_bank("kr")
                dve.tensor_scalar(work[0:4, 0, :], b[0:4, :], par1[0:4, C1["b_f"]:C1["b_f"] + 1], None, ALU.add
                                  ).then_inc(*dve_step.done("fz"))
                dve.tensor_tensor(work[64:96, 2, :], b[64:96, :], rope[64:96, 2, :], ALU.mult
                                  ).then_inc(*dve_step.done("kr_cos"))
                dve.tensor_tensor(work[64:96, 3, :], b[32:64, :], rope[32:64, 3, :], ALU.mult
                                  ).then_inc(*v_read.done("kr"))
                dve.wait_ge(*v_read.after("kr"))
                for h in range(4):
                    dve.tensor_tensor(mla_k[64:96, h, :], work[64:96, 2, :], work[64:96, 3, :], ALU.add
                                      ).then_inc(*dve_step.done(("kr", h)))
                dve.wait_ge(*sums.after(("lat", "sum", 2)))
                dve.tensor_scalar(small[:, 0:TT], stat_bank[:, 0:TT], 1.0 / 256, 1e-6, ALU.mult, ALU.add)
                dve.tensor_scalar(small[:, TT:2 * TT], stat_bank[:, TT:2 * TT], 1.0 / P, 1e-6, ALU.mult, ALU.add
                                  ).then_inc(*dve_step.done(("lat", "var")))
                inverse("lat", 2)
                for n in range(2):
                    keep(("fk", n), w_used, fox_k[:, n, :])
                for n, column in enumerate((C1["g_q"], C1["g_q"] + 1, C1["g_kv"])):
                    dve.wait_ge(*sums.after(("lat", "spread", n // 2)))
                    dve.scalar_tensor_tensor(out=cq[:, n, :], in0=cq[:, n, :], scalar=par1[:, column:column + 1],
                                             in1=bank_s[n // 2][:, :], op0=ALU.mult, op1=ALU.mult
                                             ).then_inc(*value.done(("lat", n)))
                dve.wait_ge(*act_step.after("f_ln"))
                step(dve.scalar_tensor_tensor(out=work[0:4, 2, :], in0=work[0:4, 0, :], scalar=0.0,
                                              in1=work[0:4, 1, :], op0=ALU.min, op1=ALU.subtract), "log_f")
                step(dve.memset(work[0:4, 0, :], 1.0), "log_ones")
                step(dve.tensor_tensor_scan(work[0:4, 3, :], work[0:4, 0, :], work[0:4, 2, :], 0.0,
                                            ALU.mult, ALU.add), "cum0")
                dve.tensor_copy(cum[0:4, :], work[0:4, 3, :]).then_inc(*dve_step.done("cum"))
                for tile in (1, 3):
                    dve.wait_ge(*(sums.after(("fv", 1)) if tile == 1 else w_used.after(("fv", "unit", 1))))
                    dve.tensor_copy(fox_v[:, tile, :], v_bank(("fv", tile))[:, 0:256]).then_inc(*v_read.done(("fv", tile)))
                for n in range(3):
                    split_lo("lat", n, cq[:, n, :], lat_hi, lat_lo)
                for n in range(2):
                    keep(("sk", n), w_used, sb_k[:, n, :])
                for tile in (1, 3):
                    dve.wait_ge(*(sums.after(("sv", 1)) if tile == 1 else w_used.after(("sv", "unit", 1))))
                    dve.tensor_copy(sb_v[:, tile, :], v_bank(("sv", tile))[:, 0:256]).then_inc(*v_read.done(("sv", tile)))
                keep("wk", w_used, swa_k[:, :])
                dve.wait_ge(*w_used.after("wv"))
                dve.tensor_copy(swa_v[:, :, :], v_bank("wv")[:, :].rearrange("p (t c) -> p t c", t=TT)
                                ).then_inc(*v_read.done("wv"))
                dve.tensor_copy(as_r(work[0:4, 2, :]), cum[0:4, :]).then_inc(*dve_step.done("cum_hi"))
                step(dve.tensor_copy(aug_q[:, :, :], zero[:, 0:1].unsqueeze(2).to_broadcast([P, 4, S])), "aug_zero")
                step(dve.tensor_copy(aug_k[:, :], zero[:, 0:1].to_broadcast([P, S])), "aug_k0")
                step(dve.tensor_tensor(work[0:4, 3, :], cum[0:4, :], work[0:4, 2, :], ALU.subtract), "cum_lo")
                one_hot = ident[0:4, 0:4].unsqueeze(2).to_broadcast([4, 4, S])
                for r, part in ((0, 2), (64, 3)):
                    dve.tensor_scalar(aug_k[r:r + 4, :], cum[0:4, :], 0.0, 1.0, ALU.mult, ALU.add)
                    dve.tensor_scalar(aug_k[r + 32:r + 36, :], work[0:4, part, :], -1.0, None, ALU.mult)
                    ins = dve.tensor_copy(aug_q[r + 32:r + 36, :, :], one_hot)
                ins.then_inc(*dve_step.done("aug"))
                for h in range(4):
                    key = ("uq", h)
                    dve.wait_ge(*sums.after(key))
                    b = v_bank(key)
                    dve.tensor_scalar(mla_q[0:HD, h, :], b[0:HD, :], 96.0 ** -0.5, None, ALU.mult
                                      ).then_inc(*dve_step.done(("q_plain", h)))
                    dve.tensor_tensor(mla_q[64:96, h, :], b[64:96, :], rope[64:96, 0, :], ALU.mult
                                      ).then_inc(*v_read.done(key))
                dve.wait_ge(*w_used.after("uq"))
                b = v_bank(("uq", 4))
                for h in range(4):
                    r = slice(h * ROPE, (h + 1) * ROPE)
                    ins = dve.tensor_tensor(work[64:96, h, :], b[r, :], rope[r, 1, :], ALU.mult)
                ins.then_inc(*v_read.done(("uq", 4)))
                dve.wait_ge(*v_read.after(("uq", 4)))
                for h in range(4):
                    dve.tensor_tensor(mla_q[64:96, h, :], mla_q[64:96, h, :], work[64:96, h, :], ALU.add
                                      ).then_inc(*dve_step.done(("mla_q", h)))

                causal = lambda i: (i + 1) * P
                softmax("fox", causal, lambda h: (half(h % 2), qmix[half(h % 2), h // 2, :]))
                softmax("mla", causal, lambda h: (half(h % 2), qmix[half(h % 2), 2 + h // 2, :]))
                for n in range(1, len(heads) + 4):
                    if n <= len(heads):
                        h, i = heads[n - 1]
                        key, w, k = ("stick", h, i), (i + 1) * P, (n - 1) % 2
                        tail, beta = work[:, 2 + k, :], probs[:, (n - 1) % 3, :]
                        dve.wait_ge(*s_read.after(key))
                        step(dve.tensor_tensor_scan(tail[:, 0:w][:, ::-1], work[:, k, 0:w][:, ::-1],
                                                    zero[:, 0:1].to_broadcast([P, w]), 1.0, ALU.mult, ALU.add),
                             (*key, "products"))
                        dve.tensor_tensor(beta[:, 0:w - 1], beta[:, 0:w - 1], tail[:, 1:w], ALU.mult
                                          ).then_inc(*probs_ready.done(key))
                    if n >= 4 and heads[n - 4][1] == TT - 1:
                        h = heads[n - 4][0]
                        keep(("stick", "out", h), sums, qmix[half(h % 2), 4 + h // 2, :], half(h % 2))
                softmax("swa", lambda i: min(i + 1, 2) * P + 1, lambda h: (half(h // 2), qmix[half(h // 2), 6 + h % 2, :]))
                rms("mixnorm", 4, 2, lambda c: qmix[:, c, :], lambda c: col(par1, C1, "mix_g", c), 256, 1e-6)
                for c in range(DC):
                    dve.wait_ge(*w_used.after(("wo", c)))
                    dve.scalar_tensor_tensor(out=resid[:, c, :], in0=resid[:, c, :], scalar=ALPHA,
                                             in1=v_bank(("wo", c))[:, :], op0=ALU.mult, op1=ALU.add
                                             ).then_inc(*v_read.done(("wo", c)))
                norm_ln("ln1", True)
                ffn("ffn")
                down("ffn", ALPHA, 1.0, False)
                norm_ln("ln2", True)

            dve.wait_ge(*par_in.after("par2"))
            for c in range(DC):
                gained_lo("first", C2["ffn1"], c)
            with loop(dve, "layer2", DEPTH):
                ffn_scaled("ffn1", "rms1")
                down("ffn1", 1.0, 0.5, True, lambda c: gained_lo("rms2", C2["mix"], c))
                for m, (q, k) in enumerate((("lq1", "lk1"), ("lq2", "lk2"))):
                    ins = dve.tensor_tensor(small[0:HD, 64 + m:65 + m], par2[0:HD, C2[q]:C2[q] + 1],
                                            par2[0:HD, C2[k]:C2[k] + 1], ALU.mult)
                ins.then_inc(*dve_step.done("lam_products"))
                factor("rms2")
                for n in range(2):
                    times_factor(lru_g[:, n, :], value.done(("lg", n)), a_read.after(("lg", n)))
                for n in range(2):
                    times_factor(lru_x[:, n, :], v_read.done(("lx", n)), w_used.after(("lx", n)), v_bank(("lx", n))[:, :])
                dve.wait_ge(*v_read.after(("lx", 1)))
                for c in range(2):
                    w = lambda k: par2[:, C2["lru_w"] + 2 * k + c:C2["lru_w"] + 2 * k + c + 1]
                    step(dve.tensor_scalar(xr[:, c, :], lru_x[:, c, :], w(3), col(par2, C2, "lru_b", c),
                                           ALU.mult, ALU.add), ("lconv", c, 0))
                    for d in (1, 2, 3):
                        ins = dve.scalar_tensor_tensor(out=xr[:, c, d:S], in0=lru_x[:, c, 0:S - d], scalar=w(3 - d),
                                                       in1=xr[:, c, d:S], op0=ALU.mult, op1=ALU.add)
                        step(ins, ("lconv", c, d) if d < 3 else ("xr", c))
                for n in range(2):
                    key = ("scx", n)
                    times_factor(sc_c[:, n, :], dve_step.done(("scc", n)), a_read.after(("scc", n)))
                    times_factor(sc_x[:, n, :], v_read.done(key), w_used.after(key), v_bank(key)[:, :])
                    dve.wait_ge(*dve_step.after(("scc", n)))
                    dve.wait_ge(*v_read.after(key))
                    step(dve.tensor_tensor(sc_x[:, n, :], sc_c[:, n, :], sc_x[:, n, :], ALU.mult), ("sc", n))
                for c in range(2):
                    w = lambda k: par2[:, C2["sc_w"] + 2 * k + c:C2["sc_w"] + 2 * k + c + 1]
                    step(dve.tensor_scalar(sc_c[:, c, :], sc_x[:, c, :], w(2), None, ALU.mult), ("conv", c, 0))
                    for d in (1, 2):
                        step(dve.scalar_tensor_tensor(out=sc_c[:, c, d:S], in0=sc_x[:, c, 0:S - d], scalar=w(2 - d),
                                                      in1=sc_c[:, c, d:S], op0=ALU.mult, op1=ALU.add), ("conv", c, d))
                    times_factor(sc_b[:, c, :], dve_step.done(("scb", c)), a_read.after(("scb", c)))
                    dve.wait_ge(*dve_step.after(("scb", c)))
                    dve.tensor_tensor(mix2[:, 4 + c, :], sc_c[:, c, :], sc_b[:, c, :], ALU.mult
                                      ).then_inc(*dve_step.done(("mix2", 4 + c)))
                dve.wait_ge(*act_step.after("lam_exp"))
                e, s, s2, p = (small[:, x:x + 2] for x in (98, 100, 106, 108))
                step(dve.tensor_scalar(s, e, 2.0, None, ALU.add), "sp0")
                step(dve.reciprocal(s, s), "sp1")
                step(dve.tensor_tensor(s, s, e, ALU.mult), "sp2")
                step(dve.tensor_tensor(s2, s, s, ALU.mult), "sp3")
                step(dve.tensor_scalar(p, s2, 1.0 / 13, None, ALU.mult), "sp4")
                for k in (11, 9, 7, 5, 3):
                    step(dve.scalar_tensor_tensor(out=p, in0=p, scalar=1.0 / k, in1=s2, op0=ALU.add, op1=ALU.mult), ("sp", k))
                step(dve.scalar_tensor_tensor(out=p, in0=p, scalar=1.0, in1=s, op0=ALU.add, op1=ALU.mult), "sp5")
                step(dve.tensor_scalar(s, par2[:, C2["lam"]:C2["lam"] + 2], -1.0, 0.0, ALU.mult, ALU.max), "sp6")
                step(dve.scalar_tensor_tensor(out=s, in0=p, scalar=2.0, in1=s, op0=ALU.mult, op1=ALU.add), "sp7")
                dve.tensor_scalar(small[:, 102:104], s, 8.0, None, ALU.mult)
                step(dve.tensor_scalar(small[:, 104:106], s, -8.0, None, ALU.mult), "s8")
                dve.wait_ge(*act_step.after("lam_sums"))
                step(dve.tensor_tensor(small[:, 68:69], small[:, 67:68], small[:, 66:67], ALU.subtract), "lam0")
                dve.tensor_scalar(small[:, 126:127], small[:, 68:69], par2[:, N2:N2 + 1], None, ALU.subtract
                                  ).then_inc(*dve_step.done("neg_lam"))
                step(dve.tensor_scalar(small[:, 127:128], col(par2, C2, "subln"), par2[:, N2 + 1:N2 + 2], None, ALU.mult),
                     "subln")
                for n in range(4):
                    dve.wait_ge(*a_read.after(("q2", n)))
                    dve.scalar_tensor_tensor(out=mix2[:, n, :], in0=mix2[:, n, :], scalar=HD ** -0.5, in1=scale_by[:, :],
                                             op0=ALU.mult, op1=ALU.mult).then_inc(*dve_step.done(("q2", n)))
                for n in range(4):
                    times_factor(da_k[:, n, :], v_read.done(("k2", n)), w_used.after(("k2", n)), v_bank(("k2", n))[:, :])
                for c in range(2):
                    dve.wait_ge(*act_step.after(("tanh", c)))
                    step(dve.tensor_scalar(lru_x[:, c, :], gate_r[:, c, :], 1.0, None, ALU.add), ("t1", c))
                    step(dve.reciprocal(lru_x[:, c, :], lru_x[:, c, :]), ("t2", c))
                    step(dve.scalar_tensor_tensor(out=gate_r[:, c, :], in0=gate_r[:, c, :], scalar=2.0,
                                                  in1=lru_x[:, c, :], op0=ALU.mult, op1=ALU.mult), ("mult2", c))
                for c in range(2):
                    step(dve.tensor_tensor(xr[:, c, :], xr[:, c, :], gate_i[:, c, :], ALU.mult), ("ix", c))
                    dve.wait_ge(*act_step.after(("mult", c)))
                    step(dve.tensor_tensor(xr[:, c, :], xr[:, c, :], gate_r[:, c, :], ALU.mult), ("b", c))
                    step(dve.tensor_tensor_scan(lru_x[:, c, :], lru_a[:, c, :], xr[:, c, :], 0.0, ALU.mult, ALU.add),
                         ("h", c))
                    dve.wait_ge(*act_step.after(("gelu", c)))
                    dve.tensor_tensor(mix2[:, 6 + c, :], lru_x[:, c, :], lru_g[:, c, :], ALU.mult
                                      ).then_inc(*dve_step.done(("mix2", 6 + c)))
                for tile in (1, 3):
                    dve.wait_ge(*(sums.after(("v2", 1)) if tile == 1 else w_used.after(("v2", "unit", 3))))
                    dve.tensor_scalar(da_v[:, tile, :], v_bank(("v2", tile))[:, :], small[:, tile:tile + 1], None, ALU.mult
                                      ).then_inc(*v_read.done(("v2", tile)))
                for n in range(len(heads) + 4):
                    if n < len(heads):
                        h, i = heads[n]
                        for m in range(2):
                            key, k = ("diff", h, i, m), 32 + 2 * (n % 8) + m
                            dve.wait_ge(*scores_ready.after(key))
                            dve.tensor_reduce(small[:, k:k + 1], bank_s[s_read.slot(key, 4)][:, 0:(i + 1) * P],
                                              AX.X, ALU.max, negate=True).then_inc(*row_max.done(key))
                    if 1 <= n <= len(heads):
                        h, i = heads[n - 1]
                        w, k, slot = (i + 1) * P, 2 * ((n - 1) % 8), (n - 1) % 3 * 2
                        dve.wait_ge(*s_read.after(("diff", h, i, 1)))
                        step(dve.reciprocal(small[:, 96 + k:98 + k], small[:, 64 + k:66 + k]), ("inv", h, i))
                        step(dve.tensor_scalar(small[:, 97 + k:98 + k], small[:, 97 + k:98 + k], small[:, 126:127],
                                               None, ALU.mult), ("weight", h, i))
                        step(dve.tensor_scalar(probs2[:, slot, 0:w], probs2[:, slot, 0:w], small[:, 96 + k:97 + k],
                                               None, ALU.mult), ("p0", h, i))
                        dve.scalar_tensor_tensor(out=probs2[:, slot, 0:w], in0=probs2[:, slot + 1, 0:w],
                                                 scalar=small[:, 97 + k:98 + k], in1=probs2[:, slot, 0:w],
                                                 op0=ALU.mult, op1=ALU.add).then_inc(*probs_ready.done(("diff", h, i)))
                    if n >= 4 and heads[n - 4][1] == TT - 1:
                        h = heads[n - 4][0]
                        keep(("diff", "out", h), sums, mix2[:, h, :])
                rms("subln", 4, 1, lambda c: mix2[:, c, :], lambda c: small[:, 127:128], P, 1e-5, mix_hi, mix_lo)
                for c in range(4, DC):
                    split_lo("subln", c, mix2[:, c, :], mix_hi, mix_lo)
                for c in range(DC):
                    dve.wait_ge(*w_used.after(("wout", c)))
                    dve.tensor_tensor(resid[:, c, :], resid[:, c, :], v_bank(("wout", c))[:, :], ALU.add
                                      ).then_inc(*v_read.done(("wout", c)))
                    gained_lo("rms3", C2["ffn2"], c)
                ffn_scaled("ffn2", "rms3")
                dve.wait_ge(*par_in.after("par2_next"))
                down("ffn2", 1.0, 0.5, True, lambda c: gained_lo("next", C2["ffn1"], c))
            factor("final")
            for c in range(DC):
                dve.scalar_tensor_tensor(out=resid[:, c, :], in0=resid[:, c, :], scalar=col(par2, C2, "final", c),
                                         in1=scale_by[:, :], op0=ALU.mult, op1=ALU.mult).then_inc(*scaled.done(("final", c)))
    return counts.found


def _cols_unit(w):
    return w.reshape(DC, P, P).transpose(1, 0, 2).reshape(P, UNIT)


def _proj_units(w):
    return [_cols_unit(w[:, c:c + P]) for c in range(0, w.shape[1], P)]


def _row_units(w):
    per = UNIT // w.shape[1]
    return [w[n * per * P:(n + 1) * per * P].reshape(per, P, -1).transpose(1, 0, 2).reshape(P, UNIT)
            for n in range(DC // per)]


def _ffn_units(gate, up, down):
    out = []
    for g, u in zip(_proj_units(gate), _proj_units(up)):
        out += [g, u]
    tiles = down.reshape(FC, P, DC, P).transpose(1, 2, 0, 3).reshape(P, FC, UNIT)
    return out + [tiles[:, n] for n in range(FC)]


def _columns(v):
    return v.reshape(-1, P).T


def _units(a):
    half_of = (np.arange(ROPE) + ROPE // 2) % ROPE
    pairs = [0, 2, 1, 3]
    out = []
    for l in range(DEPTH):
        w = a["w_in"][l]
        cut = dict(zip("fq fk fv fg cq ckv kr sq sk sv wq wk wv".split(), np.split(
            w, np.cumsum([256, 256, 256, 4, 256, 128, 32, 256, 256, 256, 256, 128]), axis=1)))
        first = np.zeros((D, P), np.float32)
        first[:, 0:4] = cut["fg"]
        first[:, 32:64] = cut["kr"][:, half_of]
        first[:, 64:96] = cut["kr"]
        wq = cut["wq"].reshape(D, 4, HD)[:, pairs].reshape(D, 256)
        out.append(_cols_unit(first))
        out += _proj_units(np.concatenate([cut["cq"], cut["ckv"]], 1))
        for name in ("fq", "fk"):
            out += _proj_units(cut[name])
        out += _row_units(cut["fv"])
        out += _proj_units(cut["sq"]) + _proj_units(cut["sk"]) + _row_units(cut["sv"])
        out += _proj_units(wq) + _proj_units(cut["wk"]) + _row_units(cut["wv"])
        uq = a["mla_w_uq"][l]
        turned = uq.reshape(256, 4, 96)[:, :, 64:][:, :, half_of].reshape(256, P)
        out.append(np.concatenate([uq, turned], 1).reshape(2, P, S).transpose(1, 0, 2).reshape(P, UNIT))
        ukv = np.zeros((P, UNIT), np.float32)
        ukv[:, 0:512] = a["mla_w_ukv"][l].reshape(P, 4, 2, HD).transpose(0, 2, 1, 3).reshape(P, 512)
        out.append(ukv)
        wo = a["w_o"][l].copy()
        wo[768:] = wo[768:].reshape(4, HD, D)[pairs].reshape(256, D)
        out += _proj_units(wo) + _ffn_units(a["w_gate"][l], a["w_up"][l], a["w_down"][l])
    for l in range(DEPTH):
        q, k, v, b, c, x, lx, lg = np.split(a["w_in_2"][l], [512, 1024, 1536, 1792, 2048, 2304, 2560], axis=1)
        out += _ffn_units(a["ffn1_gate_2"][l], a["ffn1_up_2"][l], a["ffn1_down_2"][l])
        for w in (lg, lx, c, x, b, q, k):
            out += _proj_units(w)
        out += _row_units(v) + [np.zeros((P, UNIT), np.float32)] * 2
        out += _proj_units(a["w_out_2"][l])
        out += _ffn_units(a["ffn2_gate_2"][l], a["ffn2_up_2"][l], a["ffn2_down_2"][l])
    assert len(out) == UNITS
    return np.stack(out).reshape(UNITS // SLOTS, SLOTS, P, UNIT)


def _parameters(a):
    pairs = [0, 2, 1, 3]
    par1 = np.zeros((DEPTH, P, N1), np.float32)
    par2 = np.zeros((DEPTH + 1, P, N2 + 2), np.float32)
    lru_w = np.zeros((DEPTH, P, 4, P), np.float32)
    for l in range(DEPTH):
        def put(par, at, v):
            v = _columns(v)
            par[l, :, at:at + v.shape[1]] = v

        mix_g = a["mix_g"][l].copy()
        mix_g[768:] = mix_g[768:].reshape(4, HD)[pairs].reshape(256)
        put(par1, C1["mix_g"], mix_g)
        for name in ("ln1_g", "ln1_b", "ln2_g", "ln2_b"):
            put(par1, C1[name], a[name][l])
        put(par1, C1["g_q"], a["mla_g_q"][l])
        put(par1, C1["g_kv"], a["mla_g_kv"][l])
        par1[l, 0:4, C1["b_f"]] = a["fox_b_f"][l]
        par1[l, :, C1["sink"]:C1["sink"] + 4] = a["swa_sinks"][l]
        for name, source in (("ffn1", "ffn1_norm_2"), ("mix", "mix_norm_2"), ("ffn2", "ffn2_norm_2"),
                             ("lru_b", "lru_conv_b_2"), ("lam", "lru_lambda_2"), ("subln", "subln_gain_2")):
            put(par2, C2[name], a[source][l])
        put(par2, C2["ba"], a["lru_ba_2"][l].reshape(-1))
        put(par2, C2["bx"], a["lru_bx_2"][l].reshape(-1))
        put(par2, C2["sc_w"], a["sc_conv_w_2"][l].reshape(-1))
        put(par2, C2["lru_w"], a["lru_conv_w_2"][l].reshape(-1))
        put(par2, C2["final"], a["final_norm_2"])
        for name in ("q1", "k1", "q2", "k2"):
            par2[l, 0:HD, C2["l" + name]] = a[f"lam_{name}_2"][l]
        lam_init = 0.8 - 0.6 * math.exp(-0.3 * l)
        par2[l, :, N2] = lam_init
        par2[l, :, N2 + 1] = 1.0 - lam_init
        for m, name in enumerate(("lru_wa_2", "lru_wx_2")):
            for n in range(4):
                r = slice(n % 2 * HD, (n % 2 + 1) * HD)
                lru_w[l, r, 2 * m + n // 2, r] = a[name][l, n]
    par2[DEPTH] = par2[DEPTH - 1]
    return par1, par2, lru_w


def _tables():
    at = np.arange(P)
    f32 = np.float32
    causal = np.where(at[None, :] <= at[:, None], 0.0, NEG).astype(f32)
    strict = np.where(at[None, :] < at[:, None], 0.0, NEG).astype(f32)
    inv = (f32(10000.0) ** (-np.arange(0, ROPE, 2, dtype=f32) / f32(ROPE))).astype(f32)
    angle = np.arange(S, dtype=f32)[:, None] * inv[None, :]
    cos, sin = np.cos(angle).astype(f32).T, np.sin(angle).astype(f32).T
    cos, sin = np.tile(cos, (8, 1)), np.tile(np.concatenate([-sin, sin]), (4, 1))
    scale = f32(96.0 ** -0.5)
    rope = np.stack([cos * scale, sin * scale, cos, sin], axis=1).astype(f32)
    dist = at[:, None] + P - np.arange(2 * P)[None, :]
    slopes = np.exp2(-8.0 * np.arange(1, 5, dtype=f32) / 4)
    alibi = np.stack([np.where((dist >= 0) & (dist < P), -s * dist, NEG) for s in slopes], axis=1).astype(f32)
    d = 2 * P - 1 - np.arange(T5W)
    n = np.maximum(d, 1).astype(f32)
    large = 16 + (np.log(n / f32(16)) / f32(math.log(8.0)) * f32(16)).astype(np.int32)
    bucket = np.where(d < 16, np.maximum(d, 0), np.minimum(large, BUCKETS - 1))
    bucket_of = np.zeros((BUCKETS + 1, T5W), f32)
    bucket_of[bucket[d >= 0], np.nonzero(d >= 0)[0]] = 1.0
    bucket_of[BUCKETS, d < 0] = 1.0
    return dict(ident=np.eye(P, dtype=f32), mask=causal, strict=strict,
                bucket_of=bucket_of, rope=np.ascontiguousarray(rope), alibi=np.ascontiguousarray(alibi))


def arrays(inputs):
    a = {k: np.asarray(v) for k, v in inputs.items()}
    par1, par2, lru_w = _parameters(a)
    return dict(_tables(), w_stream=_units(a), par1=par1, par2=par2, lru_w=lru_w,
                x=np.ascontiguousarray(a["x"][0].T.reshape(DC, P, S).transpose(1, 0, 2)),
                rel=a["rel_bias_2"], rel_far=np.tile(a["rel_bias_2"][BUCKETS - 1:], (BUCKETS, 1)))


def program(nc, ins):
    t = {name: nc.dram_tensor(f"in_{name}", a.shape, F32, kind="ExternalInput").ap() for name, a in ins.items()}
    t["out"] = nc.dram_tensor("out_0", (P, DC, S), F32, kind="ExternalOutput").ap()
    rows = nc.dram_tensor("t5_rows", (8, P, T5W), F32, kind="Internal")
    t["t5_rows"] = rows.ap()
    t["t5_skewed"] = bass.AP(rows, P - 1, [[T5W - 1, P], [P * T5W, 8], [1, 2 * P]])
    return t


def kernel(**inputs):
    from concourse import bacc
    from concourse.bass_utils import run_bass_kernel_spmd

    ins = arrays(inputs)

    def fresh():
        return bacc.Bacc("TRN2", target_bir_lowering=False, num_devices=1)

    draft = fresh()
    counted = build(draft, program(draft, ins), None)
    nc = fresh()
    build(nc, program(nc, ins), counted)
    r = run_bass_kernel_spmd(nc, [{f"in_{name}": a for name, a in ins.items()}], core_ids=[0])
    y = r.results[0]["out_0"]
    return y.transpose(2, 1, 0).reshape(1, S, D)
```

```python
from contextlib import ExitStack, contextmanager
import math

import numpy as np
import concourse.bass as bass
from concourse import mybir

F32 = mybir.dt.float32
F32R = mybir.dt.float32r
ALU = mybir.AluOpType
ACT = mybir.ActivationFunctionType
AX = mybir.AxisListType

P = 128
D = 1024
S = 512
DEPTH = 2
HD = 64
DC = D // P
TT = S // P
FF = 2816
FC = FF // P
NEG = -1e30
ALPHA = (2.0 * DEPTH) ** 0.25
ROPE = 32
BUCKETS = 32
SLOTS = 4
UNIT = 8 * P
FFN_UNITS = 3 * FC
B1_PROJ = 22
B1_UNITS = B1_PROJ + DC + FFN_UNITS
B2_PROJ = 24
B2_UNITS = 2 * FFN_UNITS + B2_PROJ + DC
UNITS = DEPTH * (B1_UNITS + B2_UNITS)

C1 = dict(mix_g=0, ln1_g=8, ln1_b=16, ln2_g=24, ln2_b=32, g_q=40, g_kv=42, b_f=43, sink=44)
N1 = 48
C2 = dict(ffn1=0, mix=8, ffn2=16, sc_w=24, lru_w=30, lru_b=38, ba=40, bx=42, lam=44, subln=46,
          final=47, lq1=55, lk1=56, lq2=57, lk2=58)
N2 = 59
UV_TILES = ((0, 1), (2,), (3,))
GROUPS = ("fox", "mla", "stick", "swa")
T5W = 3 * P


class Counts:

    def __init__(self, known):
        self.known = known or {}
        self.found = {}
        self.loops = []

    @contextmanager
    def loop(self, engine, name, rounds):
        with engine.Fori(0, rounds) as i:
            self.loops.append((name, rounds, i))
            for s in self.signals:
                s.enter()
            yield i
            for s in self.signals:
                s.leave(name, rounds)
            self.loops.pop()


class Signal:

    def __init__(self, counts, sem, name, credit=0):
        self.counts, self.sem, self.name, self.credit = counts, sem, name, credit
        self.total, self.base, self.open, self.events = credit, [], [[]], {}

    def enter(self):
        self.base.append(self.total)
        self.open.append([])

    def leave(self, name, rounds):
        start = self.base.pop()
        each = self.total - start
        mine = self.open.pop()
        for key in mine:
            self.events[key][1][name] = (each, rounds)
        self.open[-1] += mine
        self.total = start + each * rounds
        self.counts.found[self.name] = self.events

    def done(self, key, n=1):
        assert key not in self.events, (self.name, key)
        self.total += n
        self.events[key] = [self.total, {}]
        self.open[-1].append(key)
        self.counts.found[self.name] = self.events
        return self.sem, n

    def number(self, key, rounds=None):
        known = self.counts.known
        if not known:
            return 1
        value, loops = known[self.name][key]
        here = {name: i for name, _, i in self.counts.loops}
        for name, (each, total) in loops.items():
            value = value + each * (here[name] if name in here else total - 1 if rounds is None else rounds)
        return value

    def after(self, key, rounds=None):
        return self.sem, self.number(key, rounds)

    def before(self, key):
        return self.sem, self.number(key) - self.credit

    def carried(self, first, again):
        known = self.counts.known
        if not known:
            return self.sem, 1
        (start, _), (later, loops) = known[self.name][first], known[self.name][again]
        name, _, i = self.counts.loops[-1]
        each = loops[name][0]
        assert later == start + each, (self.name, first, again)
        return self.sem, start + i * each

    def slot(self, key, depth):
        if not self.counts.known:
            return 0
        value, loops = self.counts.known[self.name][key]
        assert all(each % depth == 0 for each, _ in loops.values()), (self.name, key, loops)
        return (value - self.credit - 1) % depth


def build(nc, t, known):
    counts = Counts(known)
    loop = counts.loop
    with ExitStack() as ctx:
        def sb(name, shape, dt=F32):
            return ctx.enter_context(nc.sbuf_tensor(name, shape, dt))

        def overlay(*entries):
            with ExitStack() as scope:
                return [scope.enter_context(nc.sbuf_tensor(*entry)) for entry in entries]

        counts.signals = []

        def signal(name, credit=0):
            s = Signal(counts, ctx.enter_context(nc.semaphore(name)), name, credit)
            counts.signals.append(s)
            return s

        resid = sb("resid", [P, DC, S])
        raw = sb("raw", [P, SLOTS, UNIT])
        w_hi = sb("w_hi", [P, SLOTS, UNIT], F32R)
        w_lo = sb("w_lo", [P, SLOTS, UNIT], F32R)
        ident = sb("ident", [P, P])
        ident_r = sb("ident_r", [P, P], F32R)
        mask_r = sb("mask_r", [P, P], F32R)
        strict_r = sb("strict_r", [P, P], F32R)
        ones = sb("ones", [P, P])
        zero = sb("zero", [P, 1])
        par1 = sb("par1", [P, N1])
        par2 = sb("par2", [P, N2 + 2])
        small = sb("small", [P, 128])
        cum = sb("cum", [4, S])
        scale_by, diag = overlay(("scale_by", [P, S], F32), ("diag", [P, 4 * TT, P], F32))
        aug_k, aug_q = overlay(("aug_k", [P, S], F32R), ("aug_q", [P, 4, S], F32R))
        sb("place_of_factors", [P, 5 * S])
        work = sb("work", [P, 4, S])
        xn_hi, xn_lo = overlay(("xn_hi", [P, DC, S], F32R), ("xn_lo", [P, DC, S], F32R))
        probs_t, probs = overlay(("probs_t", [P, 2, TT, S], F32), ("probs", [P, 4, S], F32))
        probs2_t, probs2 = overlay(("probs2_t", [P, 2, TT, S], F32), ("probs2", [P, 8, S], F32))
        squares, = overlay(("squares", [P, DC, S], F32))
        sb("place_of_xn", [P, 2 * DC * S])
        h_hi, h_lo = overlay(("h_hi", [P, FC, S], F32R), ("h_lo", [P, FC, S], F32R))
        (qmix, fox_k, fox_v, sb_k, sw_v, swa_k, cq, mla_q, mla_k, mla_v, rope, alibi,
         lat_hi, lat_lo) = overlay(
            ("qmix", [P, DC, S], F32), ("fox_k", [P, 2, S], F32), ("fox_v", [P, TT, 256], F32),
            ("sb_k", [P, 2, S], F32), ("sw_v", [P, TT, 384], F32), ("swa_k", [P, S], F32),
            ("cq", [P, 3, S], F32),
            ("mla_q", [P, 4, S], F32), ("mla_k", [P, 4, S], F32), ("mla_v", [P, TT, 256], F32),
            ("rope", [P, 4, S], F32), ("alibi", [P, 4, 256], F32R),
            ("lat_hi", [P, 3, S], F32R), ("lat_lo", [P, 3, S], F32R))
        (mix2, da_k, da_v, sc_c, sc_x, sc_b, lru_x, lru_g, xr, gate_r, gate_i, lru_a, lru_w, t5_hi, t5_lo) = overlay(
            ("mix2", [P, DC, S], F32), ("da_k", [P, 4, S], F32), ("da_v", [P, TT, S], F32),
            ("sc_c", [P, 2, S], F32), ("sc_x", [P, 2, S], F32), ("sc_b", [P, 2, S], F32),
            ("lru_x", [P, 2, S], F32), ("lru_g", [P, 2, S], F32), ("xr", [P, 2, S], F32),
            ("gate_r", [P, 2, S], F32), ("gate_i", [P, 2, S], F32), ("lru_a", [P, 2, S], F32),
            ("lru_w", [P, 4, P], F32), ("t5_hi", [P, 8, 256], F32R),
            ("t5_lo", [P, 8, 256], F32R))
        _, mix_hi, mix_lo = overlay(("mix2_again", [P, DC, S], F32), ("mix_hi", [P, DC, S], F32R),
                                    ("mix_lo", [P, DC, S], F32R))
        bucket_of, rel, rel_far, rel_rows, rel_hi, rel_lo, bucket_r, t5_row = overlay(
            ("bucket_of", [P, T5W], F32), ("rel", [P, 8], F32), ("rel_far", [P, 8], F32),
            ("rel_rows", [P, 8, P], F32), ("rel_hi", [P, 8, P], F32R), ("rel_lo", [P, 8, P], F32R),
            ("bucket_r", [P, T5W], F32R), ("t5_row", [P, 8, T5W], F32))
        sb("place_of_h", [P, 2 * FC * S])

        bank_a = [ctx.enter_context(nc.psum_tensor(f"bank_a{i}", [P, S], F32)) for i in range(2)]
        bank_v = [ctx.enter_context(nc.psum_tensor(f"bank_v{i}", [P, S], F32)) for i in range(2)]
        bank_s = [ctx.enter_context(nc.psum_tensor(f"bank_s{i}", [P, S], F32)) for i in range(4)]
        stat_bank = bank_s[3]
        t5_dram = t["t5_rows"]

        def as_r(ap):
            return ap.bitcast(F32R)

        raw_in = [signal(f"raw_in{u}") for u in range(SLOTS)]
        const_in = signal("const_in")
        rel_in = signal("rel_in")
        x_in = [signal(f"x_in{c}") for c in range(DC)]
        par_in = signal("par_in")
        par2_in = signal("par2_in")
        t5_out = signal("t5_out")
        out_done = signal("out_done")
        fills = signal("fills")
        hi_split = signal("hi_split")
        w_split = signal("w_split", SLOTS)
        w_used = signal("w_used", SLOTS)
        sums = signal("sums")
        scores_ready = signal("scores_ready")
        turned = signal("turned")
        a_read = signal("a_read", 2)
        s_read = signal("s_read", 4)
        x_hi = signal("x_hi")
        squared = signal("squared")
        rooted = signal("rooted")
        affine = signal("affine")
        gated = signal("gated")
        act_step = signal("act_step")
        v_read = signal("v_read", 2)
        x_lo = signal("x_lo")
        value = signal("value")
        centered = signal("centered")
        scaled = signal("scaled")
        diag_ready = signal("diag_ready")
        row_max = signal("row_max")
        probs_ready = signal("probs_ready")
        added = signal("added")
        product = signal("product")
        dve_step = signal("dve_step")

        block = ctx.enter_context(nc.Block())

        @block.sync
        def _(sp):
            for c in range(0, DC, 2):
                sp.dma_start(resid[:, c, :], t["x"][:, c, :]).then_inc(*x_in[c].done("x", 16))
            with loop(sp, "stream", UNITS // SLOTS) as i:
                for u in range(SLOTS):
                    sp.wait_ge(*w_split.before(("unit", u)))
                    sp.dma_start(raw[:, u, :], t["w_stream"][i, u]
                                 ).then_inc(*raw_in[u].done("unit", 16))
            for c in range(0, DC, 2):
                sp.wait_ge(*scaled.after(("final", c + 1)))
                sp.dma_start(t["out"][:, c:c + 2, :], resid[:, c:c + 2, :]).then_inc(*out_done.done(("out", c), 16))
            sp.wait_ge(*out_done.after(("out", DC - 2)))

        @block.gpsimd
        def _(pool):
            pool.sem_inc(w_split.sem, SLOTS)
            pool.memset(zero[:, :], 0.0).then_inc(*fills.done("zero"))
            pool.memset(ones[:, :], 1.0).then_inc(*fills.done("ones"))
            pool.wait_ge(*fills.after("ones"))
            with loop(pool, "stream", UNITS // SLOTS):
                for u in range(SLOTS):
                    pool.wait_ge(*raw_in[u].after("unit"))
                    pool.wait_ge(w_used.sem, w_split.before(("unit", u))[1])
                    pool.tensor_tensor(w_hi[:, u, :], raw[:, u, :], zero[:, 0:1].to_broadcast([P, UNIT]),
                                       ALU.add).then_inc(*hi_split.done(("unit", u)))
                    pool.wait_ge(*hi_split.after(("unit", u)))
                    pool.tensor_tensor(w_lo[:, u, :], raw[:, u, :], w_hi[:, u, :].bitcast(F32),
                                       ALU.subtract).then_inc(*w_split.done(("unit", u)))

        @block.tensor
        def _(pe):
            def a_bank(key):
                pe.wait_ge(*a_read.before(key))
                return bank_a[a_read.slot(key, 2)]

            def v_bank(key):
                pe.wait_ge(*v_read.before(key))
                return bank_v[v_read.slot(key, 2)]

            def s_bank(key):
                pe.wait_ge(*s_read.before(key))
                return bank_s[s_read.slot(key, 4)]

            def unit(key):
                pe.wait_ge(w_split.sem, w_used.number(key))
                return w_used.slot(key, SLOTS)

            def mm3(out, lhs_hi, lhs_lo, rhs_hi, rhs_lo, first, last):
                pe.matmul(out, lhs_hi, rhs_hi, start=first, stop=False)
                pe.matmul(out, lhs_hi, rhs_lo, start=False, stop=False)
                return pe.matmul(out, lhs_lo, rhs_hi, start=False, stop=last)

            def w_tile(u, k, n=P):
                return w_hi[:, u, k * n:(k + 1) * n], w_lo[:, u, k * n:(k + 1) * n]

            def project(key, bank, wait=None, hi=xn_hi, lo=xn_lo):
                u = unit(key)
                b = bank(key)
                for c in range(DC):
                    if wait:
                        pe.wait_ge(*wait(c))
                    mm = mm3(b[:, :], *w_tile(u, c), hi[:, c, :], lo[:, c, :], c == 0, c == DC - 1)
                mm.then_inc(*w_used.done(key))

            def is_split(tag):
                return lambda c: x_lo.after((tag, c))

            def project_rows(tag, n_units, cols):
                per = DC // n_units
                banks = [a_bank((tag, 0)), v_bank((tag, 1)), a_bank((tag, 2)), v_bank((tag, 3))]
                for n in range(n_units):
                    u = unit((tag, "unit", n))
                    for tile in range(TT):
                        cut = slice(tile * P, (tile + 1) * P)
                        for k in range(per):
                            c = n * per + k
                            mm = mm3(banks[tile][:, 0:cols], xn_hi[:, c, cut], xn_lo[:, c, cut],
                                     *w_tile(u, k, cols), c == 0, c == DC - 1)
                        if n == n_units - 1 and tile < TT - 1:
                            mm.then_inc(*sums.done((tag, tile)))
                    mm.then_inc(*w_used.done((tag, "unit", n)))

            def token_sums(key, source, n=0, bank=stat_bank):
                for tile in range(TT):
                    mm = pe.matmul(bank[:, n + tile:n + tile + 1], source[:, tile * P:(tile + 1) * P],
                                   ones[:, 0:1], start=True, stop=True, skip_group_check=True)
                mm.then_inc(*sums.done(key))

            def spread(tag, groups=1):
                for g in range(groups):
                    pe.wait_ge(*diag_ready.after((tag, g)))
                    pe.matmul(bank_s[g][:, :], ones[:, :], diag[:, g * TT:(g + 1) * TT, :], start=True, stop=True
                              ).then_inc(*sums.done((tag, "spread", g)))

            def square_sums(tag, wait=None):
                pe.wait_ge(*(wait or added.after((tag, DC - 1))))
                token_sums((tag, "sum"), work[:, 2, :])

            def early_sums(tag, ready, source):
                pe.wait_ge(*ready)
                token_sums((tag, "sum"), source, 0, a_bank(tag))

            def mean(tag):
                pe.wait_ge(*added.after((tag, DC - 1)))
                pe.matmul(bank_s[0][:, :], ones[:, :], work[:, 3, :], start=True, stop=True
                          ).then_inc(*sums.done((tag, "mean")))

            def variance(tag):
                for c in range(0, DC, 2):
                    pe.wait_ge(*added.after((tag, "pair", c)))
                    token_sums((tag, "pair", c), squares[:, c, :], c // 2 * TT)
                spread(tag)

            def down(tag):
                for c in range(DC):
                    key = (tag, "down", c)
                    b = v_bank(key)
                    for f in range(FC):
                        i = c * FC + f
                        if i % 8 == 0:
                            u = unit((tag, "wd", i // 8))
                        if c == 0:
                            pe.wait_ge(*(x_lo.after((tag, "h", f % 2), f // 2 - 1) if f > 1 else x_lo.after((tag, "h0", f))))
                        mm = mm3(b[:, :], *w_tile(u, i % 8), h_hi[:, f, :], h_lo[:, f, :], f == 0, f == FC - 1)
                        if i % 8 == 7:
                            mm.then_inc(*w_used.done((tag, "wd", i // 8)))
                        elif f == FC - 1:
                            mm.then_inc(*sums.done(key))

            def ffn(tag, split, stats=None):
                for k in range(2):
                    project((tag, "gate0", k), a_bank, None if k else split)
                    if stats and k == 0:
                        square_sums(*stats)
                    project((tag, "up0", k), v_bank)
                    if stats and k == 0:
                        spread(stats[0])
                with loop(pe, tag, FC // 2 - 1):
                    for k in range(2):
                        project((tag, "gate", k), a_bank)
                        project((tag, "up", k), v_bank)
                down(tag)

            def turn(key, source, n):
                pe.wait_ge(*probs_ready.after(key))
                b = a_bank(key)
                for j in range(n):
                    mm = pe.transpose(b[:, j * P:(j + 1) * P], source[:, j * P:(j + 1) * P], ident[:, :])
                mm.then_inc(*turned.done(key))

            def attend(items, scores, turn_item, finish, extra=None):
                lag = 3
                for n in range(len(items) + lag + 1):
                    if n < len(items):
                        scores(items[n])
                    if lag <= n < len(items) + lag:
                        turn_item(n - lag)
                    if n > lag and items[n - lag - 1][1] == TT - 1:
                        finish(items[n - lag - 1][0])
                    if extra:
                        extra(n)

            heads = [(h, i) for h in range(4) for i in range(TT)]

            def values(tag, h, v, pt, rows, banded=False):
                pe.wait_ge(*a_read.after((tag, h, TT - 1)))
                b = v_bank((tag, "out", h))
                for j in range(TT):
                    end = min((j + 2) * P, S) if banded else S
                    mm = pe.matmul(b[rows, j * P:end], v(j, h), pt[:, h % 2, j, j * P:end],
                                   start=(j == 0), stop=True, skip_group_check=True)
                mm.then_inc(*sums.done((tag, "out", h)))

            def half(n):
                return slice(n * HD, (n + 1) * HD)

            def fox():
                def scores(item):
                    h, i = item
                    key = ("fox", h, i)
                    n, cut, r, c = (i + 1) * P, slice(i * P, (i + 1) * P), half(h % 2), h // 2
                    b = s_bank(key)
                    pe.matmul(b[:, 0:n], qmix[r, c, cut], fox_k[r, c, 0:n], start=True, stop=True)
                    pe.matmul(b[:, 0:n], aug_q[:, h, cut], aug_k[:, 0:n], start=False, stop=True, skip_group_check=True)
                    pe.matmul(b[:, i * P:n], ident_r[:, :], mask_r[:, :], start=False, stop=True,
                              skip_group_check=True).then_inc(*scores_ready.done(key))

                pe.wait_ge(*act_step.after("aug"))
                pe.wait_ge(*dve_step.after("aug"))
                attend(heads, scores, lambda n: turn(("fox", *heads[n]), work[:, n % 4, :], heads[n][1] + 1),
                       lambda h: values("fox", h, lambda j, h: fox_v[:, j, half(h)], probs_t, half(h % 2)))

            def group_sums(tag, n):
                if n == 6:
                    early_sums(tag, added.after((tag, "squares")), cq[:, 0, :])

            def head_sums(n):
                h = n // 4 - 2
                if n % 4 == 1 and h in (0, 1):
                    early_sums(("subln", h), squared.after(("subln", h)), work[:, h, :])

            def mla():
                def scores(item):
                    h, i = item
                    key = ("mla", h, i)
                    n, cut = (i + 1) * P, slice(i * P, (i + 1) * P)
                    b = s_bank(key)
                    pe.matmul(b[:, 0:n], mla_q[0:96, h, cut], mla_k[0:96, h, 0:n], start=True, stop=True)
                    pe.matmul(b[:, i * P:n], ident_r[:, :], mask_r[:, :], start=False, stop=True,
                              skip_group_check=True).then_inc(*scores_ready.done(key))

                attend(heads, scores, lambda n: turn(("mla", *heads[n]), work[:, n % 4, :], heads[n][1] + 1),
                       lambda h: values("mla", h, lambda j, h: mla_v[:, j, half(h)], probs_t, half(h % 2)),
                       lambda n: group_sums("fox", n))

            def swa():
                def scores(item):
                    h, i = item
                    key = ("swa", h, i)
                    lo, n, cut, r = max(i - 1, 0) * P, (i + 1) * P, slice(i * P, (i + 1) * P), half(h // 2)
                    b = s_bank(key)
                    pe.matmul(b[:, n - lo:n - lo + 1], ones[0:1, :], par1[0:1, C1["sink"] + h:C1["sink"] + h + 1],
                              start=True, stop=True)
                    pe.matmul(b[:, 0:n - lo], qmix[r, 6 + h % 2, cut], swa_k[r, lo:n], start=True, stop=True)
                    pe.matmul(b[:, 0:n - lo], ident_r[:, :], alibi[:, h, 256 - (n - lo):256],
                              start=False, stop=True, skip_group_check=True).then_inc(*scores_ready.done(key))

                attend(heads, scores, lambda n: turn(("swa", *heads[n]), work[:, n % 4, :], min(heads[n][1], 1) + 1),
                       lambda h: values("swa", h, lambda j, h: sw_v[:, j, 256 + h // 2 * HD:256 + (h // 2 + 1) * HD], probs_t,
                                        half(h // 2), banded=True),
                       lambda n: group_sums("stick", n))

            def stick():
                def scores(item):
                    h, i = item
                    key = ("stick", h, i)
                    n, r = (i + 1) * P, half(h % 2)
                    b = s_bank(key)
                    pe.matmul(b[:, 0:n], qmix[r, 4 + h // 2, i * P:n], sb_k[r, h // 2, 0:n], start=True, stop=True)
                    pe.matmul(b[:, i * P:n], ident_r[:, :], strict_r[:, :], start=False, stop=True,
                              skip_group_check=True).then_inc(*scores_ready.done(key))

                attend(heads, scores, lambda n: turn(("stick", *heads[n]), probs[:, n % 4, :], heads[n][1] + 1),
                       lambda h: values("stick", h, lambda j, h: sw_v[:, j, half(h)], probs_t, half(h % 2)),
                       lambda n: group_sums("mla", n))

            def diff():
                def scores(item):
                    h, i = item
                    n, cut = (i + 1) * P, slice(i * P, (i + 1) * P)
                    lo = max(i - 1, 0) * P
                    for m in range(2):
                        key = ("diff", h, i, m)
                        b = s_bank(key)
                        pe.matmul(b[:, 0:n], mix2[half(m), h, cut], da_k[half(m), h, 0:n], start=True, stop=True)
                        pe.matmul(b[:, lo:n], ident_r[:, :], t5_hi[:, 2 * h + m, 256 - (n - lo):256],
                                  start=False, stop=True, skip_group_check=True)
                        pe.matmul(b[:, lo:n], ident_r[:, :], t5_lo[:, 2 * h + m, 256 - (n - lo):256],
                                  start=False, stop=True, skip_group_check=True
                                  ).then_inc(*scores_ready.done(key))

                attend(heads, scores,
                       lambda n: turn(("diff", *heads[n]), probs2[:, n % 4 * 2, :], heads[n][1] + 1),
                       lambda h: values("diff", h, lambda j, h: da_v[:, j, h * P:(h + 1) * P], probs2_t, slice(0, P)),
                       lambda n: head_sums(n))

            pe.sem_inc(w_used.sem, SLOTS)
            pe.wait_ge(*fills.after("ones"))
            pe.wait_ge(*rel_in.after("bucket_of"))
            pe.wait_ge(*dve_step.after("rel_lo"))
            for m in range(8):
                b = (v_bank if m % 2 else a_bank)(("t5", m))
                rows = slice(0, BUCKETS + 1)
                pe.matmul(b[:, 0:T5W], rel_hi[rows, m, :], bucket_r[rows, :], start=True, stop=False)
                pe.matmul(b[:, 0:T5W], rel_lo[rows, m, :], bucket_r[rows, :], start=False, stop=True
                          ).then_inc(*sums.done(("t5", m)))

            with loop(pe, "layer1", DEPTH):
                project("kr", v_bank, lambda c: x_lo.carried(("in1", c), ("ln2", c)))
                for n in range(3):
                    project(("c", n), a_bank)
                for n in range(2):
                    project(("fq", n), a_bank)
                pe.wait_ge(*added.after(("lat", "pair")))
                token_sums(("lat", "sum", 0), mla_q[:, 0, :])
                pe.wait_ge(*squared.after(("lat", 2)))
                token_sums(("lat", "sum", 2), mla_q[:, 2, :], TT)
                for n in range(2):
                    project(("fk", n), v_bank)
                spread("lat", 2)
                project_rows("fv", 2, 256)
                for n in range(2):
                    project(("sq", n), a_bank)
                for n in range(2):
                    project(("sk", n), v_bank)
                for n in range(2):
                    project(("wq", n), a_bank)
                banks = [a_bank(("sv", 0)), v_bank(("sv", 1)), a_bank(("sv", 2)), v_bank(("sv", 3))]
                first = w_used.slot(("sv", "unit", 0), SLOTS)
                assert first + 3 <= SLOTS
                rows_hi, rows_lo = (w[:, first:first + 3, :].rearrange("p s c -> p (s c)") for w in (w_hi, w_lo))
                for n, chunks in enumerate(((0, 1), (2, 3, 4), (5, 6, 7))):
                    pe.wait_ge(w_split.sem, w_used.number(("sv", "unit", 0)) + n)
                    for tile in range(TT):
                        cut = slice(tile * P, (tile + 1) * P)
                        for c in chunks:
                            cols = slice(c * 384, (c + 1) * 384)
                            mm = mm3(banks[tile][:, 0:384], xn_hi[:, c, cut], xn_lo[:, c, cut],
                                     rows_hi[:, cols], rows_lo[:, cols], c == 0, c == DC - 1)
                        if n == 2 and tile < TT - 1:
                            mm.then_inc(*sums.done(("sv", tile)))
                    if n == 1:
                        mm.then_inc(*w_used.done(("sv", "unit", 0)))
                    if n == 2:
                        mm.then_inc(*w_used.done(("sv", "units"), 2))
                project("wk", v_bank)
                u = unit("uq")
                for c in range(2):
                    pe.wait_ge(*x_lo.after(("lat", c)))
                for n in range(5):
                    b = v_bank(("uq", n))
                    rows = slice(0, 96 if n < 4 else P)
                    for c in range(2):
                        cols = slice(c * S + n * 96, c * S + n * 96 + rows.stop)
                        mm = mm3(b[rows, :], w_hi[:, u, cols], w_lo[:, u, cols], lat_hi[:, c, :], lat_lo[:, c, :],
                                 c == 0, c == 1)
                    mm.then_inc(*(sums.done(("uq", n)) if n < 4 else w_used.done("uq")))
                u = unit("ukv")
                pe.wait_ge(*x_lo.after(("lat", 2)))
                for h in range(4):
                    b = a_bank(("uk", h))
                    cols = slice(h * HD, h * HD + P)
                    mm3(b[:, :], w_hi[:, u, cols], w_lo[:, u, cols], lat_hi[:, 2, :], lat_lo[:, 2, :],
                        True, True).then_inc(*sums.done(("uk", h)))
                for n, tiles in enumerate(UV_TILES):
                    b = a_bank(("uv", n))
                    for k, tile in enumerate(tiles):
                        cut = slice(tile * P, (tile + 1) * P)
                        mm = mm3(b[:, k * 256:(k + 1) * 256], lat_hi[:, 2, cut], lat_lo[:, 2, cut],
                                 w_hi[:, u, 256:512], w_lo[:, u, 256:512], True, True)
                    mm.then_inc(*(sums.done(("uv", n)) if n < 2 else w_used.done("ukv")))
                fox()
                mla()
                stick()
                swa()
                early_sums("swa", added.after(("swa", "squares")), cq[:, 0, :])
                spread("mixnorm", 4)
                for c in range(DC):
                    project(("wo", c), v_bank, is_split("mixnorm") if c == 0 else None)
                mean("ln1")
                variance("ln1")
                ffn("ffn", is_split("ln1"))
                mean("ln2")
                variance("ln2")

            with loop(pe, "layer2", DEPTH):
                ffn("ffn1", lambda c: x_lo.carried(("first", c), ("next", c)),
                    ("rms1", added.carried(("first", DC - 1), ("next", DC - 1))))
                project(("lg", 0), a_bank, is_split("rms2"))
                square_sums("rms2")
                project(("lg", 1), a_bank)
                spread("rms2")
                for n in range(2):
                    project(("lx", n), v_bank)
                for n in range(2):
                    project(("scc", n), a_bank)
                for n in range(2):
                    project(("scx", n), v_bank)
                for n in range(2):
                    project(("scb", n), a_bank)
                pe.wait_ge(*dve_step.after("lam_products"))
                pe.matmul(stat_bank[:, 0:2], ones[0:HD, :], small[0:HD, 64:66], start=True, stop=True
                          ).then_inc(*sums.done("lam_sums"))
                for n in range(4):
                    project(("q2", n), a_bank)
                pe.wait_ge(*par_in.after("tables2"))
                for n in range(4):
                    if n % 2 == 0:
                        c = n // 2
                        pe.wait_ge(*dve_step.after(("xr", c)))
                        for m, name in enumerate("ri"):
                            b = a_bank(("gate", name, c))
                            pe.matmul(b[:, :], lru_w[:, 2 * m + c, :], xr[:, c, :], start=True, stop=True
                                      ).then_inc(*sums.done(("gate", name, c)))
                    project(("k2", n), v_bank)
                project_rows("v2", 4, S)
                for n in range(2):
                    unit(("pad", n))
                    pe.matmul(stat_bank[:, 2:4], ones[:, :], ones[:, 0:2], start=True, stop=True
                              ).then_inc(*w_used.done(("pad", n)))
                pe.wait_ge(*dve_step.after(("q2", 3)))
                diff()
                for h in (2, 3):
                    pe.wait_ge(*squared.after(("subln", h)))
                    token_sums((("subln", h), "sum"), work[:, h, :], h * TT)
                spread("subln", 4)
                for c in range(DC):
                    project(("wout", c), v_bank, is_split("subln") if c == 0 else None, mix_hi, mix_lo)
                ffn("ffn2", is_split("rms3"), ("rms3", None))
            square_sums("final", added.after(("next", DC - 1)))
            spread("final")

        @block.scalar
        def _(act):
            def a_bank(key):
                return bank_a[a_read.slot(key, 2)]

            def split_hi(tag, c, source, dest=xn_hi):
                act.activation(dest[:, c, :], source, ACT.Copy).then_inc(*x_hi.done((tag, c)))

            def square(key, source, out):
                act.activation(out, source, ACT.Square).then_inc(*squared.done(key))

            def root(tag, groups):
                act.wait_ge(*dve_step.after((tag, "var")))
                act.activation(small[:, 16:16 + groups * TT], small[:, 0:groups * TT], ACT.Sqrt
                               ).then_inc(*rooted.done(tag))

            def copy_bank(key, ready, out, rows=slice(0, P), n=S, func=ACT.Copy, **kw):
                act.wait_ge(*ready.after(key))
                act.activation(out, a_bank(key)[rows, 0:n], func, **kw).then_inc(*a_read.done(key))

            def apply_norm(tag, groups, per, dest):
                for c in range(groups * per):
                    last = c % per == per - 1
                    act.wait_ge(*(scaled if last else value).after((tag, c)))
                    split_hi(tag, c, work[:, c % 4, :], dest)

            def early_squares(tag, n, source):
                if n == 4:
                    act.wait_ge(*v_read.after((tag, "out", 3)))
                    for c in range(2):
                        square((tag, c), source[:, c, :], cq[:, c, :])
                if n == 6:
                    keep_sums(tag, GROUPS.index(tag))

            def keep_sums(key, g):
                act.wait_ge(*sums.after((key, "sum")))
                act.activation(small[:, g * TT:(g + 1) * TT], a_bank(key)[:, 0:TT], ACT.Copy).then_inc(*a_read.done(key))

            def gained(tag, column, ready):
                for c in range(DC):
                    ready(c)
                    act.activation(xn_hi[:, c, :], resid[:, c, :], ACT.Copy, scale=par2[:, column + c:column + c + 1]
                                   ).then_inc(*x_hi.done((tag, c)))
                    if c >= 2:
                        act.wait_ge(*added.after((tag, max(c - 2, 1))))
                    square((tag, c), resid[:, c, :], work[:, c % 2, :])

            def norm_ln(tag, columns, split):
                for c in range(DC):
                    act.wait_ge(*centered.after((tag, c)))
                    square((tag, c), resid[:, c, :], squares[:, c, :])
                root(tag, 1)
                g, b = (C1[x] for x in columns)
                for c in range(DC + 1):
                    if c < DC:
                        act.wait_ge(*scaled.after((tag, c)))
                        act.activation(resid[:, c, :], resid[:, c, :], ACT.Identity, scale=par1[:, g + c:g + c + 1],
                                       bias=par1[:, b + c:b + c + 1]).then_inc(*affine.done((tag, c)))
                    if c and split:
                        act.wait_ge(*affine.after((tag, c - 1)))
                        split_hi(tag, c - 1, resid[:, c - 1, :])
                act.wait_ge(*affine.after((tag, DC - 1)))

            def ffn(tag):
                def hidden(k, at, gate, up, h):
                    act.wait_ge(*w_used.after((tag, gate, k)))
                    act.activation(work[:, k, :], a_bank((tag, gate, k))[:, :], ACT.Silu
                                   ).then_inc(*a_read.done((tag, gate, k)))
                    act.wait_ge(*v_read.after((tag, up, k)))
                    act.activation(h_hi[:, at, :], work[:, 2 + k:3 + k, :], ACT.Copy
                                   ).then_inc(*x_hi.done((tag, h, k)))

                for k in range(2):
                    hidden(k, slice(k, k + 1), "gate0", "up0", "h0")
                with loop(act, tag, FC // 2 - 1) as i:
                    for k in range(2):
                        hidden(k, bass.ds(i * 2 + (2 + k), 1), "gate", "up", "h")

            def ffn_scaled(tag, stats):
                root(stats, 1)

                def hidden(k, at, gate, up, h):
                    key = (tag, gate, k)
                    act.wait_ge(*w_used.after(key))
                    act.activation(work[:, k, :], a_bank(key)[:, :], ACT.Copy).then_inc(*a_read.done(key))
                    act.wait_ge(*value.after(key))
                    act.activation(work[:, k, :], work[:, k, :], ACT.Silu).then_inc(*gated.done(key))
                    act.wait_ge(*product.after((tag, h, k)))
                    act.activation(h_hi[:, at, :], work[:, 2 + k:3 + k, :], ACT.Copy).then_inc(*x_hi.done((tag, h, k)))

                for k in range(2):
                    hidden(k, slice(k, k + 1), "gate0", "up0", "h0")
                with loop(act, tag, FC // 2 - 1) as i:
                    for k in range(2):
                        hidden(k, bass.ds(i * 2 + (2 + k), 1), "gate", "up", "h")

            def exp_item(key, slot, n, item):
                act.wait_ge(*row_max.after(key))
                b = bank_s[s_read.slot(key, 4)]
                act.activation(slot[:, 0:n], b[:, 0:n], ACT.Exp, bias=small[:, 32 + item:33 + item],
                               accum_out=small[:, 64 + item:65 + item]).then_inc(*s_read.done(key))

            def keep_turned(tag, n, pt, blocks):
                h, i = heads[n]
                key = (tag, h, i)
                if i == 0 and h >= 2:
                    act.wait_ge(*sums.after((tag, "out", h - 2)))
                act.wait_ge(*turned.after(key))
                lo = i + 1 - blocks
                act.activation(pt[:, h % 2, lo:i + 1, i * P:(i + 1) * P],
                               a_bank(key)[:, 0:blocks * P].rearrange("p (j q) -> p j q", q=P), ACT.Copy
                               ).then_inc(*a_read.done(key))

            heads = [(h, i) for h in range(4) for i in range(TT)]

            def softmax(tag, width, blocks, before=None, source=None):
                for n in range(len(heads) + 3):
                    if n < len(heads):
                        exp_item((tag, *heads[n]), work[:, n % 4, :], width(heads[n][1]), n)
                    if n >= 3:
                        keep_turned(tag, n - 3, probs_t, blocks(heads[n - 3][1]))
                    if before:
                        early_squares(before, n, source)

            act.sem_inc(a_read.sem, 2)
            act.sem_inc(s_read.sem, 4)
            for name, dest in (("rel", rel[0:BUCKETS, :]), ("rel_far", rel_far[0:BUCKETS, :]),
                               ("bucket_of", bucket_of[0:BUCKETS + 1, :])):
                act.dma_start(dest, t[name]).then_inc(*rel_in.done(name, 16))
            for c in range(1, DC, 2):
                act.dma_start(resid[:, c, :], t["x"][:, c, :]).then_inc(*x_in[c].done("x", 16))
            for name, dest in (("ident", ident[:, :]), ("mask", work[:, 0, 0:P]), ("strict", work[:, 0, P:2 * P])):
                act.dma_start(dest, t[name]).then_inc(*const_in.done(name, 16))
            for m in range(0, 8, 2):
                copy_bank(("t5", m), sums, t5_row[:, m, :], n=T5W)
            act.wait_ge(*a_read.after(("t5", 6)))
            act.wait_ge(*v_read.after(("t5", 7)))
            act.dma_start(t5_dram.rearrange("m q w -> q m w"), t5_row[:, :, :]).then_inc(*t5_out.done("rows", 16))
            for c in range(DC):
                act.wait_ge(*x_in[c].after("x"))
                split_hi("in1", c, resid[:, c, :])
            act.wait_ge(*const_in.after("strict"))
            act.activation(ident_r[:, :], ident[:, :], ACT.Copy).then_inc(*act_step.done("ident_r"))
            act.activation(mask_r[:, :], work[:, 0, 0:P], ACT.Copy).then_inc(*act_step.done("mask_r"))
            act.activation(strict_r[:, :], work[:, 0, P:2 * P], ACT.Copy).then_inc(*act_step.done("strict_r"))
            act.dma_start(par2[:, :], t["par2"][0]).then_inc(*par2_in.done("first", 16))
            with loop(act, "layer1", DEPTH) as l:
                act.wait_ge(*t5_out.after("rows"))
                act.dma_start(par1[:, :], t["par1"][l]).then_inc(*par_in.done("par1", 16))
                act.dma_start(rope[:, :, :], t["rope"]).then_inc(*par_in.done("rope", 16))
                act.dma_start(mla_v[:, :, :], t["alibi"]).then_inc(*par_in.done("tables1", 16))
                for n in range(3):
                    copy_bank(("c", n), w_used, cq[:, n, :])
                    act.wait_ge(*a_read.after(("c", n)))
                    square(("lat", n), cq[:, n, :], mla_q[:, n, :])
                for n in range(2):
                    copy_bank(("fq", n), w_used, qmix[:, n, :], scale=HD ** -0.5)
                act.wait_ge(*par_in.after("tables1"))
                act.activation(alibi[:, :, :], mla_v[:, :, :], ACT.Copy).then_inc(*act_step.done("alibi_r"))
                root("lat", 2)
                act.wait_ge(*dve_step.after("fz"))
                f = work[0:4, 0:4, :]
                act.activation(f[:, 1, :], f[:, 0, :], ACT.Abs).then_inc(*act_step.done("f_abs"))
                act.wait_ge(*act_step.after("f_abs"))
                act.activation(f[:, 1, :], f[:, 1, :], ACT.Exp, scale=-1.0).then_inc(*act_step.done("f_exp"))
                act.wait_ge(*act_step.after("f_exp"))
                act.activation(f[:, 1, :], f[:, 1, :], ACT.Ln, bias=ones[0:4, 0:1]).then_inc(*act_step.done("f_ln"))
                rows_bank = lambda tag, tile, out, n: copy_bank((tag, tile), sums, out, n=n)
                for tile in (0, 2):
                    rows_bank("fv", tile, fox_v[:, tile, :], 256)
                for n in range(3):
                    act.wait_ge(*value.after(("lat", n)))
                    split_hi("lat", n, cq[:, n, :], lat_hi)
                for n in range(2):
                    copy_bank(("sq", n), w_used, qmix[:, 4 + n, :], scale=HD ** -0.5)
                act.wait_ge(*dve_step.after("cum_lo"))
                for h in range(4):
                    for r, part in ((0, 2), (64, 3)):
                        ins = act.activation(aug_q[r:r + 4, h, :], work[0:4, part, :], ACT.Copy, scale=ident[0:4, h:h + 1])
                ins.then_inc(*act_step.done("aug"))
                for n in range(2):
                    copy_bank(("wq", n), w_used, qmix[:, 6 + n, :], scale=HD ** -0.5)
                for tile in (0, 2):
                    rows_bank("sv", tile, sw_v[:, tile, :], 384)
                for h in range(4):
                    copy_bank(("uk", h), sums, mla_k[0:HD, h, :], rows=slice(0, HD))
                for n, tiles in enumerate(UV_TILES):
                    k = len(tiles)
                    act.wait_ge(*(sums.after(("uv", n)) if n < 2 else w_used.after("ukv")))
                    act.activation(mla_v[:, tiles[0]:tiles[0] + k, :],
                                   a_bank(("uv", n))[:, 0:k * 256].rearrange("p (t c) -> p t c", t=k),
                                   ACT.Copy).then_inc(*a_read.done(("uv", n)))
                causal = lambda i: (i + 1) * P
                softmax("fox", causal, lambda i: i + 1)
                act.wait_ge(*sums.after(("fox", "out", 3)))
                softmax("mla", causal, lambda i: i + 1, "fox", qmix[:, 0:2, :])
                act.wait_ge(*sums.after(("mla", "out", 3)))
                for n in range(len(heads) + 3):
                    if n < len(heads):
                        key, w = ("stick", *heads[n]), (heads[n][1] + 1) * P
                        b = bank_s[s_read.slot(key, 4)]
                        act.wait_ge(*scores_ready.after(key))
                        act.activation(probs[:, n % 4, 0:w], b[:, 0:w], ACT.Sigmoid).then_inc(*act_step.done((*key, "beta")))
                        if n >= 2:
                            act.wait_ge(*dve_step.after(("stick", *heads[n - 2], "products")))
                        act.activation(work[:, n % 2, 0:w], b[:, 0:w], ACT.Sigmoid, scale=-1.0).then_inc(*s_read.done(key))
                    if n >= 3:
                        keep_turned("stick", n - 3, probs_t, heads[n - 3][1] + 1)
                    early_squares("mla", n, qmix[:, 2:4, :])
                act.wait_ge(*sums.after(("stick", "out", 3)))

                softmax("swa", lambda i: min(i + 1, 2) * P + 1, lambda i: min(i, 1) + 1, "stick", qmix[:, 4:6, :])
                act.wait_ge(*a_read.after("stick"))
                early_squares("swa", 4, qmix[:, 6:8, :])
                keep_sums("swa", 3)
                root("mixnorm", 4)
                apply_norm("mixnorm", 4, 2, xn_hi)
                norm_ln("ln1", ("ln1_g", "ln1_b"), True)
                ffn("ffn")
                norm_ln("ln2", ("ln2_g", "ln2_b"), True)

            act.wait_ge(*par2_in.after("first"))
            act.wait_ge(*x_lo.after(("ln2", DC - 1)))
            gained("first", C2["ffn1"], lambda c: None)
            with loop(act, "layer2", DEPTH) as l:
                ffn_scaled("ffn1", "rms1")
                gained("rms2", C2["mix"], lambda c: act.wait_ge(*v_read.after(("ffn1", "down", c))))
                root("rms2", 1)
                act.dma_start(lru_w[:, :, :], t["lru_w"][l]).then_inc(*par_in.done("lru_w", 16))
                t5 = da_v[:, :, :].rearrange("p t c -> p (t c)").rearrange("p (m k) -> p m k", k=256)
                act.dma_start(t5, t["t5_skewed"]).then_inc(*par_in.done("tables2", 16))
                for n in range(2):
                    copy_bank(("lg", n), w_used, lru_g[:, n, :])
                for n in range(2):
                    copy_bank(("scc", n), w_used, sc_c[:, n, :])
                for n in range(2):
                    act.wait_ge(*value.after(("lg", n)))
                    act.activation(lru_g[:, n, :], lru_g[:, n, :], ACT.Gelu_apprx_tanh).then_inc(*act_step.done(("gelu", n)))
                for n in range(2):
                    copy_bank(("scb", n), w_used, sc_b[:, n, :])
                act.wait_ge(*par_in.after("tables2"))
                act.activation(t5_hi[:, :, :], t5, ACT.Copy).then_inc(*act_step.done("t5_hi"))
                lam = par2[:, C2["lam"]:C2["lam"] + 2]
                act.activation(small[:, 96:98], lam, ACT.Abs).then_inc(*act_step.done("lam_abs"))
                act.wait_ge(*act_step.after("lam_abs"))
                act.activation(small[:, 98:100], small[:, 96:98], ACT.Exp, scale=-1.0).then_inc(*act_step.done("lam_exp"))
                act.wait_ge(*sums.after("lam_sums"))
                act.activation(small[:, 66:68], stat_bank[:, 0:2], ACT.Exp).then_inc(*act_step.done("lam_sums"))
                for n in range(4):
                    copy_bank(("q2", n), w_used, mix2[:, n, :])
                for c in range(2):
                    for name, dest, column in (("r", gate_r, "ba"), ("i", gate_i, "bx")):
                        copy_bank(("gate", name, c), sums, dest[:, c, :], func=ACT.Sigmoid,
                                  bias=par2[:, C2[column] + c:C2[column] + c + 1])
                act.wait_ge(*a_read.after(("gate", "i", 1)))
                act.wait_ge(*dve_step.after("s8"))
                for c in range(2):
                    act.activation(lru_a[:, c, :], gate_r[:, c, :], ACT.Exp, scale=small[:, 104 + c:105 + c]
                                   ).then_inc(*act_step.done(("lru_a", c)))
                    act.activation(gate_r[:, c, :], gate_r[:, c, :], ACT.Tanh, scale=small[:, 102 + c:103 + c]
                                   ).then_inc(*act_step.done(("tanh", c)))
                for c in range(2):
                    act.wait_ge(*dve_step.after(("mult2", c)))
                    act.activation(gate_r[:, c, :], gate_r[:, c, :], ACT.Sqrt).then_inc(*act_step.done(("mult", c)))
                act.wait_ge(*dve_step.after("t5_lo"))
                for tile in (0, 2):
                    copy_bank(("v2", tile), sums, da_v[:, tile, :], scale=small[:, tile:tile + 1])
                for n in range(len(heads) + 3):
                    if n < len(heads):
                        h, i = heads[n]
                        for m in range(2):
                            exp_item(("diff", h, i, m), probs2[:, n % 4 * 2 + m, :], (i + 1) * P, 2 * (n % 8) + m)
                    if n >= 3:
                        keep_turned("diff", n - 3, probs2_t, heads[n - 3][1] + 1)
                    h = n // 4 - 2
                    if h in (0, 1) and n % 4 == 0:
                        act.wait_ge(*v_read.after(("diff", "out", h)))
                        square(("subln", h), mix2[:, h, :], work[:, h, :])
                    if h in (0, 1) and n % 4 == 1:
                        keep_sums(("subln", h), h)
                for h in (2, 3):
                    act.wait_ge(*v_read.after(("diff", "out", h)))
                    square(("subln", h), mix2[:, h, :], work[:, h, :])
                root("subln", 4)
                apply_norm("subln", 4, 1, mix_hi)
                for c in range(4, DC):
                    act.wait_ge(*dve_step.after(("mix2", c)))
                    split_hi("subln", c, mix2[:, c, :], mix_hi)
                gained("rms3", C2["ffn2"], lambda c: act.wait_ge(*v_read.after(("wout", c))))
                act.wait_ge(*x_lo.after(("rms3", DC - 1)))
                act.dma_start(par2[:, :], t["par2"][l + 1]).then_inc(*par2_in.done("next", 16))
                ffn_scaled("ffn2", "rms3")
                act.wait_ge(*par2_in.after("next"))
                gained("next", C2["ffn1"], lambda c: act.wait_ge(*v_read.after(("ffn2", "down", c))))
            root("final", 1)

        @block.vector
        def _(dve):
            def v_bank(key):
                return bank_v[v_read.slot(key, 2)]

            def step(ins, key):
                ins.then_inc(*dve_step.done(key))
                dve.wait_ge(*dve_step.after(key))

            def split_lo(tag, c, source, hi=xn_hi, lo=xn_lo):
                dve.wait_ge(*x_hi.after((tag, c)))
                dve.tensor_tensor(lo[:, c, :], source, hi[:, c, :].bitcast(F32), ALU.subtract
                                  ).then_inc(*x_lo.done((tag, c)))

            def diagonals(tag, groups, column):
                for g in range(groups):
                    for tile in range(TT):
                        j = g * TT + tile
                        ins = dve.tensor_scalar(diag[:, j, :], ident[:, :], small[:, column + j:column + j + 1],
                                                None, ALU.mult)
                    ins.then_inc(*diag_ready.done((tag, g)))

            def inverse_root(tag, groups, n, eps, source=stat_bank):
                dve.tensor_scalar(small[:, 0:groups * TT], source[:, 0:groups * TT], 1.0 / n, eps,
                                  ALU.mult, ALU.add).then_inc(*dve_step.done((tag, "var")))
                inverse(tag, groups)

            def add_pair(key, a, b):
                dve.tensor_tensor(a, a, b, ALU.add).then_inc(*added.done(key))

            def inverse(tag, groups):
                dve.wait_ge(*rooted.after(tag))
                step(dve.reciprocal(small[:, 0:groups * TT], small[:, 16:16 + groups * TT]), (tag, "rstd"))
                diagonals(tag, groups, 0)

            def apply_norm(tag, groups, per, source, par, hi, lo):
                total = groups * per
                for c in range(total + 1):
                    if c < total:
                        g, last = c // per, c % per == per - 1
                        if c % per == 0:
                            dve.wait_ge(*sums.after((tag, "spread", g)))
                        if c >= 4:
                            dve.wait_ge(*x_lo.after((tag, c - 4)))
                        dve.scalar_tensor_tensor(out=work[:, c % 4, :], in0=source(c), scalar=par(c), in1=bank_s[g][:, :],
                                                 op0=ALU.mult, op1=ALU.mult
                                                 ).then_inc(*(scaled if last else value).done((tag, c)))
                    if c:
                        split_lo(tag, c - 1, work[:, (c - 1) % 4, :], hi, lo)

            def accumulate(tag, c, out, chunk, ready=None):
                if c:
                    if ready:
                        dve.wait_ge(*ready)
                    if c > 1:
                        dve.wait_ge(*added.after((tag, c - 1)))
                    dve.tensor_tensor(out, chunk(0) if c == 1 else out, chunk(c), ALU.add).then_inc(*added.done((tag, c)))

            def sum_squares(tag, c):
                accumulate(tag, c, work[:, 2, :], lambda c: work[:, c % 2, :], squared.after((tag, c)))

            def factor(tag):
                dve.wait_ge(*sums.after((tag, "sum")))
                inverse_root(tag, 1, D, 1e-6)
                dve.wait_ge(*sums.after((tag, "spread", 0)))
                step(dve.tensor_copy(scale_by[:, :], bank_s[0][:, :]), (tag, "factor"))

            def gained_lo(tag, column, c):
                dve.wait_ge(*x_hi.after((tag, c)))
                dve.scalar_tensor_tensor(out=xn_lo[:, c, :], in0=resid[:, c, :], scalar=par2[:, column + c:column + c + 1],
                                         in1=xn_hi[:, c, :].bitcast(F32), op0=ALU.mult, op1=ALU.subtract
                                         ).then_inc(*x_lo.done((tag, c)))
                sum_squares(tag, c)

            def times_factor(out, signalled, ready, source=None):
                dve.wait_ge(*ready)
                dve.tensor_tensor(out, out if source is None else source, scale_by[:, :], ALU.mult).then_inc(*signalled)

            def col(par, table, name, c=0):
                return par[:, table[name] + c:table[name] + c + 1]

            def sum_chunks(tag, c, ready):
                accumulate(tag, c, work[:, 3, :], lambda c: resid[:, c, :], ready)

            def norm_ln(tag, split):
                dve.wait_ge(*sums.after((tag, "mean")))
                for c in range(DC + 2):
                    if c < DC:
                        dve.scalar_tensor_tensor(out=resid[:, c, :], in0=bank_s[0][:, :], scalar=-1.0 / D,
                                                 in1=resid[:, c, :], op0=ALU.mult, op1=ALU.add
                                                 ).then_inc(*centered.done((tag, c)))
                    if c >= 2 and c % 2:
                        dve.wait_ge(*squared.after((tag, c - 2)))
                        add_pair((tag, "pair", c - 3), squares[:, c - 3, :], squares[:, c - 2, :])
                dve.wait_ge(*sums.after((tag, "pair", DC - 2)))
                step(dve.tensor_reduce(small[:, 16:16 + TT], stat_bank[:, 0:4 * TT].rearrange("p (g t) -> p t g", t=TT),
                                       AX.X, ALU.add), (tag, "sum"))
                inverse_root(tag, 1, D, 1e-5, small[:, 16:16 + TT])
                dve.wait_ge(*sums.after((tag, "spread", 0)))
                for c in range(DC + 2):
                    if c < DC:
                        dve.tensor_tensor(resid[:, c, :], resid[:, c, :], bank_s[0][:, :], ALU.mult
                                          ).then_inc(*scaled.done((tag, c)))
                    if c >= 2 and split:
                        split_lo(tag, c - 2, resid[:, c - 2, :])

            def ffn(tag):
                def hidden(k, at, gate, up, h):
                    dve.wait_ge(*a_read.after((tag, gate, k)))
                    dve.wait_ge(*w_used.after((tag, up, k)))
                    dve.tensor_tensor(work[:, 2 + k, :], work[:, k, :], v_bank((tag, up, k))[:, :], ALU.mult
                                      ).then_inc(*v_read.done((tag, up, k)))
                    hidden_lo(tag, k, at, h)

                for k in range(2):
                    hidden(k, slice(k, k + 1), "gate0", "up0", "h0")
                with loop(dve, tag, FC // 2 - 1) as i:
                    for k in range(2):
                        hidden(k, bass.ds(i * 2 + (2 + k), 1), "gate", "up", "h")

            def hidden_lo(tag, k, at, h):
                dve.wait_ge(*x_hi.after((tag, h, k)))
                dve.tensor_tensor(h_lo[:, at, :], work[:, 2 + k:3 + k, :], h_hi[:, at, :].bitcast(F32),
                                  ALU.subtract).then_inc(*x_lo.done((tag, h, k)))

            def ffn_scaled(tag, stats):
                factor(stats)

                def hidden(k, at, gate, up, h):
                    times_factor(work[:, k, :], value.done((tag, gate, k)), a_read.after((tag, gate, k)))
                    times_factor(work[:, 2 + k, :], v_read.done((tag, up, k)), w_used.after((tag, up, k)),
                                 v_bank((tag, up, k))[:, :])
                    dve.wait_ge(*v_read.after((tag, up, k)))
                    dve.wait_ge(*gated.after((tag, gate, k)))
                    dve.tensor_tensor(work[:, 2 + k, :], work[:, k, :], work[:, 2 + k, :], ALU.mult
                                      ).then_inc(*product.done((tag, h, k)))
                    hidden_lo(tag, k, at, h)

                for k in range(2):
                    hidden(k, slice(k, k + 1), "gate0", "up0", "h0")
                with loop(dve, tag, FC // 2 - 1) as i:
                    for k in range(2):
                        hidden(k, bass.ds(i * 2 + (2 + k), 1), "gate", "up", "h")

            def down(tag, first, second, swap, after_chunk=None):
                for c in range(DC):
                    key = (tag, "down", c)
                    end = c * FC + FC - 1
                    dve.wait_ge(*(w_used.after((tag, "wd", end // 8)) if end % 8 == 7 else sums.after(key)))
                    b = v_bank(key)
                    if swap:
                        ins = dve.scalar_tensor_tensor(out=resid[:, c, :], in0=b[:, :], scalar=second,
                                                       in1=resid[:, c, :], op0=ALU.mult, op1=ALU.add)
                    else:
                        ins = dve.scalar_tensor_tensor(out=resid[:, c, :], in0=resid[:, c, :], scalar=first,
                                                       in1=b[:, :], op0=ALU.mult, op1=ALU.add)
                    ins.then_inc(*v_read.done(key))
                    if after_chunk:
                        after_chunk(c)

            def keep(key, ready, out, rows=slice(0, P), n=S):
                dve.wait_ge(*ready.after(key))
                dve.tensor_copy(out, v_bank(key)[rows, 0:n]).then_inc(*v_read.done(key))

            heads = [(h, i) for h in range(4) for i in range(TT)]

            def half(n):
                return slice(n * HD, (n + 1) * HD)

            def softmax(tag, width, out, before=None):
                for n in range(len(heads) + 5):
                    if n < len(heads):
                        h, i = heads[n]
                        key = (tag, h, i)
                        b = bank_s[s_read.slot(key, 4)]
                        dve.wait_ge(*scores_ready.after(key))
                        dve.tensor_reduce(small[:, 32 + n:33 + n], b[:, 0:width(i)], AX.X, ALU.max, negate=True
                                          ).then_inc(*row_max.done(key))
                    if 1 <= n <= len(heads):
                        m = n - 1
                        h, i = heads[m]
                        key = (tag, h, i)
                        total = small[:, 64 + m:65 + m]
                        dve.wait_ge(*s_read.after(key))
                        step(dve.reciprocal(small[:, 96 + m:97 + m], total), (*key, "inverse"))
                        dve.tensor_scalar(work[:, m % 4, 0:width(i)], work[:, m % 4, 0:width(i)],
                                          small[:, 96 + m:97 + m], None, ALU.mult).then_inc(*probs_ready.done(key))
                    if n >= 5 and heads[n - 5][1] == TT - 1:
                        h = heads[n - 5][0]
                        rows, dest = out(h)
                        keep((tag, "out", h), sums, dest, rows)
                    if before and n == 5:
                        early_add(before)

            def early_add(tag):
                dve.wait_ge(*squared.after((tag, 1)))
                add_pair((tag, "squares"), cq[:, 0, :], cq[:, 1, :])

            dve.sem_inc(v_read.sem, 2)
            dve.wait_ge(*fills.after("ones"))
            dve.wait_ge(*rel_in.after("bucket_of"))
            dve.memset(rel_rows[BUCKETS:BUCKETS + 1, :, :], NEG)
            dve.tensor_tensor(rel[0:BUCKETS, :], rel[0:BUCKETS, :], rel_far[0:BUCKETS, :], ALU.subtract
                              ).then_inc(*dve_step.done("rel"))
            dve.wait_ge(*dve_step.after("rel"))
            dve.tensor_copy(rel_rows[0:BUCKETS, :, :], rel[0:BUCKETS, :].unsqueeze(2).to_broadcast([BUCKETS, 8, P])
                            ).then_inc(*dve_step.done("rel_rows"))
            rows = slice(0, BUCKETS + 1)
            dve.wait_ge(*dve_step.after("rel_rows"))
            dve.tensor_copy(bucket_r[rows, :], bucket_of[rows, :])
            step(dve.tensor_copy(rel_hi[rows, :, :], rel_rows[rows, :, :]), "rel_hi")
            dve.tensor_tensor(rel_lo[rows, :, :], rel_rows[rows, :, :], rel_hi[rows, :, :].bitcast(F32), ALU.subtract
                              ).then_inc(*dve_step.done("rel_lo"))

            for m in range(1, 8, 2):
                keep(("t5", m), sums, t5_row[:, m, :], n=T5W)
            for c in range(DC):
                dve.wait_ge(*x_in[c].after("x"))
                split_lo("in1", c, resid[:, c, :])
            dve.wait_ge(*act_step.after("strict_r"))

            with loop(dve, "layer1", DEPTH):
                dve.wait_ge(*par_in.after("tables1"))
                dve.wait_ge(*w_used.after("kr"))
                b = v_bank("kr")
                dve.tensor_scalar(work[0:4, 0, :], b[0:4, :], par1[0:4, C1["b_f"]:C1["b_f"] + 1], None, ALU.add
                                  ).then_inc(*dve_step.done("fz"))
                dve.tensor_tensor(work[64:96, 2, :], b[64:96, :], rope[64:96, 2, :], ALU.mult
                                  ).then_inc(*dve_step.done("kr_cos"))
                dve.tensor_tensor(work[64:96, 3, :], b[32:64, :], rope[32:64, 3, :], ALU.mult
                                  ).then_inc(*v_read.done("kr"))
                dve.wait_ge(*v_read.after("kr"))
                for h in range(4):
                    dve.tensor_tensor(mla_k[64:96, h, :], work[64:96, 2, :], work[64:96, 3, :], ALU.add
                                      ).then_inc(*dve_step.done(("kr", h)))
                dve.wait_ge(*squared.after(("lat", 1)))
                add_pair(("lat", "pair"), mla_q[:, 0, :], mla_q[:, 1, :])
                dve.wait_ge(*sums.after(("lat", "sum", 2)))
                dve.tensor_scalar(small[:, 0:TT], stat_bank[:, 0:TT], 1.0 / 256, 1e-6, ALU.mult, ALU.add)
                dve.tensor_scalar(small[:, TT:2 * TT], stat_bank[:, TT:2 * TT], 1.0 / P, 1e-6, ALU.mult, ALU.add
                                  ).then_inc(*dve_step.done(("lat", "var")))
                inverse("lat", 2)
                for n in range(2):
                    keep(("fk", n), w_used, fox_k[:, n, :])
                for n, column in enumerate((C1["g_q"], C1["g_q"] + 1, C1["g_kv"])):
                    dve.wait_ge(*sums.after(("lat", "spread", n // 2)))
                    dve.scalar_tensor_tensor(out=cq[:, n, :], in0=cq[:, n, :], scalar=par1[:, column:column + 1],
                                             in1=bank_s[n // 2][:, :], op0=ALU.mult, op1=ALU.mult
                                             ).then_inc(*value.done(("lat", n)))
                dve.wait_ge(*act_step.after("f_ln"))
                step(dve.scalar_tensor_tensor(out=work[0:4, 2, :], in0=work[0:4, 0, :], scalar=0.0,
                                              in1=work[0:4, 1, :], op0=ALU.min, op1=ALU.subtract), "log_f")
                step(dve.memset(work[0:4, 0, :], 1.0), "log_ones")
                step(dve.tensor_tensor_scan(work[0:4, 3, :], work[0:4, 0, :], work[0:4, 2, :], 0.0,
                                            ALU.mult, ALU.add), "cum0")
                dve.tensor_copy(cum[0:4, :], work[0:4, 3, :]).then_inc(*dve_step.done("cum"))
                for tile in (1, 3):
                    dve.wait_ge(*(sums.after(("fv", 1)) if tile == 1 else w_used.after(("fv", "unit", 1))))
                    dve.tensor_copy(fox_v[:, tile, :], v_bank(("fv", tile))[:, 0:256]).then_inc(*v_read.done(("fv", tile)))
                for n in range(3):
                    split_lo("lat", n, cq[:, n, :], lat_hi, lat_lo)
                dve.wait_ge(*dve_step.after("cum"))
                dve.tensor_copy(as_r(work[0:4, 2, :]), cum[0:4, :]).then_inc(*dve_step.done("cum_hi"))
                step(dve.tensor_copy(aug_q[:, :, :], zero[:, 0:1].unsqueeze(2).to_broadcast([P, 4, S])), "aug_zero")
                step(dve.tensor_copy(aug_k[:, :], zero[:, 0:1].to_broadcast([P, S])), "aug_k0")
                step(dve.tensor_tensor(work[0:4, 3, :], cum[0:4, :], work[0:4, 2, :], ALU.subtract), "cum_lo")
                one_hot = ident[0:4, 0:4].unsqueeze(2).to_broadcast([4, 4, S])
                for r, part in ((0, 2), (64, 3)):
                    dve.tensor_scalar(aug_k[r:r + 4, :], cum[0:4, :], 0.0, 1.0, ALU.mult, ALU.add)
                    dve.tensor_scalar(aug_k[r + 32:r + 36, :], work[0:4, part, :], -1.0, None, ALU.mult)
                    ins = dve.tensor_copy(aug_q[r + 32:r + 36, :, :], one_hot)
                ins.then_inc(*dve_step.done("aug"))
                for n in range(2):
                    keep(("sk", n), w_used, sb_k[:, n, :])
                for tile in (1, 3):
                    dve.wait_ge(*(sums.after(("sv", 1)) if tile == 1 else w_used.after(("sv", "units"))))
                    dve.tensor_copy(sw_v[:, tile, :], v_bank(("sv", tile))[:, 0:384]).then_inc(*v_read.done(("sv", tile)))
                keep("wk", w_used, swa_k[:, :])
                dve.wait_ge(*v_read.after("wk"))
                dve.sem_inc(*v_read.done("skipped"))
                for h in range(4):
                    key = ("uq", h)
                    dve.wait_ge(*sums.after(key))
                    b = v_bank(key)
                    dve.tensor_scalar(mla_q[0:HD, h, :], b[0:HD, :], 96.0 ** -0.5, None, ALU.mult
                                      ).then_inc(*dve_step.done(("q_plain", h)))
                    dve.tensor_tensor(mla_q[64:96, h, :], b[64:96, :], rope[64:96, 0, :], ALU.mult
                                      ).then_inc(*v_read.done(key))
                dve.wait_ge(*w_used.after("uq"))
                b = v_bank(("uq", 4))
                for h in range(4):
                    r = slice(h * ROPE, (h + 1) * ROPE)
                    ins = dve.tensor_tensor(work[64:96, h, :], b[r, :], rope[r, 1, :], ALU.mult)
                ins.then_inc(*v_read.done(("uq", 4)))
                dve.wait_ge(*v_read.after(("uq", 4)))
                for h in range(4):
                    dve.tensor_tensor(mla_q[64:96, h, :], mla_q[64:96, h, :], work[64:96, h, :], ALU.add
                                      ).then_inc(*dve_step.done(("mla_q", h)))

                causal = lambda i: (i + 1) * P
                softmax("fox", causal, lambda h: (half(h % 2), qmix[half(h % 2), h // 2, :]))
                softmax("mla", causal, lambda h: (half(h % 2), qmix[half(h % 2), 2 + h // 2, :]), "fox")
                for n in range(1, len(heads) + 5):
                    if n <= len(heads):
                        h, i = heads[n - 1]
                        key, w, k = ("stick", h, i), (i + 1) * P, (n - 1) % 2
                        tail, beta = work[:, 2 + k, :], probs[:, (n - 1) % 4, :]
                        dve.wait_ge(*s_read.after(key))
                        step(dve.tensor_tensor_scan(tail[:, 0:w][:, ::-1], work[:, k, 0:w][:, ::-1],
                                                    zero[:, 0:1].to_broadcast([P, w]), 1.0, ALU.mult, ALU.add),
                             (*key, "products"))
                        dve.tensor_tensor(beta[:, 0:w - 1], beta[:, 0:w - 1], tail[:, 1:w], ALU.mult
                                          ).then_inc(*probs_ready.done(key))
                    if n >= 5 and heads[n - 5][1] == TT - 1:
                        h = heads[n - 5][0]
                        keep(("stick", "out", h), sums, qmix[half(h % 2), 4 + h // 2, :], half(h % 2))
                    if n == 5:
                        early_add("mla")
                softmax("swa", lambda i: min(i + 1, 2) * P + 1, lambda h: (half(h // 2), qmix[half(h // 2), 6 + h % 2, :]),
                        "stick")
                early_add("swa")
                dve.wait_ge(*a_read.after("swa"))
                inverse_root("mixnorm", 4, 256, 1e-6, small)
                apply_norm("mixnorm", 4, 2, lambda c: qmix[:, c, :], lambda c: col(par1, C1, "mix_g", c), xn_hi, xn_lo)
                for c in range(DC):
                    dve.wait_ge(*w_used.after(("wo", c)))
                    dve.scalar_tensor_tensor(out=resid[:, c, :], in0=resid[:, c, :], scalar=ALPHA,
                                             in1=v_bank(("wo", c))[:, :], op0=ALU.mult, op1=ALU.add
                                             ).then_inc(*v_read.done(("wo", c)))
                    sum_chunks("ln1", c, v_read.after(("wo", c)))
                norm_ln("ln1", True)
                ffn("ffn")
                down("ffn", ALPHA, 1.0, False, lambda c: sum_chunks("ln2", c, v_read.after(("ffn", "down", c))))
                norm_ln("ln2", True)

            dve.wait_ge(*par2_in.after("first"))
            for c in range(DC):
                gained_lo("first", C2["ffn1"], c)
            with loop(dve, "layer2", DEPTH):
                ffn_scaled("ffn1", "rms1")
                down("ffn1", 1.0, 0.5, True, lambda c: gained_lo("rms2", C2["mix"], c))
                for m, (q, k) in enumerate((("lq1", "lk1"), ("lq2", "lk2"))):
                    ins = dve.tensor_tensor(small[0:HD, 64 + m:65 + m], par2[0:HD, C2[q]:C2[q] + 1],
                                            par2[0:HD, C2[k]:C2[k] + 1], ALU.mult)
                ins.then_inc(*dve_step.done("lam_products"))
                factor("rms2")
                for n in range(2):
                    times_factor(lru_g[:, n, :], value.done(("lg", n)), a_read.after(("lg", n)))
                for n in range(2):
                    times_factor(lru_x[:, n, :], v_read.done(("lx", n)), w_used.after(("lx", n)), v_bank(("lx", n))[:, :])
                dve.wait_ge(*v_read.after(("lx", 1)))
                for c in range(2):
                    w = lambda k: par2[:, C2["lru_w"] + 2 * k + c:C2["lru_w"] + 2 * k + c + 1]
                    step(dve.tensor_scalar(xr[:, c, :], lru_x[:, c, :], w(3), col(par2, C2, "lru_b", c),
                                           ALU.mult, ALU.add), ("lconv", c, 0))
                    for d in (1, 2, 3):
                        ins = dve.scalar_tensor_tensor(out=xr[:, c, d:S], in0=lru_x[:, c, 0:S - d], scalar=w(3 - d),
                                                       in1=xr[:, c, d:S], op0=ALU.mult, op1=ALU.add)
                        step(ins, ("lconv", c, d) if d < 3 else ("xr", c))
                for n in range(2):
                    key = ("scx", n)
                    times_factor(sc_c[:, n, :], dve_step.done(("scc", n)), a_read.after(("scc", n)))
                    times_factor(sc_x[:, n, :], v_read.done(key), w_used.after(key), v_bank(key)[:, :])
                    dve.wait_ge(*dve_step.after(("scc", n)))
                    dve.wait_ge(*v_read.after(key))
                    step(dve.tensor_tensor(sc_x[:, n, :], sc_c[:, n, :], sc_x[:, n, :], ALU.mult), ("sc", n))
                for c in range(2):
                    w = lambda k: par2[:, C2["sc_w"] + 2 * k + c:C2["sc_w"] + 2 * k + c + 1]
                    step(dve.tensor_scalar(sc_c[:, c, :], sc_x[:, c, :], w(2), None, ALU.mult), ("conv", c, 0))
                    for d in (1, 2):
                        step(dve.scalar_tensor_tensor(out=sc_c[:, c, d:S], in0=sc_x[:, c, 0:S - d], scalar=w(2 - d),
                                                      in1=sc_c[:, c, d:S], op0=ALU.mult, op1=ALU.add), ("conv", c, d))
                    times_factor(sc_b[:, c, :], dve_step.done(("scb", c)), a_read.after(("scb", c)))
                    dve.wait_ge(*dve_step.after(("scb", c)))
                    dve.tensor_tensor(mix2[:, 4 + c, :], sc_c[:, c, :], sc_b[:, c, :], ALU.mult
                                      ).then_inc(*dve_step.done(("mix2", 4 + c)))
                dve.wait_ge(*act_step.after("t5_hi"))
                t5 = da_v[:, :, :].rearrange("p t c -> p (t c)").rearrange("p (m k) -> p m k", k=256)
                dve.tensor_tensor(t5_lo[:, :, :], t5, t5_hi[:, :, :].bitcast(F32), ALU.subtract).then_inc(*dve_step.done("t5_lo"))
                dve.wait_ge(*act_step.after("lam_exp"))
                e, s, s2, p = (small[:, x:x + 2] for x in (98, 100, 106, 108))
                step(dve.tensor_scalar(s, e, 2.0, None, ALU.add), "sp0")
                step(dve.reciprocal(s, s), "sp1")
                step(dve.tensor_tensor(s, s, e, ALU.mult), "sp2")
                step(dve.tensor_tensor(s2, s, s, ALU.mult), "sp3")
                step(dve.tensor_scalar(p, s2, 1.0 / 13, None, ALU.mult), "sp4")
                for k in (11, 9, 7, 5, 3):
                    step(dve.scalar_tensor_tensor(out=p, in0=p, scalar=1.0 / k, in1=s2, op0=ALU.add, op1=ALU.mult), ("sp", k))
                step(dve.scalar_tensor_tensor(out=p, in0=p, scalar=1.0, in1=s, op0=ALU.add, op1=ALU.mult), "sp5")
                step(dve.tensor_scalar(s, par2[:, C2["lam"]:C2["lam"] + 2], -1.0, 0.0, ALU.mult, ALU.max), "sp6")
                step(dve.scalar_tensor_tensor(out=s, in0=p, scalar=2.0, in1=s, op0=ALU.mult, op1=ALU.add), "sp7")
                dve.tensor_scalar(small[:, 102:104], s, 8.0, None, ALU.mult)
                step(dve.tensor_scalar(small[:, 104:106], s, -8.0, None, ALU.mult), "s8")
                dve.wait_ge(*act_step.after("lam_sums"))
                step(dve.tensor_tensor(small[:, 68:69], small[:, 67:68], small[:, 66:67], ALU.subtract), "lam0")
                dve.tensor_scalar(small[:, 126:127], small[:, 68:69], par2[:, N2:N2 + 1], None, ALU.subtract
                                  ).then_inc(*dve_step.done("neg_lam"))
                step(dve.tensor_scalar(small[:, 127:128], col(par2, C2, "subln"), par2[:, N2 + 1:N2 + 2], None, ALU.mult),
                     "subln")
                for n in range(4):
                    dve.wait_ge(*a_read.after(("q2", n)))
                    dve.scalar_tensor_tensor(out=mix2[:, n, :], in0=mix2[:, n, :], scalar=HD ** -0.5, in1=scale_by[:, :],
                                             op0=ALU.mult, op1=ALU.mult).then_inc(*dve_step.done(("q2", n)))
                for n in range(4):
                    times_factor(da_k[:, n, :], v_read.done(("k2", n)), w_used.after(("k2", n)), v_bank(("k2", n))[:, :])
                for c in range(2):
                    dve.wait_ge(*act_step.after(("tanh", c)))
                    step(dve.tensor_scalar(lru_x[:, c, :], gate_r[:, c, :], 1.0, None, ALU.add), ("t1", c))
                    step(dve.reciprocal(lru_x[:, c, :], lru_x[:, c, :]), ("t2", c))
                    step(dve.scalar_tensor_tensor(out=gate_r[:, c, :], in0=gate_r[:, c, :], scalar=2.0,
                                                  in1=lru_x[:, c, :], op0=ALU.mult, op1=ALU.mult), ("mult2", c))
                for c in range(2):
                    step(dve.tensor_tensor(xr[:, c, :], xr[:, c, :], gate_i[:, c, :], ALU.mult), ("ix", c))
                    dve.wait_ge(*act_step.after(("mult", c)))
                    step(dve.tensor_tensor(xr[:, c, :], xr[:, c, :], gate_r[:, c, :], ALU.mult), ("b", c))
                    step(dve.tensor_tensor_scan(lru_x[:, c, :], lru_a[:, c, :], xr[:, c, :], 0.0, ALU.mult, ALU.add),
                         ("h", c))
                    dve.wait_ge(*act_step.after(("gelu", c)))
                    dve.tensor_tensor(mix2[:, 6 + c, :], lru_x[:, c, :], lru_g[:, c, :], ALU.mult
                                      ).then_inc(*dve_step.done(("mix2", 6 + c)))
                for tile in (1, 3):
                    dve.wait_ge(*(sums.after(("v2", 1)) if tile == 1 else w_used.after(("v2", "unit", 3))))
                    dve.tensor_scalar(da_v[:, tile, :], v_bank(("v2", tile))[:, :], small[:, tile:tile + 1], None, ALU.mult
                                      ).then_inc(*v_read.done(("v2", tile)))
                for n in range(len(heads) + 5):
                    if n < len(heads):
                        h, i = heads[n]
                        for m in range(2):
                            key, k = ("diff", h, i, m), 32 + 2 * (n % 8) + m
                            dve.wait_ge(*scores_ready.after(key))
                            dve.tensor_reduce(small[:, k:k + 1], bank_s[s_read.slot(key, 4)][:, 0:(i + 1) * P],
                                              AX.X, ALU.max, negate=True).then_inc(*row_max.done(key))
                    if 1 <= n <= len(heads):
                        h, i = heads[n - 1]
                        w, k, slot = (i + 1) * P, 2 * ((n - 1) % 8), (n - 1) % 4 * 2
                        dve.wait_ge(*s_read.after(("diff", h, i, 1)))
                        step(dve.reciprocal(small[:, 96 + k:98 + k], small[:, 64 + k:66 + k]), ("inv", h, i))
                        step(dve.tensor_scalar(small[:, 97 + k:98 + k], small[:, 97 + k:98 + k], small[:, 126:127],
                                               None, ALU.mult), ("weight", h, i))
                        step(dve.tensor_scalar(probs2[:, slot, 0:w], probs2[:, slot, 0:w], small[:, 96 + k:97 + k],
                                               None, ALU.mult), ("p0", h, i))
                        dve.scalar_tensor_tensor(out=probs2[:, slot, 0:w], in0=probs2[:, slot + 1, 0:w],
                                                 scalar=small[:, 97 + k:98 + k], in1=probs2[:, slot, 0:w],
                                                 op0=ALU.mult, op1=ALU.add).then_inc(*probs_ready.done(("diff", h, i)))
                    if n >= 5 and heads[n - 5][1] == TT - 1:
                        h = heads[n - 5][0]
                        keep(("diff", "out", h), sums, mix2[:, h, :])
                dve.wait_ge(*a_read.after(("subln", 1)))
                dve.wait_ge(*sums.after((("subln", 3), "sum")))
                step(dve.tensor_copy(small[:, 2 * TT:4 * TT], stat_bank[:, 2 * TT:4 * TT]), ("subln", "sums"))
                inverse_root("subln", 4, P, 1e-5, small)
                apply_norm("subln", 4, 1, lambda c: mix2[:, c, :], lambda c: small[:, 127:128], mix_hi, mix_lo)
                for c in range(4, DC):
                    split_lo("subln", c, mix2[:, c, :], mix_hi, mix_lo)
                for c in range(DC):
                    dve.wait_ge(*w_used.after(("wout", c)))
                    dve.tensor_tensor(resid[:, c, :], resid[:, c, :], v_bank(("wout", c))[:, :], ALU.add
                                      ).then_inc(*v_read.done(("wout", c)))
                    gained_lo("rms3", C2["ffn2"], c)
                ffn_scaled("ffn2", "rms3")
                dve.wait_ge(*par2_in.after("next"))
                down("ffn2", 1.0, 0.5, True, lambda c: gained_lo("next", C2["ffn1"], c))
            factor("final")
            for c in range(DC):
                dve.scalar_tensor_tensor(out=resid[:, c, :], in0=resid[:, c, :], scalar=col(par2, C2, "final", c),
                                         in1=scale_by[:, :], op0=ALU.mult, op1=ALU.mult).then_inc(*scaled.done(("final", c)))
    return counts.found


def _cols_unit(w):
    return w.reshape(DC, P, P).transpose(1, 0, 2).reshape(P, UNIT)


def _proj_units(w):
    return [_cols_unit(w[:, c:c + P]) for c in range(0, w.shape[1], P)]


def _row_units(w):
    per = UNIT // w.shape[1]
    return [w[n * per * P:(n + 1) * per * P].reshape(per, P, -1).transpose(1, 0, 2).reshape(P, UNIT)
            for n in range(DC // per)]


def _ffn_units(gate, up, down):
    out = []
    for g, u in zip(_proj_units(gate), _proj_units(up)):
        out += [g, u]
    tiles = down.reshape(FC, P, DC, P).transpose(1, 2, 0, 3).reshape(P, FC, UNIT)
    return out + [tiles[:, n] for n in range(FC)]


def _columns(v):
    return v.reshape(-1, P).T


def _units(a):
    half_of = (np.arange(ROPE) + ROPE // 2) % ROPE
    pairs = [0, 2, 1, 3]
    out = []
    for l in range(DEPTH):
        w = a["w_in"][l]
        cut = dict(zip("fq fk fv fg cq ckv kr sq sk sv wq wk wv".split(), np.split(
            w, np.cumsum([256, 256, 256, 4, 256, 128, 32, 256, 256, 256, 256, 128]), axis=1)))
        first = np.zeros((D, P), np.float32)
        first[:, 0:4] = cut["fg"]
        first[:, 32:64] = cut["kr"][:, half_of]
        first[:, 64:96] = cut["kr"]
        wq = cut["wq"].reshape(D, 4, HD)[:, pairs].reshape(D, 256)
        out.append(_cols_unit(first))
        out += _proj_units(np.concatenate([cut["cq"], cut["ckv"]], 1))
        for name in ("fq", "fk"):
            out += _proj_units(cut[name])
        out += _row_units(cut["fv"])
        out += _proj_units(cut["sq"]) + _proj_units(cut["sk"]) + _proj_units(wq)
        rows = np.concatenate([cut["sv"], cut["wv"]], 1).reshape(DC, P, 384).transpose(1, 0, 2)
        out += list(rows.reshape(P, 3, UNIT).transpose(1, 0, 2)) + _proj_units(cut["wk"])
        uq = a["mla_w_uq"][l]
        turned = uq.reshape(256, 4, 96)[:, :, 64:][:, :, half_of].reshape(256, P)
        out.append(np.concatenate([uq, turned], 1).reshape(2, P, S).transpose(1, 0, 2).reshape(P, UNIT))
        ukv = np.zeros((P, UNIT), np.float32)
        ukv[:, 0:512] = a["mla_w_ukv"][l].reshape(P, 4, 2, HD).transpose(0, 2, 1, 3).reshape(P, 512)
        out.append(ukv)
        wo = a["w_o"][l].copy()
        wo[768:] = wo[768:].reshape(4, HD, D)[pairs].reshape(256, D)
        out += _proj_units(wo) + _ffn_units(a["w_gate"][l], a["w_up"][l], a["w_down"][l])
    for l in range(DEPTH):
        q, k, v, b, c, x, lx, lg = np.split(a["w_in_2"][l], [512, 1024, 1536, 1792, 2048, 2304, 2560], axis=1)
        out += _ffn_units(a["ffn1_gate_2"][l], a["ffn1_up_2"][l], a["ffn1_down_2"][l])
        for w in (lg, lx, c, x, b, q, k):
            out += _proj_units(w)
        out += _row_units(v) + [np.zeros((P, UNIT), np.float32)] * 2
        out += _proj_units(a["w_out_2"][l])
        out += _ffn_units(a["ffn2_gate_2"][l], a["ffn2_up_2"][l], a["ffn2_down_2"][l])
    assert len(out) == UNITS
    return np.stack(out).reshape(UNITS // SLOTS, SLOTS, P, UNIT)


def _parameters(a):
    pairs = [0, 2, 1, 3]
    par1 = np.zeros((DEPTH, P, N1), np.float32)
    par2 = np.zeros((DEPTH + 1, P, N2 + 2), np.float32)
    lru_w = np.zeros((DEPTH, P, 4, P), np.float32)
    for l in range(DEPTH):
        def put(par, at, v):
            v = _columns(v)
            par[l, :, at:at + v.shape[1]] = v

        mix_g = a["mix_g"][l].copy()
        mix_g[768:] = mix_g[768:].reshape(4, HD)[pairs].reshape(256)
        put(par1, C1["mix_g"], mix_g)
        for name in ("ln1_g", "ln1_b", "ln2_g", "ln2_b"):
            put(par1, C1[name], a[name][l])
        put(par1, C1["g_q"], a["mla_g_q"][l])
        put(par1, C1["g_kv"], a["mla_g_kv"][l])
        par1[l, 0:4, C1["b_f"]] = a["fox_b_f"][l]
        par1[l, :, C1["sink"]:C1["sink"] + 4] = a["swa_sinks"][l]
        for name, source in (("ffn1", "ffn1_norm_2"), ("mix", "mix_norm_2"), ("ffn2", "ffn2_norm_2"),
                             ("lru_b", "lru_conv_b_2"), ("lam", "lru_lambda_2"), ("subln", "subln_gain_2")):
            put(par2, C2[name], a[source][l])
        put(par2, C2["ba"], a["lru_ba_2"][l].reshape(-1))
        put(par2, C2["bx"], a["lru_bx_2"][l].reshape(-1))
        put(par2, C2["sc_w"], a["sc_conv_w_2"][l].reshape(-1))
        put(par2, C2["lru_w"], a["lru_conv_w_2"][l].reshape(-1))
        put(par2, C2["final"], a["final_norm_2"])
        for name in ("q1", "k1", "q2", "k2"):
            par2[l, 0:HD, C2["l" + name]] = a[f"lam_{name}_2"][l]
        lam_init = 0.8 - 0.6 * math.exp(-0.3 * l)
        par2[l, :, N2] = lam_init
        par2[l, :, N2 + 1] = 1.0 - lam_init
        for m, name in enumerate(("lru_wa_2", "lru_wx_2")):
            for n in range(4):
                r = slice(n % 2 * HD, (n % 2 + 1) * HD)
                lru_w[l, r, 2 * m + n // 2, r] = a[name][l, n]
    par2[DEPTH] = par2[DEPTH - 1]
    return par1, par2, lru_w


def _tables():
    at = np.arange(P)
    f32 = np.float32
    causal = np.where(at[None, :] <= at[:, None], 0.0, NEG).astype(f32)
    strict = np.where(at[None, :] < at[:, None], 0.0, NEG).astype(f32)
    inv = (f32(10000.0) ** (-np.arange(0, ROPE, 2, dtype=f32) / f32(ROPE))).astype(f32)
    angle = np.arange(S, dtype=f32)[:, None] * inv[None, :]
    cos, sin = np.cos(angle).astype(f32).T, np.sin(angle).astype(f32).T
    cos, sin = np.tile(cos, (8, 1)), np.tile(np.concatenate([-sin, sin]), (4, 1))
    scale = f32(96.0 ** -0.5)
    rope = np.stack([cos * scale, sin * scale, cos, sin], axis=1).astype(f32)
    dist = at[:, None] + P - np.arange(2 * P)[None, :]
    slopes = np.exp2(-8.0 * np.arange(1, 5, dtype=f32) / 4)
    alibi = np.stack([np.where((dist >= 0) & (dist < P), -s * dist, NEG) for s in slopes], axis=1).astype(f32)
    d = 2 * P - 1 - np.arange(T5W)
    n = np.maximum(d, 1).astype(f32)
    large = 16 + (np.log(n / f32(16)) / f32(math.log(8.0)) * f32(16)).astype(np.int32)
    bucket = np.where(d < 16, np.maximum(d, 0), np.minimum(large, BUCKETS - 1))
    bucket_of = np.zeros((BUCKETS + 1, T5W), f32)
    bucket_of[bucket[d >= 0], np.nonzero(d >= 0)[0]] = 1.0
    bucket_of[BUCKETS, d < 0] = 1.0
    return dict(ident=np.eye(P, dtype=f32), mask=causal, strict=strict,
                bucket_of=bucket_of, rope=np.ascontiguousarray(rope), alibi=np.ascontiguousarray(alibi))


def arrays(inputs):
    a = {k: np.asarray(v) for k, v in inputs.items()}
    par1, par2, lru_w = _parameters(a)
    return dict(_tables(), w_stream=_units(a), par1=par1, par2=par2, lru_w=lru_w,
                x=np.ascontiguousarray(a["x"][0].T.reshape(DC, P, S).transpose(1, 0, 2)),
                rel=a["rel_bias_2"], rel_far=np.tile(a["rel_bias_2"][BUCKETS - 1:], (BUCKETS, 1)))


def program(nc, ins):
    t = {name: nc.dram_tensor(f"in_{name}", a.shape, F32, kind="ExternalInput").ap() for name, a in ins.items()}
    t["out"] = nc.dram_tensor("out_0", (P, DC, S), F32, kind="ExternalOutput").ap()
    rows = nc.dram_tensor("t5_rows", (8, P, T5W), F32, kind="Internal")
    t["t5_rows"] = rows.ap()
    t["t5_skewed"] = bass.AP(rows, P - 1, [[T5W - 1, P], [P * T5W, 8], [1, 2 * P]])
    return t


def kernel(**inputs):
    from concourse import bacc
    from concourse.bass_utils import run_bass_kernel_spmd

    ins = arrays(inputs)

    def fresh():
        return bacc.Bacc("TRN2", target_bir_lowering=False, num_devices=1)

    draft = fresh()
    counted = build(draft, program(draft, ins), None)
    nc = fresh()
    build(nc, program(nc, ins), counted)
    r = run_bass_kernel_spmd(nc, [{f"in_{name}": a for name, a in ins.items()}], core_ids=[0])
    y = r.results[0]["out_0"]
    return y.transpose(2, 1, 0).reshape(1, S, D)
```
